# Optimizing a Trainium2 kernel written in Bass

```python
import math
import jax
import jax.numpy as jnp
from jax import lax
import numpy as np
import jax, jax.numpy as jnp

D_MODEL = 1024
BATCH = 1
SEQ = 256
DEPTH = 1

HEAD_DIM = 64
NSA_HEADS = 8
NSA_GROUPS = 2
NSA_REP = NSA_HEADS // NSA_GROUPS
CMP_BLOCK = 32
CMP_STRIDE = 16
CMP_HIDDEN = 256
SEL_BLOCK = 64
SEL_TOPK = 16
NSA_WINDOW = 512
NSA_QBLOCK = 128
SWA_HEADS = 8
SWA_KV_HEADS = 2
SWA_REP = SWA_HEADS // SWA_KV_HEADS
SWA_WINDOW = 128
SWA_QBLOCK = 128
D_FF = 4 * D_MODEL
NUM_BUCKETS = 32
MAX_DISTANCE = 1024
N_BIAS_HEADS = NSA_HEADS + SWA_HEADS
RMS_EPS = 1e-6

NSA_Q_DIM = NSA_HEADS * HEAD_DIM
NSA_KV_DIM = NSA_GROUPS * HEAD_DIM
SWA_Q_DIM = SWA_HEADS * HEAD_DIM
SWA_KV_DIM = SWA_KV_HEADS * HEAD_DIM
IN_SIZES = (NSA_Q_DIM,) + (NSA_KV_DIM,) * 6 + (3 * NSA_HEADS, SWA_Q_DIM, SWA_KV_DIM, SWA_KV_DIM, D_MODEL, D_MODEL)
IN_DIM = int(sum(IN_SIZES))
IN_OFFSETS = tuple(int(o) for o in np.cumsum(IN_SIZES)[:-1])


def rms_norm(x, g):
    xf = x.astype(jnp.float32)
    y = xf * lax.rsqrt(jnp.mean(xf * xf, axis=-1, keepdims=True) + RMS_EPS)
    return (y * g.astype(jnp.float32)).astype(x.dtype)

def t5_bucket(dist):
    max_exact = NUM_BUCKETS // 2
    d = jnp.maximum(dist, 0)
    df = jnp.maximum(d, 1).astype(jnp.float32)
    large = max_exact + (jnp.log(df / max_exact) / math.log(MAX_DISTANCE / max_exact)
                         * (NUM_BUCKETS - max_exact)).astype(jnp.int32)
    large = jnp.minimum(large, NUM_BUCKETS - 1)
    return jnp.where(d < max_exact, d, large)

def masked_softmax(s, mask):
    s = jnp.where(mask, s.astype(jnp.float32), -jnp.inf)
    m = jnp.max(s, axis=-1, keepdims=True)
    m = jnp.where(jnp.isfinite(m), m, 0.0)
    e = jnp.exp(s - m)
    return e / jnp.maximum(jnp.sum(e, axis=-1, keepdims=True), 1e-30)

def compress_kv(kv, pos, w1, w2):
    b, s, g, d = kv.shape
    n_cmp = (s - CMP_BLOCK) // CMP_STRIDE + 1
    kb = kv.reshape(b, s // CMP_STRIDE, CMP_STRIDE, g, d)
    blocks = jnp.concatenate([kb[:, o:o + n_cmp] for o in range(CMP_BLOCK // CMP_STRIDE)], axis=2)
    blocks = blocks + pos[None, None, :, None, :]
    flat = blocks.transpose(0, 1, 3, 2, 4).reshape(b, n_cmp, g, CMP_BLOCK * d)
    return jax.nn.gelu(flat @ w1) @ w2

def nsa_attention(q, kc, vc, k_slc, v_slc, k_win, v_win, gates, bias_tab):
    b, s, g, r, d = q.shape
    scale = d ** -0.5
    n_cmp = kc.shape[1]
    n_sel = s // SEL_BLOCK
    topk = min(SEL_TOPK, n_sel)
    n_chunks = s // NSA_QBLOCK
    ratio = SEL_BLOCK // CMP_STRIDE
    pad_front = CMP_BLOCK // CMP_STRIDE - 1
    pad_back = n_sel * ratio - n_cmp
    ks_blk = k_slc.reshape(b, n_sel, SEL_BLOCK, g, d).transpose(0, 3, 1, 2, 4)
    vs_blk = v_slc.reshape(b, n_sel, SEL_BLOCK, g, d).transpose(0, 3, 1, 2, 4)
    kw = jnp.pad(k_win, ((0, 0), (NSA_WINDOW, 0), (0, 0), (0, 0)))
    vw = jnp.pad(v_win, ((0, 0), (NSA_WINDOW, 0), (0, 0), (0, 0)))
    cmp_end = jnp.arange(n_cmp) * CMP_STRIDE + CMP_BLOCK - 1
    b_idx = jnp.arange(b)[:, None, None, None]
    g_idx = jnp.arange(g)[None, :, None, None]
    win_off = jnp.arange(NSA_QBLOCK + NSA_WINDOW) - NSA_WINDOW
    sel_off = jnp.arange(SEL_BLOCK)
    blk_ids = jnp.arange(n_sel)

    def chunk(args):
        qc, gc, ci = args
        t = ci * NSA_QBLOCK + jnp.arange(NSA_QBLOCK)
        sc = jnp.einsum('bqgrd,bngd->bgrqn', qc, kc).astype(jnp.float32) * scale
        pc = masked_softmax(sc, cmp_end[None, :] <= t[:, None])
        oc = jnp.einsum('bgrqn,bngd->bqgrd', pc.astype(vc.dtype), vc)
        pg = jnp.pad(pc.sum(axis=2), ((0, 0), (0, 0), (0, 0), (pad_front, pad_back)))
        ps = sum(pg[..., o:o + n_sel * ratio:ratio] for o in range(ratio + pad_front))
        cur = t // SEL_BLOCK
        valid = blk_ids[None, :] <= cur[:, None]
        forced = (blk_ids[None, :] == 0) | (blk_ids[None, :] == cur[:, None]) | (blk_ids[None, :] == cur[:, None] - 1)
        score = jnp.where(valid, jnp.where(forced, jnp.inf, ps), -jnp.inf)
        _, idx = lax.top_k(score, topk)
        kg = ks_blk[b_idx, g_idx, idx]
        vg = vs_blk[b_idx, g_idx, idx]
        pos = idx[..., None] * SEL_BLOCK + sel_off
        tq = t[None, None, :, None, None]
        bias_s = bias_tab[t5_bucket(tq - pos), g_idx[..., None]]
        ss = jnp.einsum('bqgrd,bgqjkd->bgrqjk', qc, kg).astype(jnp.float32) * scale + jnp.moveaxis(bias_s, -1, 2)
        n_keys = topk * SEL_BLOCK
        mask_s = (pos <= tq).reshape(b, g, 1, NSA_QBLOCK, n_keys)
        p_s = masked_softmax(ss.reshape(b, g, r, NSA_QBLOCK, n_keys), mask_s)
        o_s = jnp.einsum('bgrqn,bgqnd->bqgrd', p_s.astype(vg.dtype), vg.reshape(b, g, NSA_QBLOCK, n_keys, d))
        kwc = lax.dynamic_slice_in_dim(kw, ci * NSA_QBLOCK, NSA_QBLOCK + NSA_WINDOW, axis=1)
        vwc = lax.dynamic_slice_in_dim(vw, ci * NSA_QBLOCK, NSA_QBLOCK + NSA_WINDOW, axis=1)
        spos = ci * NSA_QBLOCK + win_off
        dist = t[:, None] - spos[None, :]
        mask_w = (dist >= 0) & (dist < NSA_WINDOW) & (spos[None, :] >= 0)
        bias_w = jnp.transpose(bias_tab[t5_bucket(dist)], (2, 3, 0, 1))
        sw = jnp.einsum('bqgrd,bkgd->bgrqk', qc, kwc).astype(jnp.float32) * scale + bias_w
        p_w = masked_softmax(sw, mask_w)
        o_w = jnp.einsum('bgrqk,bkgd->bqgrd', p_w.astype(vwc.dtype), vwc)
        gs = jax.nn.sigmoid(gc.astype(jnp.float32)).astype(qc.dtype)
        return gs[..., 0:1] * oc + gs[..., 1:2] * o_s + gs[..., 2:3] * o_w

    q_ch = q.reshape(b, n_chunks, NSA_QBLOCK, g, r, d).swapaxes(0, 1)
    g_ch = gates.reshape(b, n_chunks, NSA_QBLOCK, g, r, 3).swapaxes(0, 1)
    out = lax.map(chunk, (q_ch, g_ch, jnp.arange(n_chunks)))
    return out.swapaxes(0, 1).reshape(b, s, g * r * d)

def swa_sink_attention(q, k, v, sinks, bias_tab):
    b, s, g, r, d = q.shape
    scale = d ** -0.5
    nb = s // SWA_QBLOCK
    qb = q.reshape(b, nb, SWA_QBLOCK, g, r, d)
    kb = k.reshape(b, nb, SWA_QBLOCK, g, d)
    vb = v.reshape(b, nb, SWA_QBLOCK, g, d)
    pad = ((0, 0), (1, 0), (0, 0), (0, 0), (0, 0))
    kk = jnp.concatenate([jnp.pad(kb, pad)[:, :-1], kb], axis=2)
    vv = jnp.concatenate([jnp.pad(vb, pad)[:, :-1], vb], axis=2)
    qi = jnp.arange(SWA_QBLOCK)[:, None]
    ki = jnp.arange(2 * SWA_QBLOCK)[None, :]
    dist = qi - ki + SWA_QBLOCK
    band = (dist >= 0) & (dist < SWA_WINDOW)
    first = (jnp.arange(nb) > 0)[:, None, None] | (ki >= SWA_QBLOCK)[None]
    mask = (band[None] & first)[None, :, None, None]
    bias = jnp.transpose(bias_tab[t5_bucket(dist)], (2, 3, 0, 1))
    sc = jnp.einsum('bnqgrd,bnkgd->bngrqk', qb, kk).astype(jnp.float32) * scale + bias
    sc = jnp.where(mask, sc, -jnp.inf)
    sink = sinks.astype(jnp.float32)[None, None, :, :, None, None]
    m = jnp.maximum(jnp.max(sc, axis=-1, keepdims=True), sink)
    e = jnp.exp(sc - m)
    p = e / (jnp.sum(e, axis=-1, keepdims=True) + jnp.exp(sink - m))
    o = jnp.einsum('bngrqk,bnkgd->bnqgrd', p.astype(vv.dtype), vv)
    return o.reshape(b, s, g * r * d)

def first_inputs(seed: int = 0) -> dict:
    key = jax.random.key(seed)
    ks = jax.random.split(key, 20)
    nrm = lambda k, shape, scale: jax.random.normal(k, shape, jnp.float32) * scale
    gain = lambda k: 1.0 + nrm(k, (DEPTH, D_MODEL), 0.05)
    cin = CMP_BLOCK * HEAD_DIM
    return {
        'x': nrm(ks[0], (BATCH, SEQ, D_MODEL), 1.0),
        'norm_mix_pre': gain(ks[1]),
        'norm_mix_post': gain(ks[2]),
        'norm_mlp_pre': gain(ks[3]),
        'norm_mlp_post': gain(ks[4]),
        'w_in': nrm(ks[5], (DEPTH, D_MODEL, IN_DIM), D_MODEL ** -0.5),
        'cmp_pos_k': nrm(ks[6], (DEPTH, CMP_BLOCK, HEAD_DIM), 0.5),
        'cmp_w1_k': nrm(ks[7], (DEPTH, cin, CMP_HIDDEN), cin ** -0.5),
        'cmp_w2_k': nrm(ks[8], (DEPTH, CMP_HIDDEN, HEAD_DIM), CMP_HIDDEN ** -0.5),
        'cmp_pos_v': nrm(ks[9], (DEPTH, CMP_BLOCK, HEAD_DIM), 0.5),
        'cmp_w1_v': nrm(ks[10], (DEPTH, cin, CMP_HIDDEN), cin ** -0.5),
        'cmp_w2_v': nrm(ks[11], (DEPTH, CMP_HIDDEN, HEAD_DIM), CMP_HIDDEN ** -0.5),
        'attn_sinks': nrm(ks[12], (DEPTH, SWA_HEADS), 0.5),
        'rel_bias': nrm(ks[13], (NUM_BUCKETS, N_BIAS_HEADS), 0.5),
        'w_up_nsa': nrm(ks[14], (DEPTH, NSA_Q_DIM, D_MODEL), NSA_Q_DIM ** -0.5),
        'w_up_swa': nrm(ks[15], (DEPTH, SWA_Q_DIM, D_MODEL), SWA_Q_DIM ** -0.5),
        'w_out': nrm(ks[16], (DEPTH, D_MODEL, D_MODEL), D_MODEL ** -0.5),
        'w_mlp_in': nrm(ks[17], (DEPTH, D_MODEL, D_FF), D_MODEL ** -0.5),
        'w_mlp_out': nrm(ks[18], (DEPTH, D_FF, D_MODEL), D_FF ** -0.5),
    }

def first_block(x, norm_mix_pre, norm_mix_post, norm_mlp_pre, norm_mlp_post, w_in,
              cmp_pos_k, cmp_w1_k, cmp_w2_k, cmp_pos_v, cmp_w1_v, cmp_w2_v,
              attn_sinks, rel_bias, w_up_nsa, w_up_swa, w_out, w_mlp_in, w_mlp_out):
    b, s, _ = x.shape
    bias_nsa = rel_bias[:, :NSA_HEADS].reshape(NUM_BUCKETS, NSA_GROUPS, NSA_REP)
    bias_swa = rel_bias[:, NSA_HEADS:].reshape(NUM_BUCKETS, SWA_KV_HEADS, SWA_REP)
    h = x
    for l in range(DEPTH):
        u = rms_norm(h, norm_mix_pre[l])
        (q_n, kc_n, vc_n, ks_n, vs_n, kw_n, vw_n, g_n,
         q_s, k_s, v_s, gate_a, gate_b) = jnp.split(u @ w_in[l], IN_OFFSETS, axis=-1)
        kvr = lambda t_: t_.reshape(b, s, NSA_GROUPS, HEAD_DIM)
        kc = compress_kv(kvr(kc_n), cmp_pos_k[l], cmp_w1_k[l], cmp_w2_k[l])
        vc = compress_kv(kvr(vc_n), cmp_pos_v[l], cmp_w1_v[l], cmp_w2_v[l])
        o_a = nsa_attention(q_n.reshape(b, s, NSA_GROUPS, NSA_REP, HEAD_DIM), kc, vc,
                            kvr(ks_n), kvr(vs_n), kvr(kw_n), kvr(vw_n),
                            g_n.reshape(b, s, NSA_GROUPS, NSA_REP, 3), bias_nsa)
        o_b = swa_sink_attention(q_s.reshape(b, s, SWA_KV_HEADS, SWA_REP, HEAD_DIM),
                                 k_s.reshape(b, s, SWA_KV_HEADS, HEAD_DIM),
                                 v_s.reshape(b, s, SWA_KV_HEADS, HEAD_DIM),
                                 attn_sinks[l].reshape(SWA_KV_HEADS, SWA_REP), bias_swa)
        y = jax.nn.sigmoid(gate_a) * (o_a @ w_up_nsa[l]) + jax.nn.sigmoid(gate_b) * (o_b @ w_up_swa[l])
        h = h + rms_norm(y @ w_out[l], norm_mix_post[l])
        u = rms_norm(h, norm_mlp_pre[l])
        f = jnp.square(jax.nn.relu(u @ w_mlp_in[l])) @ w_mlp_out[l]
        h = h + rms_norm(f, norm_mlp_post[l])
    return h


EPS = 1e-6
POOL_WINDOWS = (2, 4, 8, 16)
POOL_GROUPS = 4
POOL_WIDTH = D_MODEL // 2
POOL_GROUP_DIM = POOL_WIDTH // POOL_GROUPS
DN_HEADS = 8
DN_HEAD_DIM = 128
DN_WIDTH = DN_HEADS * DN_HEAD_DIM
CONV_WIDTH = 4
CHUNK = 64
PEER_HEADS = 8
N_KEYS = 128
N_EXPERTS = N_KEYS * N_KEYS
PEER_TOPK = 16
PEER_HALF = 128
PEER_QUERY_DIM = 2 * PEER_HALF
PEER_BLOCK = 64
SPLIT_POINTS = (
    POOL_WIDTH,
    POOL_WIDTH + 3 * DN_WIDTH,
    POOL_WIDTH + 4 * DN_WIDTH,
    POOL_WIDTH + 4 * DN_WIDTH + DN_HEADS,
    POOL_WIDTH + 4 * DN_WIDTH + 2 * DN_HEADS,
    POOL_WIDTH + 4 * DN_WIDTH + 2 * DN_HEADS + D_MODEL,
)
IN_COLS = POOL_WIDTH + 4 * DN_WIDTH + 2 * DN_HEADS + 2 * D_MODEL


def rmsnorm(x, w):
    xf = x.astype(jnp.float32)
    y = xf * lax.rsqrt(jnp.mean(xf * xf, axis=-1, keepdims=True) + EPS)
    return (y * w.astype(jnp.float32)).astype(x.dtype)

def l2norm(x):
    return x * lax.rsqrt(jnp.sum(x * x, axis=-1, keepdims=True) + EPS)

def pool_mixer(xa, pool_w, pool_scale):
    b, s, _ = xa.shape
    xf = xa.astype(jnp.float32)
    csum = jnp.cumsum(xf, axis=1)
    count = jnp.arange(1, s + 1, dtype=jnp.float32)[None, :, None]
    groups = []
    for g, win in enumerate(POOL_WINDOWS):
        sl = slice(g * POOL_GROUP_DIM, (g + 1) * POOL_GROUP_DIM)
        c = csum[..., sl]
        c_lag = jnp.pad(c, ((0, 0), (win, 0), (0, 0)))[:, :s]
        mean = (c - c_lag) / jnp.minimum(count, float(win))
        groups.append(mean - xf[..., sl])
    pooled = jnp.stack(groups, axis=2)
    y = jnp.einsum("bsgc,gcd->bsgd", pooled, pool_w.astype(jnp.float32))
    y = y.reshape(b, s, POOL_WIDTH) * pool_scale.astype(jnp.float32)
    return y.astype(xa.dtype)

def causal_dwconv(x, w):
    s = x.shape[1]
    k = w.shape[0]
    xp = jnp.pad(x, ((0, 0), (k - 1, 0), (0, 0)))
    y = xp[:, 0:s] * w[0]
    for j in range(1, k):
        y = y + xp[:, j:j + s] * w[j]
    return y

def gated_delta_rule(q, k, v, g, beta):
    b, h, s, dk = q.shape
    dv = v.shape[-1]
    nc = s // CHUNK
    q = q * (dk ** -0.5)
    k_beta = k * beta[..., None]
    v_beta = v * beta[..., None]

    def chunks(t):
        return t.reshape(b, h, nc, CHUNK, t.shape[-1])

    q, k, k_beta, v_beta = chunks(q), chunks(k), chunks(k_beta), chunks(v_beta)
    gc = jnp.cumsum(g.reshape(b, h, nc, CHUNK), axis=-1)
    tril = jnp.tril(jnp.ones((CHUNK, CHUNK), dtype=bool))
    strict = jnp.tril(jnp.ones((CHUNK, CHUNK), dtype=bool), -1)
    diff = gc[..., :, None] - gc[..., None, :]
    decay = jnp.where(tril, jnp.exp(jnp.where(tril, diff, 0.0)), 0.0)
    lower = jnp.where(strict, jnp.einsum("bhnid,bhnjd->bhnij", k_beta, k) * decay, 0.0)
    eye = jnp.eye(CHUNK, dtype=jnp.float32)
    t_inv = lax.linalg.triangular_solve(eye + lower, jnp.broadcast_to(eye, lower.shape),
                                        left_side=True, lower=True, unit_diagonal=True)
    u = jnp.einsum("bhnij,bhnjd->bhnid", t_inv, v_beta)
    w = jnp.einsum("bhnij,bhnjd->bhnid", t_inv, k_beta * jnp.exp(gc)[..., None])
    attn = jnp.where(tril, jnp.einsum("bhnid,bhnjd->bhnij", q, k) * decay, 0.0)

    def step(state, inp):
        q_i, k_i, u_i, w_i, a_i, g_i = inp
        v_new = u_i - jnp.einsum("bhcd,bhde->bhce", w_i, state)
        o = (jnp.einsum("bhcd,bhde->bhce", q_i * jnp.exp(g_i)[..., None], state)
             + jnp.einsum("bhij,bhje->bhie", a_i, v_new))
        g_last = g_i[..., -1]
        k_dec = k_i * jnp.exp(g_last[..., None] - g_i)[..., None]
        state = state * jnp.exp(g_last)[..., None, None] + jnp.einsum("bhcd,bhce->bhde", k_dec, v_new)
        return state, o

    xs = tuple(jnp.moveaxis(t, 2, 0) for t in (q, k, u, w, attn, gc))
    state0 = jnp.zeros((b, h, dk, dv), dtype=jnp.float32)
    _, o = lax.scan(step, state0, xs)
    return jnp.moveaxis(o, 0, 2).reshape(b, h, s, dv)

def deltanet_branch(qkv, z, beta_logit, a_logit, conv_w, a_log, dt_bias, dn_norm_w):
    b, s, _ = qkv.shape
    out_dtype = qkv.dtype
    f32 = jnp.float32
    qkv = jax.nn.silu(causal_dwconv(qkv.astype(f32), conv_w.astype(f32)))
    q, k, v = jnp.split(qkv, 3, axis=-1)

    def heads(t):
        return t.reshape(b, s, DN_HEADS, DN_HEAD_DIM).transpose(0, 2, 1, 3)

    q = l2norm(heads(q))
    k = l2norm(heads(k))
    v = heads(v)
    beta = jax.nn.sigmoid(beta_logit.astype(f32)).transpose(0, 2, 1)
    g = (-jnp.exp(a_log.astype(f32))
         * jax.nn.softplus(a_logit.astype(f32) + dt_bias.astype(f32))).transpose(0, 2, 1)
    o = gated_delta_rule(q, k, v, g, beta).transpose(0, 2, 1, 3)
    zf = z.astype(f32).reshape(b, s, DN_HEADS, DN_HEAD_DIM)
    o = rmsnorm(o, dn_norm_w) * jax.nn.silu(zf)
    return o.reshape(b, s, DN_WIDTH).astype(out_dtype)

def peer_ffn(x, w_query, keys_1, keys_2, expert_down, expert_up):
    b, s, d = x.shape
    f32 = jnp.float32
    q = (x @ w_query).astype(f32).reshape(b, s, PEER_HEADS, 2, PEER_HALF)
    s1 = jnp.einsum("bshc,hkc->bshk", q[..., 0, :], keys_1.astype(f32))
    s2 = jnp.einsum("bshc,hkc->bshk", q[..., 1, :], keys_2.astype(f32))
    v1, i1 = lax.top_k(s1, PEER_TOPK)
    v2, i2 = lax.top_k(s2, PEER_TOPK)
    cand_score = (v1[..., :, None] + v2[..., None, :]).reshape(b, s, PEER_HEADS, PEER_TOPK * PEER_TOPK)
    cand_idx = (i1[..., :, None] * N_KEYS + i2[..., None, :]).reshape(b, s, PEER_HEADS, PEER_TOPK * PEER_TOPK)
    top_score, pos = lax.top_k(cand_score, PEER_TOPK)
    experts = jnp.take_along_axis(cand_idx, pos, axis=-1)
    gates = jax.nn.softmax(top_score, axis=-1)

    nb = s // PEER_BLOCK
    xb = x.reshape(b, nb, PEER_BLOCK, d).transpose(1, 0, 2, 3)
    eb = experts.reshape(b, nb, PEER_BLOCK, PEER_HEADS, PEER_TOPK).transpose(1, 0, 2, 3, 4)
    gb = gates.reshape(b, nb, PEER_BLOCK, PEER_HEADS, PEER_TOPK).transpose(1, 0, 2, 3, 4)

    def block(args):
        xi, ei, gi = args
        u = jnp.take(expert_down, ei, axis=0)
        act = jax.nn.gelu(jnp.einsum("btd,bthkd->bthk", xi, u).astype(f32), approximate=False)
        vv = jnp.take(expert_up, ei, axis=0)
        return jnp.einsum("bthk,bthkd->btd", (gi * act).astype(x.dtype), vv)

    y = lax.map(block, (xb, eb, gb))
    return y.transpose(1, 0, 2, 3).reshape(b, s, d)

def second_inputs(seed: int = 0) -> dict:
    key = jax.random.key(seed)
    ks = jax.random.split(key, 20)
    f32 = jnp.float32

    def nrm(k, shape, scale):
        return scale * jax.random.normal(k, shape, f32)

    def gain(k, shape):
        return 1.0 + 0.05 * jax.random.normal(k, shape, f32)

    dt = jnp.exp(jax.random.uniform(ks[7], (DEPTH, DN_HEADS), f32, math.log(1e-3), math.log(1e-1)))
    dt_bias = dt + jnp.log(-jnp.expm1(-dt))
    a_log = jnp.log(jax.random.uniform(ks[8], (DEPTH, DN_HEADS), f32, 1.0, 16.0))
    return {
        "x": jax.random.normal(ks[0], (BATCH, SEQ, D_MODEL), f32),
        "mix_norm_w": gain(ks[1], (DEPTH, D_MODEL)),
        "w_in": nrm(ks[2], (DEPTH, D_MODEL, IN_COLS), D_MODEL ** -0.5),
        "pool_w": nrm(ks[3], (DEPTH, POOL_GROUPS, POOL_GROUP_DIM, POOL_GROUP_DIM), POOL_GROUP_DIM ** -0.5),
        "pool_scale": 1.0 + 0.1 * jax.random.normal(ks[4], (DEPTH, POOL_WIDTH), f32),
        "conv_w": nrm(ks[5], (DEPTH, CONV_WIDTH, 3 * DN_WIDTH), CONV_WIDTH ** -0.5),
        "a_log": a_log,
        "dt_bias": dt_bias,
        "dn_norm_w": gain(ks[6], (DEPTH, DN_HEAD_DIM)),
        "w_pool_up": nrm(ks[9], (DEPTH, POOL_WIDTH, D_MODEL), POOL_WIDTH ** -0.5),
        "w_dn_up": nrm(ks[10], (DEPTH, DN_WIDTH, D_MODEL), DN_WIDTH ** -0.5),
        "w_mix_out": nrm(ks[11], (DEPTH, D_MODEL, D_MODEL), D_MODEL ** -0.5),
        "ffn_norm_w": gain(ks[12], (DEPTH, D_MODEL)),
        "peer_w_query": nrm(ks[13], (DEPTH, D_MODEL, PEER_HEADS * PEER_QUERY_DIM), D_MODEL ** -0.5),
        "peer_keys_1": nrm(ks[14], (DEPTH, PEER_HEADS, N_KEYS, PEER_HALF), PEER_HALF ** -0.5),
        "peer_keys_2": nrm(ks[15], (DEPTH, PEER_HEADS, N_KEYS, PEER_HALF), PEER_HALF ** -0.5),
        "peer_down": nrm(ks[16], (DEPTH, N_EXPERTS, D_MODEL), D_MODEL ** -0.5),
        "peer_up": nrm(ks[17], (DEPTH, N_EXPERTS, D_MODEL), PEER_HEADS ** -0.5),
        "final_norm_w": gain(ks[18], (D_MODEL,)),
    }

def second_block(x, mix_norm_w, w_in, pool_w, pool_scale, conv_w, a_log, dt_bias, dn_norm_w,
              w_pool_up, w_dn_up, w_mix_out, ffn_norm_w, peer_w_query, peer_keys_1,
              peer_keys_2, peer_down, peer_up, final_norm_w):
    h = x
    for l in range(DEPTH):
        xn = rmsnorm(h, mix_norm_w[l])
        proj = xn @ w_in[l]
        xa, qkv, z, beta_logit, a_logit, gate_a, gate_b = jnp.split(proj, SPLIT_POINTS, axis=-1)
        y_a = pool_mixer(xa, pool_w[l], pool_scale[l]) @ w_pool_up[l]
        y_b = deltanet_branch(qkv, z, beta_logit, a_logit, conv_w[l], a_log[l], dt_bias[l],
                              dn_norm_w[l]) @ w_dn_up[l]
        merged = jax.nn.sigmoid(gate_a) * y_a + jax.nn.sigmoid(gate_b) * y_b
        h = h + merged @ w_mix_out[l]
        h = h + peer_ffn(rmsnorm(h, ffn_norm_w[l]), peer_w_query[l], peer_keys_1[l],
                         peer_keys_2[l], peer_down[l], peer_up[l])
    return rmsnorm(h, final_norm_w)


def setup_inputs(seed=0):
    out = dict(first_inputs(seed))
    for name, value in second_inputs(seed + 1).items():
        if name != "x":
            out[name + "_2"] = value
    return out


def reference(
    x, norm_mix_pre, norm_mix_post, norm_mlp_pre, norm_mlp_post, w_in, cmp_pos_k, cmp_w1_k,
    cmp_w2_k, cmp_pos_v, cmp_w1_v, cmp_w2_v, attn_sinks, rel_bias, w_up_nsa, w_up_swa, w_out,
    w_mlp_in, w_mlp_out, mix_norm_w_2, w_in_2, pool_w_2, pool_scale_2, conv_w_2, a_log_2,
    dt_bias_2, dn_norm_w_2, w_pool_up_2, w_dn_up_2, w_mix_out_2, ffn_norm_w_2, peer_w_query_2,
    peer_keys_1_2, peer_keys_2_2, peer_down_2, peer_up_2, final_norm_w_2,
):
    x = first_block(
        x, norm_mix_pre, norm_mix_post, norm_mlp_pre, norm_mlp_post, w_in, cmp_pos_k, cmp_w1_k,
        cmp_w2_k, cmp_pos_v, cmp_w1_v, cmp_w2_v, attn_sinks, rel_bias, w_up_nsa, w_up_swa,
        w_out, w_mlp_in, w_mlp_out,
    )
    return second_block(
        x, mix_norm_w_2, w_in_2, pool_w_2, pool_scale_2, conv_w_2, a_log_2, dt_bias_2,
        dn_norm_w_2, w_pool_up_2, w_dn_up_2, w_mix_out_2, ffn_norm_w_2, peer_w_query_2,
        peer_keys_1_2, peer_keys_2_2, peer_down_2, peer_up_2, final_norm_w_2,
    )


_drawn_inputs = setup_inputs


def setup_inputs(seed=0):
    import zlib

    import numpy as np

    out = dict(_drawn_inputs(seed))
    spreads = {}
    factors = {'attn_sinks': 6.288, 'dn_norm_w_2': 4.043, 'ffn_norm_w_2': 2.957}
    for name, (base, spread) in spreads.items():
        noise = np.random.default_rng([zlib.crc32(name.encode()), seed]).standard_normal(out[name].shape)
        drawn = base * np.exp(spread * noise) if base else spread * noise
        out[name] = jnp.asarray(drawn.astype(out[name].dtype))
    for name, factor in factors.items():
        out[name] = (out[name] * factor).astype(out[name].dtype)
    return out
```

```python
import concourse.bass as bass
from concourse import mybir
from contextlib import ExitStack

T = 256
D = 1024
UNITS1 = 4 + 4 + 5 + 4 + 16 + 8 + 8 + 64
UNITS2 = 24 + 4 + 24 + 4 + 8 + 8 + 16
DOWN = 128
UP = 128
UNITS = UNITS1 + UNITS2 + DOWN + UP


class Sem:

    def __init__(self, handle):
        self.handle = handle
        self.value = 0

    def add(self, n):
        self.value += n
        return (self, self.value)


class Lane:

    def __init__(self, sem):
        self.sem = sem
        self.queue = []
        self.passed = {}

    def wait(self, *after):
        for a in after:
            if a is None:
                continue
            if isinstance(a, list):
                self.wait(*a)
                continue
            sem, value = a
            if self.passed.get(id(sem), 0) < value:
                self.passed[id(sem)] = value
                self.queue.append(lambda e, s=sem, v=value: e.wait_ge(s.handle, v))

    def do(self, fn, after=(), signal=True):
        self.wait(*after)
        if not signal:
            self.queue.append(fn)
            return None
        self.queue.append(lambda e: fn(e).then_inc(self.sem.handle, 1))
        return self.sem.add(1)

    def dma(self, out, in_, sem, *after, **kw):
        self.wait(*after)
        self.queue.append(lambda e: e.dma_start(out, in_, **kw).then_inc(sem.handle, 16))
        return sem.add(16)

    def emit(self, engine):
        for fn in self.queue:
            fn(engine)


class Vec(Lane):
    def tt(self, out, in0, in1, op, *after):
        return self.do(lambda e: e.tensor_tensor(out, in0, in1, op), after)

    def ts(self, out, in0, s1, s2, op0, op1, *after):
        if s2 is None:
            return self.do(lambda e: e.tensor_scalar(out, in0, s1, None, op0), after)
        return self.do(lambda e: e.tensor_scalar(out, in0, s1, s2, op0, op1), after)

    def stt(self, out, in0, s, in1, op0, op1, *after):
        return self.do(lambda e: e.scalar_tensor_tensor(out, in0, s, in1, op0, op1), after)

    def copy(self, out, in_, *after):
        return self.do(lambda e: e.tensor_copy(out, in_), after)

    def recip(self, out, in_, *after):
        return self.do(lambda e: e.reciprocal(out, in_), after)

    def memset(self, out, v, *after):
        return self.do(lambda e: e.memset(out, v), after)

    def reduce(self, out, in_, op, *after):
        return self.do(lambda e: e.tensor_reduce(out, in_, mybir.AxisListType.X, op), after)


class Act(Lane):
    def act(self, out, in_, func, *after, **kw):
        return self.do(lambda e: e.activation(out, in_, func, **kw), after)


class Pe(Lane):
    def mm(self, out, lhsT, rhs, start, stop, *after, signal=False):
        return self.do(lambda e: e.matmul(out, lhsT, rhs, start=start, stop=stop, skip_group_check=True),
                       after, signal)

    def tr(self, out, in_, ident, *after, signal=False):
        return self.do(lambda e: e.transpose(out, in_, ident), after, signal)


def program(nc, I, out):
    F32 = mybir.dt.float32
    F32R = mybir.dt.float32r
    U32 = mybir.dt.uint32
    ALU = mybir.AluOpType
    AF = mybir.ActivationFunctionType

    RR, RW = 4, 3
    LS = RW - 1
    LD = LS + RR

    ctx = ExitStack()
    with ctx:
        sb = lambda name, shape, dt: ctx.enter_context(nc.sbuf_tensor(name, shape, dt))
        sem = lambda name: Sem(ctx.enter_context(nc.semaphore(name)))

        pe, act, dve, pool, sp = Pe(sem("pe")), Act(sem("act")), Vec(sem("dve")), Vec(sem("pool")), Lane(sem("sp"))
        big = sb("big", [128, 32768], F32)
        XH = sb("xh", [128, 8, T], F32R)
        XL = sb("xl", [128, 8, T], F32R)
        GH = sb("gh", [128, 8, T], F32R)
        GL = sb("gl", [128, 8, T], F32R)
        raw = sb("raw", [128, RR, 1024], F32)
        WH = sb("wh", [128, RW, 1024], F32R)
        WL = sb("wl", [128, RW, 1024], F32R)
        ident = sb("ident", [128, 128], F32)
        ones = sb("ones", [128, 128], F32)
        misc = sb("misc", [128, 1536], F32)
        ET = misc[:, 0:512].rearrange("p (n t) -> p n t", n=2)
        GATE = misc[:, 512:768]
        VG = misc[:, 768:1280].rearrange("p (a b) -> p a b", b=128)
        TG = misc[:, 1280:1536]
        cols = sb("cols", [128, I["cols"].shape[1]], F32)
        banks = [ctx.enter_context(nc.psum_tensor(f"bank{i}", [128, 512], F32)) for i in range(8)]
        idle = [[] for _ in range(8)]

        class Arena:
            def __init__(self, at, end):
                self.at, self.end = at, end

            def take(self, n, m=None):
                a = big[:, self.at:self.at + n]
                self.at += n
                assert self.at <= self.end, (self.at, self.end)
                return a if m is None else a.rearrange("p (a b) -> p a b", b=m)

        def take_bank(i):
            free = idle[i]
            idle[i] = []
            return banks[i], free

        s_const = sem("const")
        pool.dma(cols[:, :], I["cols"], s_const)
        pool.dma(ident[:, :], I["ident"], s_const)
        c_ready = (s_const, 32)
        ones_ready = dve.memset(ones[:, :], 1.0)
        COL = {}
        n = 0
        for name, w in (("mix_pre", 8), ("mix_post", 8), ("mlp_pre", 8), ("mlp_post", 8), ("mix2", 8), ("ffn", 8),
                        ("pool_scale", 4), ("conv", 96), ("dn", 1), ("eps", 1)):
            COL[name] = cols[:, n:n + w]
            n += w
        EPS = COL["eps"]

        class Stream:

            def __init__(self):
                self.used = self.cut = self.got = 0
                self.load_sem = [sem(f"load{i}") for i in range(RR)]
                self.load = {}
                self.lo = {}
                self.hi = {}
                self.done = {}

            def fetch(self, upto):
                while self.got < min(upto, UNITS) and (self.got < RR or self.got - RR in self.lo):
                    v = self.got
                    self.load[v] = sp.dma(raw[:, v % RR, :], I["wst"][v], self.load_sem[v % RR],
                                          self.lo.get(v - RR))
                    self.got += 1

            def split(self, upto):
                while self.cut < min(upto, UNITS):
                    v = self.cut
                    self.hi[v] = act.act(WH[:, v % RW, :], raw[:, v % RR, :], AF.Copy,
                                         self.load[v], self.done.get(v - RW))
                    self.lo[v] = dve.tt(WL[:, v % RW, :], raw[:, v % RR, :],
                                        WH[:, v % RW, :].bitcast(F32), ALU.subtract, self.load[v], self.hi[v],
                                        self.done.get(v - RW))
                    self.cut += 1

            def take(self):
                v = self.used
                self.used += 1
                self.fetch(v + LD + 1)
                self.split(v + LS + 1)
                self.fetch(v + LD + 1)
                self.v = v
                return WH[:, v % RW, :], WL[:, v % RW, :], [self.hi[v]], [self.lo[v]]

            def release(self, token):
                self.done[self.v] = token

        st = Stream()

        def fm_unit(out, free, xh, xl, ready, nk=8, k0=0, first=True, last=True, groups=1, widths=128):
            wh, wl, h_ok, l_ok = st.take()
            tok = None
            for g in range(groups):
                for k in range(nk):
                    c = k * groups + g
                    a = wh[:, c * 128:(c + 1) * 128]
                    b = wl[:, c * 128:(c + 1) * 128]
                    f = first and k == 0 and g == 0
                    o = out[g]
                    pe.mm(o, a, xh(k0 + k), f, False, free, h_ok, ready[k0 + k])
                    pe.mm(o, a, xl(k0 + k), False, False)
                    end = k == nk - 1 and g == groups - 1
                    tok = pe.mm(o, b, xh(k0 + k), False, last and k == nk - 1, l_ok, signal=end)
            st.release(tok)
            return tok

        def split_into(h, l, src, *after):
            a = act.act(h, src, AF.Copy, *after)
            b = dve.tt(l, src, h.bitcast(F32), ALU.subtract, a, *after)
            return [a, b]

        main_at = [0]

        def main_bank():
            i = main_at[0] % 3
            main_at[0] += 1
            return i

        pending = []

        def flush():
            while pending:
                pending.pop(0)()

        sides = []

        def tick(n=1):
            for _ in range(n):
                for s in list(sides):
                    if next(s, "end") == "end":
                        sides.remove(s)

        def unit(mm, evac):
            r = mm()
            flush()
            pending.append(lambda: evac(r))
            tick()

        def proj_unit(evac, ready, xh=None, xl=None):
            xh = xh or (lambda k: XH[:, k, :])
            xl = xl or (lambda k: XL[:, k, :])
            i = main_bank()
            b, free = take_bank(i)

            def mm():
                return fm_unit([b[:, 0:T]], free, xh, xl, ready)

            def ev(tok):
                idle[i] = [evac(b[:, 0:T], tok)]
            unit(mm, ev)

        def col_rstd(st_bank, free, squares, dst, n, tmp):
            for c, (sq, ok) in enumerate(squares):
                tok = pe.mm(st_bank[:, 0:T], ones[:, :], sq, c == 0, c == len(squares) - 1, free if c == 0 else None,
                            ok, ones_ready, signal=c == len(squares) - 1)
            a = act.act(tmp, st_bank[:, 0:T], AF.Sqrt, tok, c_ready, scale=1.0 / n, bias=EPS)
            return dve.recip(dst, tmp, a), a

        A = Arena(0, 32768)
        H = A.take(2048, T)
        RS = A.take(256)
        TMP = A.take(1024, T)
        SQ = A.take(2048, T)
        s_x = [sem(f"x{i}") for i in range(2)]
        x_ok = []
        for i in range(2):
            x_ok += [sp.dma(H[:, 4 * i:4 * i + 4, :], I["xT"][:, 4 * i:4 * i + 4, :], s_x[i])] * 4
        st.fetch(3)

        def norm_split(gain, ready, stat_bank, free=()):
            b, bank_free = take_bank(stat_bank)
            squares = []
            for c in range(8):
                squares.append((SQ[:, c, :], act.act(SQ[:, c, :], H[:, c, :], AF.Square, ready[c], *free)))
            rs, stat_read = col_rstd(b, bank_free, squares, RS[:, :], D, TMP[:, 3, :])
            idle[stat_bank] = [stat_read]
            out = []
            for c in range(8):
                m = dve.stt(SQ[:, c, :], H[:, c, :], gain[:, c:c + 1], RS[:, :], ALU.mult, ALU.mult, rs, c_ready)
                out.append(split_into(XH[:, c, :], XL[:, c, :], SQ[:, c, :], m, *free))
            return out

        X = norm_split(COL["mix_pre"], x_ok, 7)

        QN_QS = A.take(2048, T)
        QN, QS = QN_QS[:, 0:4, :], QN_QS[:, 4:8, :]
        KS, KW, KK = A.take(T), A.take(T), A.take(T)
        V = A.take(2 * 384, 384)
        GT = A.take(48, 24)
        SA, SB = A.take(2048, T), A.take(2048, T)
        BT = A.take(4096, T)
        KC2, VC2 = A.take(2 * 258, 258), A.take(2 * 258, 258)
        CX = A.take(480, 30)
        CV = A.take(480, 30)
        W1K = A.take(4096, 256)
        W1V = A.take(4096, 256)
        MIS = A.take(1600)
        s_l1 = sem("l1")
        POS = MIS[:, 0:32]
        W2K = MIS[:, 32:32 + 256].rearrange("p (a b) -> p a b", b=128)
        W2V = MIS[:, 288:288 + 128].rearrange("p (a b) -> p a b", b=64)
        RELB = MIS[0:32, 416:432]
        ONEH = MIS[0:32, 432:432 + 384]
        BMASK = MIS[0:16, 816:816 + 384]
        SINK = MIS[:, 1200:1208]
        CM = MIS[:, 1208:1208 + 60].rearrange("p (a b) -> p a b", b=30)
        BD = MIS[:, 1268:1276]
        SEL = MIS[0:30, 1280:1280 + 128]
        for a, b in ((RELB, I["relb"]), (ONEH, I["oneh"]), (BMASK, I["bmask"]), (POS, I["pos"]), (W2K, I["w2k"]),
                     (W2V, I["w2v"]), (SINK, I["sinks"]),
                     (CM, I["cmask"]), (BD, I["bdmask"]), (SEL, I["sel"])):
            l1_ok = pool.dma(a, b, s_l1)
        s_w1k, s_w1v = sem("w1k"), sem("w1v")
        scr = nc.dram_tensor("toeplitz", [16, 16, 384], F32).ap()

        bt_ok = []

        def bias_side():
            VB = QS[0:16, :, :].rearrange("p a b -> p (a b)")[:, 0:384]
            b, free = take_bank(7)
            t = pe.mm(b[0:16, 0:384], RELB, ONEH, True, True, free, l1_ok, signal=True)
            t = dve.tt(VB, b[0:16, 0:384], BMASK, ALU.add, t)
            idle[7] = [t]
            s_w, s_r = sem("toep_w"), sem("toep_r")
            t = pool.dma(scr, VB[:, None, :].broadcast_to([16, 16, 384]), s_w, t)
            for a in range(8):
                src = bass.AP(scr.tensor, 127 - 16 * a, [[383, 16], [6144, 16], [1, 256]])
                t = pool.dma(BT[16 * a:16 * a + 16, :, :], src, s_r, t if a == 0 else None)
            bt_ok.append(t)
            vb_read.append(t)
            yield

        vb_read = []

        tok = {}
        s_sw = {}

        def ev_kc(dst, name):
            def f(ps, t):
                a = act.act(dst[0:64, 0, 1:257], ps[0:64, :], AF.Copy, t)
                b = act.act(dst[64:128, 1, 0:256], ps[64:128, :], AF.Copy, t)
                s = sem("sw_" + name)
                pool.dma(dst[64:128, 0, 0:256], dst[0:64, 0, 1:257], s, a)
                d = pool.dma(dst[0:64, 1, 1:257], dst[64:128, 1, 0:256], s, b)
                tok[name] = [b, d]
                return b
            return f

        def ev_copy(dst, name, *after):
            def f(ps, t):
                tok[name] = act.act(dst, ps, AF.Copy, t, *after)
                return tok[name]
            return f

        sides.append(bias_side())
        tick()
        w1k_ok = sp.dma(W1K, I["w1k"], s_w1k)
        proj_unit(ev_kc(KC2, "kc"), X)
        proj_unit(ev_kc(VC2, "vc"), X)
        w1v_ok = sp.dma(W1V, I["w1v"], s_w1v)
        proj_unit(ev_copy(KS[:, :], "ks"), X)
        proj_unit(ev_copy(KW[:, :], "kw"), X)
        for c in range(4):
            proj_unit(ev_copy(QN[:, c, :], f"qn{c}"), X)
        HID = MIS[:, 1408:1408 + 120].rearrange("p (a b) -> p a b", b=30)
        KCT = MIS[:, 1528:1558]

        def compress_side():
            while "vc" not in tok:
                yield
            ready = []
            for src, dst, col, name in ((KC2, CX, 0, "kc"), (VC2, CV, 16, "vc")):
                v = src[:, :, 1:257].rearrange("p g (n j two) -> p g j n two", j=8, two=2)
                o = dst.rearrange("p j (g n) -> p g j n", n=15)
                for half in range(2):
                    p = POS[:, col + 8 * half:col + 8 * half + 8]
                    for g in range(2):
                        ready.append(dve.tt(o[:, g, 8 * half:8 * half + 8, :], v[:, g, :, half:half + 15, 0],
                                            p[:, :, None].broadcast_to([128, 8, 15]), ALU.add, tok[name], l1_ok))
            yield
            b, free = take_bank(7)
            hid = b[:, 0:128].rearrange("p (a b) -> p a b", b=32)[:, :, 0:30]
            for i, (w, x, w_ok) in enumerate(((W1K, CX, w1k_ok), (W1K, CX, w1k_ok), (W1V, CV, w1v_ok), (W1V, CV, w1v_ok))):
                for j in range(16):
                    t = pe.mm(hid[:, i, :], w[:, j, 128 * (i % 2):128 * (i % 2) + 128], x[:, j, :], j == 0, j == 15,
                              free, ready, w_ok, signal=j == 15)
                yield
            tok["w1"] = t
            t = act.act(HID, hid, AF.Gelu_apprx_tanh, t)
            yield
            for i in range(2):
                k = pe.mm(b[:, 128:158], W2K[:, i, :], HID[:, i, :], i == 0, i == 1, t, l1_ok, signal=True)
            for i in range(2):
                v = pe.mm(b[0:30, 160:224], HID[:, 2 + i, :], W2V[:, i, :], i == 0, i == 1, signal=True)
            tok["kct"] = act.act(KCT, b[:, 128:158], AF.Copy, k, v)
            v = act.act(VCS, b[0:30, 160:224], AF.Copy, v)
            yield
            v = pe.mm(b[:, 256:320], SEL, VCS, True, True, v, signal=True)
            t = dve.tt(BDV, b[:, None, 256:320].broadcast_to([128, 8, 64]), BD[:, :, None].broadcast_to([128, 8, 64]),
                       ALU.mult, v, tok["w1"])
            tok["bdv"] = t
            idle[7] = [t, tok["kct"]]

        Z = W1K.rearrange("p a b -> p (a b)")
        BDV = Z[:, 0:512].rearrange("p (a b) -> p a b", b=64)
        OA = Z[:, 512:1536].rearrange("p (t a b) -> p t a b", t=2, b=64)
        OB = Z[:, 1536:2560].rearrange("p (t a b) -> p t a b", t=2, b=64)
        PTS = [Z[:, 2560 + 512 * i:3072 + 512 * i] for i in range(2)]
        TMPO = Z[:, 3584:4096].rearrange("p (a b) -> p a b", b=64)
        Z = W1V.rearrange("p a b -> p (a b)")
        S = [Z[:, 512 * i:512 * i + 512].rearrange("p (a b) -> p a b", b=T) for i in range(4)]
        VCS = Z[0:30, 2048:2112]
        PCT = Z[:, 2240:2368]
        Z = A.take(384)
        SC = Z[:, 256:384].rearrange("p (a b) -> p a b", b=16)
        ST = Z[:, 0:64].rearrange("p (a b) -> p a b", b=8)
        NM = Z[:, 64:128].rearrange("p (a b) -> p a b", b=8)
        SUM = Z[:, 128:192].rearrange("p (a b) -> p a b", b=8)
        GS = Z[:, 192:240].rearrange("p (a b) -> p a b", b=24)
        NS = Z[:, 240:248]
        W8 = Z[:, 248:256]

        o_ok = [None, None]

        def compressed(tile):
            ts = slice(128 * tile, 128 * tile + 128)
            i = 6 + tile % 2
            b, free = take_bank(5)
            ob, ofree = take_bank(i)
            m = CM[:, tile:tile + 1, :]
            x = SC[:, :, 0:15]
            masked = []
            for g, bank in ((0, b), (1, ob)):
                r = slice(64 * g, 64 * g + 64)
                sc = bank[:, 0:64].rearrange("p (a b) -> p a b", b=16)[:, :, 0:15]
                for c in range(4):
                    t = pe.mm(sc[:, c, :], QN[r, c, ts], KCT[r, 15 * g:15 * g + 15], True, True, free, ofree,
                              tok["kct"], tok[f"qn{c}"], signal=c == 3)
                masked.append(dve.tt(SC.rearrange("p (c g) n -> p g c n", g=2)[:, g, :, 0:15], sc,
                                     m[:, :, 0:15].broadcast_to([128, 4, 15]), ALU.add, t, tok["w1"], tok["bdv"],
                                     tok.get("pct")))
            t = masked
            yield
            t = dve.reduce(ST[:, 0, :], x, ALU.max, t)
            t = dve.tt(x, x, ST[:, 0, :, None].broadcast_to([128, 8, 15]), ALU.subtract, t)
            t = act.act(x, x, AF.Exp, t, scale=0.125)
            yield
            t = dve.tt(x, x, m[:, :, 15:30].broadcast_to([128, 8, 15]), ALU.mult, t)
            s = dve.reduce(ST[:, 1, :], x, ALU.add, t)
            s = dve.ts(ST[:, 1, :], ST[:, 1, :], 1e-30, None, ALU.max, None, s)
            s = dve.recip(ST[:, 2, :], ST[:, 1, :], s)
            s = dve.tt(ST[:, 3, :], ST[:, 2, :], GS[:, tile, 0:8], ALU.mult, s, tok["gs"])
            t = pe.tr(b[:, 128:256], SC.rearrange("p a b -> p (a b)"), ident[:, :], t, pad_ok, c_ready, signal=True)
            t = act.act(PCT, b[:, 128:256], AF.Copy, t)
            idle[5] = [t]
            yield
            t = pe.mm(ob[:, :], PCT, BDV.rearrange("p a b -> p (a b)"), True, True, masked, t, signal=True)
            tok["pct"] = t
            yield
            t = dve.tt(OA[:, tile, :, :], ob[:, :].rearrange("p (a b) -> p a b", b=64),
                       ST[:, 3, :, None].broadcast_to([128, 8, 64]), ALU.mult, t, s)
            idle[i] = [t]
            o_ok[0] = t

        step_at = [0]
        pt_free = [[], []]
        s_free = [[] for _ in range(4)]

        def branch(tile, kind):
            q, k, v0 = ((QN, KS, 0), (QN, KW, 128), (QS, KK, 256))[kind]
            n = 128 * (tile + 1)
            lo = 256 - n
            ob_i = 6 + (2 * tile + kind + 1) % 2
            row = 3 * tile + kind
            parts = []
            for c in range(4):
                at = step_at[0]
                step_at[0] += 1
                sb_i = 3 + at % 2
                b, free = take_bank(sb_i)
                s = S[at % 4]
                w = s_free[at % 4]
                ps = b[:, :].rearrange("p (a b) -> p a b", b=T)
                g = c % 2
                r = slice(64 * g, 64 * g + 64)
                for i in range(2):
                    cc = c // 2 * 2 + i
                    scores = pe.mm(ps[:, i, 0:n], q[r, cc, 128 * tile:128 * tile + 128], k[r, 0:n], True, True, free,
                                   tok[("qn", "qn", "qs")[kind] + str(cc)], tok[("ks", "kw", "kk")[kind]],
                                   signal=i == 1)
                for i in range(2):
                    h = c // 2 * 4 + 2 * i + g
                    init = NS[:, h:h + 1] if kind == 2 else 3e38
                    nm = NM[:, row, h:h + 1]
                    t = dve.do(lambda e, o=s[:, i, 0:n], i0=ps[:, i, 0:n],
                               i1=BT[:, (8 if kind == 2 else 0) + h, lo:256], init=init, nm=nm:
                               e.tensor_tensor_reduce(o, i0, i1, -0.125, init, ALU.add, ALU.min, nm),
                               [scores, bt_ok, w, tok["w1"], tok["ns"]])
                    idle[sb_i] = [t]
                    t = act.act(s[:, i, 0:n], s[:, i, 0:n], AF.Exp, t, scale=-1.0, bias=nm,
                                accum_out=SUM[:, row, h:h + 1])
                    parts.append(t)
                yield
                if c:
                    transposed(c - 1, at - 1, parts, tile, ob_i, v0)
                if c > 1:
                    values(c - 2, at - 2, tile, ob_i, v0)
            transposed(3, at, parts, tile, ob_i, v0)
            values(2, at - 1, tile, ob_i, v0)
            yield
            t = values(3, at, tile, ob_i, v0)
            yield
            if kind == 2:
                e = dve.tt(W8, NM[:, row, :], NS, ALU.subtract, parts[-1])
                e = act.act(W8, W8, AF.Exp, e)
                e = dve.tt(SUM[:, row, :], SUM[:, row, :], W8, ALU.add, e)
                s = dve.recip(ST[:, 4, :], SUM[:, row, :], e)
            else:
                s = dve.recip(ST[:, 4, :], SUM[:, row, :], parts[-1])
                s = dve.tt(ST[:, 4, :], ST[:, 4, :], GS[:, tile, 8 + 8 * kind:16 + 8 * kind], ALU.mult, s, tok["gs"])
            o = banks[ob_i][:, :].rearrange("p (a b) -> p a b", b=64)
            sc = ST[:, 4, :, None].broadcast_to([128, 8, 64])
            if kind == 2:
                o_ok[1] = dve.tt(OB[:, tile, :, :], o, sc, ALU.mult, t, s)
                idle[ob_i] = [o_ok[1]]
            else:
                t = dve.tt(TMPO, o, sc, ALU.mult, t, s, o_ok[0])
                idle[ob_i] = [t]
                o_ok[0] = dve.tt(OA[:, tile, :, :], OA[:, tile, :, :], TMPO, ALU.add, t)

        pt_ok = {}

        def transposed(c, at, parts, tile, ob_i, v0):
            b, free = take_bank(5)
            nb = tile + 1
            for g in range(2):
                for j in range(nb):
                    t = pe.tr(b[:, (g * nb + j) * 128:(g * nb + j) * 128 + 128], S[at % 4][:, g, 128 * j:128 * j + 128],
                              ident[:, :], free, parts[2 * c + g], c_ready, signal=True)
            s_free[at % 4] = [t]
            t = act.act(PTS[at % 2][:, 0:256 * nb], b[:, 0:256 * nb], AF.Copy, t, pt_free[at % 2])
            idle[5] = [t]
            pt_ok[at] = t

        def values(c, at, tile, ob_i, v0):
            nb = tile + 1
            free = []
            if c == 0:
                _, free = take_bank(ob_i)
            ob = banks[ob_i]
            for i in range(2):
                for j in range(nb):
                    h = c // 2 * 4 + 2 * i + c % 2
                    v = v0 + 64 * (c % 2)
                    t = pe.mm(ob[:, 64 * h:64 * h + 64], PTS[at % 2][:, (i * nb + j) * 128:(i * nb + j) * 128 + 128],
                              V[:, j, v:v + 64], j == 0, j == nb - 1, free, pt_ok[at], tok["v"],
                              signal=i == 1 and j == nb - 1)
            pt_free[at % 2] = [t]
            return t

        up_in = {}

        def to_features(src, chunk0, tile, i):
            b, free = take_bank(i)
            for c in range(4):
                t = pe.tr(b[:, 128 * c:128 * c + 128], src[:, tile, 2 * c:2 * c + 2, :].rearrange("p a b -> p (a b)"),
                          ident[:, :], free, o_ok, signal=c == 3)
            ps = b[:, :].rearrange("p (a b) -> p a b", b=128)
            ts = slice(128 * tile, 128 * tile + 128)
            r = split_into(GH[:, chunk0:chunk0 + 4, ts], GL[:, chunk0:chunk0 + 4, ts], ps, t)
            idle[i] = list(r)
            for c in range(4):
                up_in.setdefault(chunk0 + c, []).extend(r)

        def attention_side():
            while "kct" not in tok:
                yield
            tok["ns"] = dve.ts(NS, SINK, -1.0, None, ALU.mult, None, l1_ok, tok["w1"])
            while "v" not in tok:
                yield
            for tile in range(2):
                yield from compressed(tile)
                yield from branch(tile, 0)
                yield from branch(tile, 1)
                to_features(OA, 0, tile, 5)
                yield from branch(tile, 2)
                to_features(OB, 4, tile, 5)
            tok["attn"] = True

        pad_ok = None
        sides.append(compress_side())
        sides.append(attention_side())
        pad_ok = dve.memset(SC[:, :, 15:16], 0.0)
        proj_unit(ev_copy(KK[:, :], "kk"), X)
        for c in range(4):
            proj_unit(ev_copy(QS[:, c, :], f"qs{c}", vb_read), X)

        i0, i1 = main_bank(), main_bank()
        (b0, f0), (b1, f1) = take_bank(i0), take_bank(i1)
        for u in range(4):
            def mm(u=u):
                wh, wl, h_ok, l_ok = st.take()
                for kk in range(2):
                    k = 2 * u + kk
                    w = slice(512 * kk, 512 * kk + 512)
                    for b, f, ts in ((b0, f0, slice(0, 128)), (b1, f1, slice(128, 256))):
                        pe.mm(b[:, :], XH[:, k, ts], wh[:, w], k == 0, False, f if u == 0 else None, h_ok)
                        pe.mm(b[:, :], XL[:, k, ts], wh[:, w], False, False)
                        t = pe.mm(b[:, :], XH[:, k, ts], wl[:, w], False, k == 7, l_ok, signal=kk == 1)
                st.release(t)
                return t

            def ev(t, u=u):
                if u < 3:
                    return
                for tile, (b, i) in enumerate(((b0, i0), (b1, i1))):
                    r = [act.act(V[:, tile, :], b[:, 0:384], AF.Copy, t),
                         act.act(GT[:, tile, :], b[:, 384:408], AF.Tanh, t, scale=0.5)]
                    idle[i] = r
                tok["gs"] = dve.ts(GS[:, :, :], GT, 1.0, 0.5, ALU.add, ALU.mult, r)
                tok["v"] = r
            unit(mm, ev)

        def ev_tanh(dst, name):
            def f(ps, t):
                tok[name] = act.act(dst, ps, AF.Tanh, t, scale=0.5)
                return tok[name]
            return f

        for c in range(8):
            proj_unit(ev_tanh(SA[:, c, :], f"ga{c}"), X)
        for c in range(8):
            proj_unit(ev_tanh(SB[:, c, :], f"gb{c}"), X)
        while "attn" not in tok:
            tick()
        flush()
        Y = QN_QS
        Y2 = [TMP[:, 0:2, :].rearrange("p a b -> p (a b)"), TMP[:, 2:4, :].rearrange("p a b -> p (a b)")]
        gated = {}
        y_ok = {}
        for i in range(4):
            for n, (gate, chunk0) in enumerate(((SA, 0), (SB, 4))):
                bi = main_bank()
                b, free = take_bank(bi)

                def mm(b=b, free=free, chunk0=chunk0):
                    return fm_unit([b[:, 0:T], b[:, T:2 * T]], free, lambda k: GH[:, k, :], lambda k: GL[:, k, :],
                                   up_in, nk=4, k0=chunk0, groups=2)

                def ev(t, i=i, n=n, b=b, bi=bi, gate=gate):
                    g = gate[:, 2 * i:2 * i + 2, :].rearrange("p a b -> p (a b)")
                    names = [tok[("ga", "gb")[n] + str(c)] for c in (2 * i, 2 * i + 1)]
                    y_free = gated.get("y")
                    a = dve.stt(Y2[n], g, 1.0, b[:, :], ALU.add, ALU.mult, t, names, y_free)
                    idle[bi] = [a]
                    if n == 0:
                        gated["a"] = a
                        return
                    s = dve.tt(Y2[0], Y2[0], Y2[1], ALU.add, a, gated["a"])
                    for c in range(2):
                        src = Y2[0][:, T * c:T * c + T]
                        h = act.act(XH[:, 2 * i + c, :], src, AF.Copy, s, x_free, scale=0.5)
                        l = dve.stt(XL[:, 2 * i + c, :], src, 0.5, XH[:, 2 * i + c, :].bitcast(F32), ALU.mult,
                                    ALU.subtract, h, x_free)
                        y_ok[2 * i + c] = [h, l]
                    gated["y"] = l
                x_free = st.done[32]
                unit(mm, ev)
        flush()
        def out_units(ready, dst, sq, xh=None, xl=None):
            done = []
            for c in range(8):
                def f(ps, t, c=c):
                    a = act.act(dst[:, c, :], ps, AF.Copy, t)
                    b = dve.tt(sq[:, c, :], dst[:, c, :], dst[:, c, :], ALU.mult, a)
                    done.append((a, b))
                    return a
                proj_unit(f, ready, xh, xl)
            flush()
            return done

        def add_normed(y, gain, squares, rs, tmp, bank):
            b, free = take_bank(bank)
            t, read = col_rstd(b, free, squares, rs, D, tmp)
            idle[bank] = [read]
            out = []
            for c in range(8):
                m = dve.stt(y[:, c, :], y[:, c, :], gain[:, c:c + 1], rs, ALU.mult, ALU.mult, t)
                out.append(dve.tt(H[:, c, :], H[:, c, :], y[:, c, :], ALU.add, m))
            return out

        done = out_units(y_ok, Y, SQ)
        h_ok = add_normed(Y, COL["mix_post"], [(SQ[:, c, :], done[c][1]) for c in range(8)], RS, TMP[:, 0, :], 7)
        gain = COL["mlp_pre"]
        u_ok = []
        squares = []
        x_free = st.done[st.v]
        for c in range(8):
            a = act.act(XH[:, c, :], H[:, c, :], AF.Copy, h_ok[c], x_free, scale=gain[:, c:c + 1])
            b = dve.stt(XL[:, c, :], H[:, c, :], gain[:, c:c + 1], XH[:, c, :].bitcast(F32), ALU.mult, ALU.subtract,
                        a, x_free)
            u_ok.append([a, b])
            squares.append((SQ[:, c, :], act.act(SQ[:, c, :], H[:, c, :], AF.Square, h_ok[c])))

        def mlp_stat_side():
            yield
            yield
            b, free = take_bank(7)
            t, read = col_rstd(b, free, squares, RS, D, TMP[:, 0, :])
            idle[7] = [read]
            tok["rs2"] = dve.tt(RS, RS, RS, ALU.mult, t)

        sides.append(mlp_stat_side())
        hid_ok = {}
        hid_free = {}
        HT = [TMP[:, 1, :], TMP[:, 2, :]]
        ht_free = [None, None]

        def mlp_in(q):
            for i in range(4):
                def f(ps, t, n=4 * q + i):
                    e = act.act(HT[n % 2], ps, AF.Relu, t, ht_free[n % 2])
                    r = dve.tt(HT[n % 2], HT[n % 2], HT[n % 2], ALU.mult, e)
                    free = hid_free.get(n - 8)
                    a = act.act(GH[:, n % 8, :], HT[n % 2], AF.Copy, r, free)
                    b = dve.tt(GL[:, n % 8, :], HT[n % 2], GH[:, n % 8, :].bitcast(F32), ALU.subtract, a, free)
                    ht_free[n % 2] = b
                    hid_ok[n % 8] = [a, b]
                    return e
                proj_unit(f, u_ok)

        def mlp_out(q):
            for i in range(4):
                b, free = take_bank(3 + i) if q == 0 else (banks[3 + i], None)

                def mm(q=q, i=i, b=b, free=free):
                    return fm_unit([b[:, 0:T], b[:, T:2 * T]], free, lambda k: GH[:, k, :], lambda k: GL[:, k, :],
                                   hid_ok, nk=4, k0=4 * (q % 2), groups=2, first=q == 0, last=q == 7)

                def ev(t, q=q, i=i):
                    for k in range(4):
                        hid_free[4 * q + k] = t
                    if q == 7:
                        f_done.append((i, t))
                        if i:
                            evac_f(i - 1)
                unit(mm, ev)

        f_done = []
        f_sq = {}

        def evac_f(i):
            t = f_done[i][1]
            for c in range(2):
                n = 2 * i + c
                r = dve.tt(Y[:, n, :], banks[3 + i][:, T * c:T * c + T], RS, ALU.mult, t, tok["rs2"])
                f_sq[n] = act.act(SQ[:, n, :], Y[:, n, :], AF.Square, r)
            idle[3 + i] = [r]

        mlp_in(0)
        for q in range(1, 8):
            mlp_in(q)
            mlp_out(q - 1)
        mlp_out(7)
        flush()
        evac_f(3)
        h_ok = add_normed(Y, COL["mlp_post"], [(SQ[:, c, :], f_sq[c]) for c in range(8)], RS, TMP[:, 0, :], 7)
        later_jobs = []

        def later(n, fn):
            later_jobs.append([n, fn])

        def clock_side():
            while True:
                for job in later_jobs:
                    job[0] -= 1
                while later_jobs and later_jobs[0][0] <= 0:
                    later_jobs.pop(0)[1]()
                yield
        clock = clock_side()
        sides.append(clock)

        tok.clear()
        A = Arena(2048 + 256 + 1024 + 2048, 32768)
        QKV = A.take(24 * T, T)
        Q, K, VF = QKV[:, 0:8, :], QKV[:, 8:16, :], QKV[:, 16:24, :]
        SZ = A.take(2048, T)
        GA, GB = A.take(2048, T), A.take(2048, T)
        XA = A.take(1024, T)
        KB = A.take(2048, T)
        DC = A.take(2048, 128)
        LT = A.take(2048, 128)
        TT = A.take(2048, 128)
        VB = A.take(2048, 128)
        KD = A.take(1024, 128)
        CT = [A.take(256) for _ in range(2)]
        SM = A.take(1900)
        TRI, SUF, NEGM = SM[:, 0:128], SM[:, 128:256], SM[:, 256:384]
        LM = SM[:, 384:768].rearrange("p (a b) -> p a b", b=128)
        BAW = SM[:, 768:896]
        ALOG, DTB = SM[:, 896:904], SM[:, 904:912]
        B2 = SM[:, 912:928].rearrange("p (a b) -> p a b", b=8)
        G2 = SM[:, 928:944].rearrange("p (a b) -> p a b", b=8)
        E2, U2, W2 = (SM[:, 944 + 16 * i:960 + 16 * i].rearrange("p (a b) -> p a b", b=8) for i in range(3))
        NGC = SM[:, 992:1008].rearrange("p (a b) -> p a b", b=8)
        EGC = SM[:, 1008:1024].rearrange("p (a b) -> p a b", b=8)
        ESF = SM[:, 1024:1040].rearrange("p (a b) -> p a b", b=8)
        RQ = SM[:, 1040:1056].rearrange("p (a b) -> p a b", b=8)
        SS = SM[:, 1056:1072].rearrange("p (a b) -> p a b", b=8)
        BE = SM[:, 1072:1088].rearrange("p (a b) -> p a b", b=8)
        PW = SM[:, 1100:1612].rearrange("p (a b) -> p a b", b=128)
        T0 = KB.rearrange("p a b -> p (a b)").rearrange("p (a b) -> p a b", b=128)
        LMT = SQ.rearrange("p a b -> p (a b)").rearrange("p (a b) -> p a b", b=128)
        VN = VF.rearrange("p a b -> p (a b)").rearrange("p (a b) -> p a b", b=128)

        s_l2 = sem("l2")
        for a, b in ((TRI, I["tri"]), (SUF, I["suf"]), (NEGM, I["negm"]), (LM, I["lmask"]), (BAW, I["baw"]),
                     (ALOG, I["alog"]), (DTB, I["dtb"]), (PW, I["poolw"])):
            l2_ok = pool.dma(a, b, s_l2, h_ok)

        X = norm_split(COL["mix2"], h_ok, 7, free=[st.done[st.v], list(f_sq.values())])
        baw = split_into(GH[:, 0, 0:128], GL[:, 0, 0:128], BAW, l2_ok, st.done[st.v])
        b, free = take_bank(7)
        for tile in range(2):
            o = b[:, 16 * tile:16 * tile + 16]
            ts = slice(128 * tile, 128 * tile + 128)
            for k in range(8):
                w = slice(16 * k, 16 * k + 16)
                pe.mm(o, XH[:, k, ts], GH[:, 0, w], k == 0, False, free, X[k], baw)
                pe.mm(o, XL[:, k, ts], GH[:, 0, w], False, False)
                t = pe.mm(o, XH[:, k, ts], GL[:, 0, w], False, k == 7, signal=True)
        ba = b[:, 0:32].rearrange("p (a b) -> p a b", b=16)

        def both(x):
            return x[:, None, :].broadcast_to([128, 2, 8])

        def gates_side():
            e = act.act(B2, ba[:, :, 0:8], AF.Exp, t, scale=-1.0)
            c = dve.tt(G2, ba[:, :, 8:16], both(DTB), ALU.add, t, l2_ok, e)
            idle[7] = [e, c]
            e = dve.ts(B2, B2, 1.0, None, ALU.add, None, e)
            tok["beta"] = dve.recip(B2, B2, e)
            a = act.act(ALOG, ALOG, AF.Exp, l2_ok)
            u = act.act(U2, G2, AF.Abs, c)
            u = act.act(E2, U2, AF.Exp, u, scale=-1.0)
            yield
            r = dve.ts(U2, E2, 2.0, None, ALU.add, None, u)
            r = dve.recip(U2, U2, r)
            z = dve.tt(E2, E2, U2, ALU.mult, r)
            r = dve.tt(U2, E2, E2, ALU.mult, z)
            w = dve.ts(W2, U2, 1.0 / 19, 1.0 / 17, ALU.mult, ALU.add, r)
            for n in (15, 13, 11, 9, 7, 5, 3, 1):
                w = dve.tt(W2, W2, U2, ALU.mult, w)
                w = dve.ts(W2, W2, 1.0 / n, None, ALU.add, None, w)
            yield
            w = dve.tt(W2, W2, E2, ALU.mult, w)
            w = dve.ts(W2, W2, 2.0, None, ALU.mult, None, w)
            g = dve.stt(G2, G2, 0.0, W2, ALU.max, ALU.add, w)
            g = dve.tt(G2, G2, both(ALOG), ALU.mult, g, a)
            g = dve.ts(G2, G2, -1.0, None, ALU.mult, None, g)
            tok["g"] = g
            yield
            b, free = take_bank(7)
            for tile in range(2):
                c = pe.mm(b[:, 8 * tile:8 * tile + 8], TRI, G2[:, tile, :], True, True, free, g, signal=True)
                d = pe.mm(b[:, 16 + 8 * tile:24 + 8 * tile], SUF, G2[:, tile, :], True, True, signal=True)
            gc = b[:, 0:16].rearrange("p (a b) -> p a b", b=8)
            sf = b[:, 16:32].rearrange("p (a b) -> p a b", b=8)
            yield
            n = dve.ts(NGC, gc, -1.0, None, ALU.mult, None, c, d)
            x = act.act(EGC, gc, AF.Exp, n)
            y = act.act(ESF, sf, AF.Exp)
            tok["be"] = dve.tt(BE, B2, EGC, ALU.mult, x, tok["beta"])
            tok["gc"] = [n, x, y]
            idle[7] = [n, y]

        def ev_conv(u):
            def f(ps, t):
                w = COL["conv"][:, 4 * u:4 * u + 4]
                c = CT[u % 2]
                t = act.act(c, ps, AF.Copy, t, tok.get(f"ct{u % 2}"), scale=w[:, 3:4])
                for j, n in ((2, 1), (1, 2), (0, 3)):
                    t = dve.stt(c[:, n:T], ps[:, 0:T - n], w[:, j:j + 1], c[:, n:T], ALU.mult, ALU.add, t)
                last = t
                a = act.act(QKV[:, u, :], c, AF.Silu, t)
                tok[f"ct{u % 2}"] = a
                tok[f"c{u}"] = a
                if u < 16:
                    c = act.act(c, QKV[:, u, :], AF.Square, a)
                    tok[f"ct{u % 2}"] = c
                    later(1, lambda: sums(u, c))
                return last
            return f

        qb, qfree = [None], [None]

        def sums(u, t):
            h = u % 8
            if u < 8:
                if qb[0] is None:
                    qb[0], qfree[0] = take_bank(6)
                for tile in range(2):
                    r = pe.mm(qb[0][:, 8 * tile + h:8 * tile + h + 1], CT[u % 2][:, 128 * tile:128 * tile + 128],
                              ones[:, 0:1], True, True, qfree[0], t, ones_ready, signal=True)
                tok[f"ct{u % 2}"] = tok["rq"] = r
                return
            i = 3 + h % 2
            b, free = take_bank(i)
            r = pe.mm(b[:, 0:T], ones[:, :], CT[u % 2], True, True, free, t, signal=True)
            tok[f"ct{u % 2}"] = r
            r = act.act(SQ[:, h, :], b[:, 0:T], AF.Copy, r, X)
            idle[i] = [r]
            tok["sums"] = r

        order = []
        for h in range(8):
            order += [h, 8 + h, 16 + h]
        for u in order:
            proj_unit(ev_conv(u), X)

        def ev_act(dst, name, func, **kw):
            def f(ps, t):
                tok[name] = act.act(dst, ps, func, t, **kw)
                return tok[name]
            return f

        for c in range(8):
            proj_unit(ev_act(SZ[:, c, :], f"z{c}", AF.Silu), X)
        flush()
        tick()
        while later_jobs:
            tick()
        side_at = [0]

        def side_bank():
            i = 3 + side_at[0] % 4
            side_at[0] += 1
            b, free = take_bank(i)
            return i, b, free

        def quad(x):
            return x[:, :].rearrange("p (a b) -> p a b", b=128)

        s_d1, s_d2, s_d3, s_d4 = (sem(f"diag{i}") for i in range(4))
        scr1 = nc.dram_tensor("diag_in", [16, 8, 16, 16], F32).ap()
        scr2 = nc.dram_tensor("diag_out", [2, 16, 8, 16, 16], F32).ap()

        def delta_side():
            c_ok = [tok[f"c{u}"] for u in range(24)]
            t = act.act(SQ, SQ, AF.Sqrt, tok["sums"], bias=EPS)
            q = act.act(RQ, qb[0][:, 0:16].rearrange("p (a b) -> p a b", b=8), AF.Sqrt, tok["rq"], bias=EPS)
            idle[6] = [q]
            q = dve.recip(RQ, RQ, q)
            tok["rq"] = dve.ts(RQ, RQ, 128 ** -0.5, None, ALU.mult, None, q)
            yield from gates_side()
            k_ok = []
            for i in range(4):
                r = dve.recip(SQ[:, 2 * i:2 * i + 2, :], SQ[:, 2 * i:2 * i + 2, :], t)
                k_ok.append(dve.tt(K[:, 2 * i:2 * i + 2, :], K[:, 2 * i:2 * i + 2, :], SQ[:, 2 * i:2 * i + 2, :],
                                   ALU.mult, r, c_ok))
                yield
            zero = [pool.memset(T0, 0.0) if False else None]
            lt_ok, at_ok = [], []
            for i in range(4):
                n, b, free = side_bank()
                for j in range(4):
                    h, tile = 2 * i + j // 2, j % 2
                    t = pe.mm(quad(b)[:, j, :], B2[:, tile, h:h + 1].broadcast_to([128, 128]), ident[:, :], True, True,
                              free, tok["beta"], signal=j == 3)
                kb = dve.tt(KB[:, 2 * i:2 * i + 2, :], K[:, 2 * i:2 * i + 2, :],
                            b[:, :].rearrange("p (a b) -> p a b", b=T), ALU.mult, t, k_ok[i])
                idle[n] = [kb]
                n, b, free = side_bank()
                for j in range(4):
                    h, tile = 2 * i + j // 2, j % 2
                    t = pe.mm(quad(b)[:, j, :], G2[:, tile, h:h + 1].broadcast_to([128, 128]), TRI, True, True,
                              free, tok["g"], signal=j == 3)
                d = DC[:, 4 * i:4 * i + 4, :]
                t = dve.tt(d, quad(b), NEGM[:, None, :].broadcast_to([128, 4, 128]), ALU.add, t)
                idle[n] = [t]
                dd = []
                for j in range(4):
                    h, tile = 2 * i + j // 2, j % 2
                    dd.append(act.act(d[:, j, :], d[:, j, :], AF.Exp, t, tok["gc"], bias=NGC[:, tile, h:h + 1]))
                yield
                n, b, free = side_bank()
                for j in range(4):
                    h, ts = 2 * i + j // 2, slice(128 * (j % 2), 128 * (j % 2) + 128)
                    t = pe.mm(quad(b)[:, j, :], K[:, h, ts], KB[:, h, ts], True, True, free, kb, signal=j == 3)
                t = dve.tt(LT[:, 4 * i:4 * i + 4, :], quad(b), d, ALU.mult, t, dd)
                idle[n] = [t]
                lt_ok.append(t)
                n, b, free = side_bank()
                for j in range(4):
                    h, ts = 2 * i + j // 2, slice(128 * (j % 2), 128 * (j % 2) + 128)
                    t = pe.mm(quad(b)[:, j, :], K[:, h, ts], Q[:, h, ts], True, True, free, c_ok, signal=j == 3)
                t = dve.tt(d, quad(b), d, ALU.mult, t, lt_ok[-1])
                idle[n] = [t]
                at_ok.append(t)
                yield
            for i in range(8):
                p = slice(16 * i, 16 * i + 16)
                t = pool.dma(scr1[:, i, :, :].rearrange("a j i -> j a i"), LT[p, :, p], s_d1, lt_ok)
            BL = CT[0].rearrange("p (a b) -> p a b", b=16)
            BT_ = CT[1].rearrange("p (a b) -> p a b", b=16)
            t = pool.dma(CT[0], scr1.rearrange("a b j i -> (a b) (j i)"), s_d2, t, c_ok, tok["ct0"])
            m = dve.memset(CT[1], 0.0, c_ok, tok["ct1"])
            m = dve.memset(CT[1][:, 0:256:17], 1.0, m)
            vb_ok = []
            for i in range(4):
                n, b, free = side_bank()
                for j in range(4):
                    h, ts = 2 * i + j // 2, slice(128 * (j % 2), 128 * (j % 2) + 128)
                    r = pe.tr(quad(b)[:, j, :], VF[:, h, ts], ident[:, :], free, c_ok, signal=j == 3)
                    
                beta = B2[:, :, 2 * i:2 * i + 2].rearrange("p t h -> p h t")[:, :, :, None].broadcast_to([128, 2, 2, 128])
                r = dve.tt(VB[:, 4 * i:4 * i + 4, :].rearrange("p (h t) e -> p h t e", t=2),
                           quad(b).rearrange("p (h t) e -> p h t e", t=2), beta, ALU.mult, r, tok["beta"])
                idle[n] = [r]
                vb_ok.append(r)
                if i % 2:
                    yield
            kd_ok = []
            for i in range(2):
                n, b, free = side_bank()
                for j in range(4):
                    r = pe.tr(quad(b)[:, j, :], K[:, 4 * i + j, 0:128], ident[:, :], free, k_ok, signal=j == 3)
                r = dve.tt(KD[:, 4 * i:4 * i + 4, :], quad(b), ESF[:, 0, 4 * i:4 * i + 4, None].broadcast_to([128, 4, 128]),
                           ALU.mult, r, tok["gc"])
                idle[n] = [r]
                kd_ok.append(r)
            z = [pool.memset(T0, 0.0, lt_ok), pool.memset(TT, 0.0)]
            yield
            TP = TMP[:, 0, :]
            for j in range(15):
                n = 15 - j
                o = TP[:, 0:n * (j + 1)].rearrange("p (a b) -> p a b", b=j + 1)
                p = dve.tt(o, BL[:, j, j + 1:16, None].broadcast_to([128, n, j + 1]),
                           BT_[:, j:j + 1, 0:j + 1].broadcast_to([128, n, j + 1]), ALU.mult, t, m)
                x = BT_[:, j + 1:16, 0:j + 1]
                m = dve.tt(x, x, o, ALU.subtract, p)
                if j % 5 == 4:
                    yield
            r = dve.copy(BL, BT_.rearrange("p i c -> p c i"), m)
            for n, src in ((0, CT[1]), (1, CT[0])):
                w = pool.dma(scr2[n].rearrange("a b i c -> (a b) (i c)"), src, s_d3, m, r)
            for n, dst in ((0, T0), (1, TT)):
                for i in range(8):
                    p = slice(16 * i, 16 * i + 16)
                    w = pool.dma(dst[p, :, p], scr2[n][:, i, :, :].rearrange("a i c -> i a c"), s_d4, w, z)
            yield
            yield
            t_ok = [[w, w] for _ in range(4)]
            for level in range(3):
                for i in range(4):
                    s4 = slice(4 * i, 4 * i + 4)
                    m = dve.tt(LMT[:, s4, :], LT[:, s4, :], LM[:, level:level + 1, :].broadcast_to([128, 4, 128]),
                               ALU.mult, tok.get(f"y{i}"), k_ok, lt_ok)
                    n, b, free = side_bank()
                    for j in range(4):
                        y = pe.mm(quad(b)[:, j, :], LMT[:, 4 * i + j, :], T0[:, 4 * i + j, :], True, True, free, m,
                                  t_ok[i], signal=j == 3)
                    tok[f"y{i}"] = y
                    y = act.act(LMT[:, s4, :], quad(b), AF.Copy, y)
                    idle[n] = [y]
                    t_ok[i].append(y)
                    if i % 2:
                        yield
                for i in range(4):
                    s4 = slice(4 * i, 4 * i + 4)
                    res = []
                    zs = []
                    for which in ((1,) if level == 2 else (0, 1)):
                        n, b, free = side_bank()
                        for j in range(4):
                            hc = 4 * i + j
                            if which == 0:
                                z = pe.mm(quad(b)[:, j, :], TT[:, hc, :], LMT[:, hc, :], True, True, free, t_ok[i],
                                          signal=j == 3)
                            else:
                                z = pe.mm(quad(b)[:, j, :], LMT[:, hc, :], TT[:, hc, :], True, True, free, t_ok[i],
                                          signal=j == 3)
                        zs.append((which, n, b, z))
                    for which, n, b, z in zs:
                        x = (T0, TT)[which][:, s4, :]
                        r = dve.tt(x, x, quad(b), ALU.subtract, [q[3] for q in zs])
                        idle[n] = [r]
                        res.append(r)
                    t_ok[i] = res
                    tok[f"y{i}"] = zs[-1][3]
                    if i % 2:
                        yield
            hc = lambda h, tile: 2 * h + tile
            o_done = []
            OR = LT
            for i in range(2):
                hs = range(4 * i, 4 * i + 4)

                def product(lhs, rhs, *after):
                    n, b, free = side_bank()
                    for j, h in enumerate(hs):
                        t = pe.mm(quad(b)[:, j, :], lhs(h), rhs(h), True, True, free, *after, signal=j == 3)
                    return n, b, t
                rows = lambda x, tile: x[:, 8 * i + tile:8 * i + 8:2, :]
                n, b, t = product(lambda h: TT[:, hc(h, 0), :], lambda h: VB[:, hc(h, 0), :], t_ok, vb_ok)
                v0 = act.act(rows(VN, 0), quad(b), AF.Copy, t, vb_ok)
                idle[n] = [v0]
                yield
                n, b, t = product(lambda h: KD[:, h, :], lambda h: VN[:, hc(h, 0), :], v0, kd_ok)
                s = act.act(T0[:, 4 * i:4 * i + 4, :], quad(b), AF.Copy, t, tok["y0"], tok["y1"], tok["y2"], tok["y3"])
                idle[n] = [s]
                n, b, t = product(lambda h: DC[:, hc(h, 0), :], lambda h: VN[:, hc(h, 0), :], v0, at_ok)
                o = act.act(rows(OR, 0), quad(b), AF.Copy, t)
                idle[n] = [o]
                o_done.append(o)
                yield
                n, b, t = product(lambda h: K[:, h, 128:256], lambda h: T0[:, h, :], s)
                be = BE[:, 1, 4 * i:4 * i + 4, None].broadcast_to([128, 4, 128])
                tmp = TMP[:, 0:2, :].rearrange("p a b -> p (a b)").rearrange("p (a b) -> p a b", b=128)
                r = dve.tt(tmp, quad(b), be, ALU.mult, t, tok["be"], tok.get("o1"))
                idle[n] = [r]
                r = dve.tt(rows(VB, 1), rows(VB, 1), tmp, ALU.subtract, r)
                n2, b2, t2 = product(lambda h: Q[:, h, 128:256], lambda h: T0[:, h, :], s)
                eg = EGC[:, 1, 4 * i:4 * i + 4, None].broadcast_to([128, 4, 128])
                r2 = dve.tt(rows(OR, 1), quad(b2), eg, ALU.mult, t2, tok["gc"])
                idle[n2] = [r2]
                yield
                n, b, t = product(lambda h: TT[:, hc(h, 1), :], lambda h: VB[:, hc(h, 1), :], r)
                v1 = act.act(rows(VN, 1), quad(b), AF.Copy, t)
                idle[n] = [v1]
                yield
                n, b, t = product(lambda h: DC[:, hc(h, 1), :], lambda h: VN[:, hc(h, 1), :], v1)
                o = dve.tt(rows(OR, 1), rows(OR, 1), quad(b), ALU.add, t, r2)
                tok["o1"] = r
                idle[n] = [o]
                o_done.append(o)
                yield
            acc = []
            for h in range(8):
                for tile in range(2):
                    acc.append(act.act(TMP[:, 3, 0:128], OR[:, hc(h, tile), :], AF.Square, o_done,
                                       acc[-1] if acc else None, accum_out=SS[:, tile, h:h + 1]))
                if h % 4 == 3:
                    yield
            r = dve.tt(SS, SS, RQ, ALU.mult, acc, tok["rq"])
            r = dve.tt(SS, SS, RQ, ALU.mult, r)
            r = act.act(SS, SS, AF.Sqrt, r, scale=1.0 / 128, bias=EPS)
            r = dve.recip(SS, SS, r)
            r = dve.tt(SS, SS, RQ, ALU.mult, r)
            for i in range(4):
                x = OR[:, 4 * i:4 * i + 4, :].rearrange("p (h t) e -> p h t e", t=2)
                sc = SS[:, :, 2 * i:2 * i + 2].rearrange("p t h -> p h t")[:, :, :, None].broadcast_to([128, 2, 2, 128])
                x_ok = dve.tt(x, x, sc, ALU.mult, r, acc)
                n, b, free = side_bank()
                for j in range(4):
                    t = pe.tr(quad(b)[:, j, :], OR[:, 4 * i + j, :], ident[:, :], free, x_ok, signal=j == 3)
                o = VB[:, 4 * i:4 * i + 4, :]
                m = dve.stt(o.rearrange("p a b -> p (a b)"), b[:, :], COL["dn"],
                            SZ[:, 2 * i:2 * i + 2, :].rearrange("p a b -> p (a b)"), ALU.mult, ALU.mult, t,
                            [tok[f"z{c}"] for c in range(8)])
                idle[n] = [m]
                gh = GH[:, 2 * i:2 * i + 2, :].rearrange("p a b -> p (a b)")
                gl = GL[:, 2 * i:2 * i + 2, :].rearrange("p a b -> p (a b)")
                while "pooled" not in tok:
                    yield
                r2 = split_into(gh, gl, o.rearrange("p a b -> p (a b)"), m, tok["pooled"])
                for c in (2 * i, 2 * i + 1):
                    dn_ok[c] = r2
                yield

        dn_ok = {}
        sides.append(delta_side())
        for c in range(4):
            proj_unit(ev_act(XA[:, c, :], f"xa{c}", AF.Copy), X)

        s_inv = sem("inv")
        INV = CTI = None
        pool_in = {}

        def pool_side():
            inv = TMP[:, 2, :]
            for g in range(4):
                while f"xa{g}" not in tok:
                    yield
                x = XA[:, g, :]
                a, b = POOLT
                prev, t = x, tok[f"xa{g}"]
                for i in range(g + 1):
                    n = 1 << i
                    dst = (a, b)[i % 2]
                    u = [pool.copy(dst[:, 0:n], prev[:, 0:n], t, tok.get("pool_free")),
                         pool.tt(dst[:, n:T], prev[:, n:T], prev[:, 0:T - n], ALU.add)]
                    prev, t = dst, u
                iv = pool.dma(INVT, I["inv"][:, g, :], s_inv, tok.get("pool_free"))
                t = pool.tt(prev, prev, INVT, ALU.mult, t, iv)
                t = pool.tt(x, prev, x, ALU.subtract, t)
                tok["pool_free"] = t
                i, b, free = side_bank()
                yield
                t = pe.mm(b[:, 0:T], PW[:, g, :], x, True, True, free, t, l2_ok, signal=True)
                sc = COL["pool_scale"][:, g:g + 1]
                h = act.act(GH[:, g, :], b[:, 0:T], AF.Copy, t, baw_free, scale=sc)
                l = dve.stt(GL[:, g, :], b[:, 0:T], sc, GH[:, g, :].bitcast(F32), ALU.mult, ALU.subtract, h)
                idle[i] = [l]
                pool_in[g] = [h, l]
                yield

        POOLT = (SM[:, 1612:1868], TMP[:, 2, :])
        INVT = TMP[:, 1, :] if False else RS[:, :]
        baw_free = t
        sides.append(pool_side())
        for c in range(8):
            proj_unit(ev_act(GA[:, c, :], f"ga{c}", AF.Tanh, scale=0.5), X)
        for c in range(8):
            proj_unit(ev_act(GB[:, c, :], f"gb{c}", AF.Tanh, scale=0.5), X)
        x_free = st.done[st.v]
        while 3 not in pool_in:
            tick()
        for i in range(4):
            bi = main_bank()
            b, free = take_bank(bi)

            def mm(b=b, free=free):
                return fm_unit([b[:, 0:T], b[:, T:2 * T]], free, lambda k: GH[:, k, :], lambda k: GL[:, k, :],
                               pool_in, nk=4, groups=2)

            def ev(t, i=i, b=b, bi=bi):
                g = GA[:, 2 * i:2 * i + 2, :].rearrange("p a b -> p (a b)")
                a = dve.stt(g, g, 1.0, b[:, :], ALU.add, ALU.mult, t, [tok[f"ga{c}"] for c in range(8)])
                idle[bi] = [a]
                tok[f"ya{i}"] = a
                if i == 3:
                    tok["pooled"] = t
            unit(mm, ev)
        flush()
        while len(dn_ok) < 8:
            tick()
        sides.remove(clock)
        y_ok = {}
        for c in range(8):
            def f(ps, t, c=c):
                g = GB[:, c, :]
                a = dve.stt(g, g, 1.0, ps, ALU.add, ALU.mult, t, tok[f"gb{c}"])
                s = dve.tt(g, g, GA[:, c, :], ALU.add, a, tok[f"ya{c // 2}"])
                h = act.act(XH[:, c, :], g, AF.Copy, s, x_free, scale=0.5)
                l = dve.stt(XL[:, c, :], g, 0.5, XH[:, c, :].bitcast(F32), ALU.mult, ALU.subtract, h, x_free)
                y_ok[c] = [h, l]
                return a
            proj_unit(f, dn_ok, lambda k: GH[:, k, :], lambda k: GL[:, k, :])
        flush()
        h_ok = []
        squares = []
        for c in range(8):
            def f(ps, t, c=c):
                a = dve.tt(H[:, c, :], H[:, c, :], ps, ALU.add, t)
                h_ok.append(a)
                return a
            proj_unit(f, y_ok)
        flush()
        tok.clear()
        ACTS = big[:, :].rearrange("p (e t) -> p e t", t=T)
        A = Arena(16384, 32768)
        QP = A.take(4096, T)
        SC = A.take(4096, 128)
        KEYS = A.take(2048, 128)
        XT = [A.take(128) for _ in range(4)]
        CA = [[A.take(256) for _ in range(2)] for _ in range(2)]
        SMALL = A.take(12 * 256)
        V1, V2, TS, F1, F2, FP, FJ = (SMALL[:, 256 * i:256 * i + 256].rearrange("p (t h k) -> p t h k", t=2, k=16)
                                      for i in range(7))
        U1, U2_, UPOS, UJ = (SMALL[:, 256 * (7 + i):256 * (8 + i)].bitcast(U32).rearrange("p (t h k) -> p t h k", t=2, k=16)
                           for i in range(4))
        S8 = SMALL[:, 2816:2832].rearrange("p (t h) -> p t h", t=2)
        R8 = SMALL[:, 2832:2848].rearrange("p (t h) -> p t h", t=2)
        I16 = SMALL[:, 2848:2864]
        HS = QP.rearrange("p a b -> p (a b)")[:, 0:2048].rearrange("p (t d) -> p t d", t=2)
        s_l3 = sem("l3")
        mixed = [y for v in y_ok.values() for y in v] + h_ok
        pool.dma(KEYS, I["keys"], s_l3, mixed)
        l3_ok = pool.dma(I16, I["iota16"], s_l3)

        X = norm_split(COL["ffn"], h_ok, 7, free=[st.done[st.v]])
        hscr = nc.dram_tensor("residual", [256, 1024], F32).ap()
        s_h = sem("hscr")
        s_h2 = sem("hscr2")
        HSX = A.take(512)

        def residual_side():
            last = []
            for tile in range(2):
                for half in range(2):
                    i = 3 + (2 * tile + half) % 2
                    b, free = take_bank(i)
                    for c in range(4):
                        t = pe.tr(b[:, 128 * c:128 * c + 128], H[:, 4 * half + c, 128 * tile:128 * tile + 128],
                                  ident[:, :], free, h_ok, signal=c == 3)
                    t = act.act(HSX, b[:, :], AF.Copy, t, mixed, last)
                    idle[i] = [t]
                    last = [pool.dma(hscr[128 * tile:128 * tile + 128, 512 * half:512 * half + 512], HSX, s_h, t)]
                    tok["h_saved"] = t
                    yield
                    yield
            tok["h_scr"] = last[0]

        sides.append(residual_side())
        tmp_at = [0]

        def scores(h):
            i = 3 + h % 2
            b, free = take_bank(i)
            for tile in range(2):
                for half in range(2):
                    t = pe.mm(b[:, 256 * tile + 128 * half:256 * tile + 128 * half + 128],
                              QP[:, 2 * h + half, 128 * tile:128 * tile + 128], KEYS[:, 2 * h + half, :], True, True,
                              free, tok[f"q{2 * h + half}"], l3_ok, signal=tile == 1 and half == 1)
            t = act.act(SC[:, 4 * h:4 * h + 4, :].rearrange("p a b -> p (a b)"), b[:, :], AF.Copy, t, mixed)
            idle[i] = [t]
            tok[f"s{h}"] = t

        def top16(src, spare, vals, idx, *after):
            a = dve.do(lambda e: e.max(vals[:, 0:8], src), after)
            b = dve.do(lambda e: e.match_replace(spare, vals[:, 0:8], src, -3.0e38), [a])
            c = dve.do(lambda e: e.max(vals[:, 8:16], spare), [b])
            d = dve.do(lambda e: e.max_index(idx[:, 0:8], vals[:, 0:8], src), [a])
            e_ = dve.do(lambda e: e.max_index(idx[:, 8:16], vals[:, 8:16], spare), [c])
            return [c, d, e_]

        def topk_side():
            for h in range(8):
                while f"s{h}" not in tok:
                    yield
                for tile in range(2):
                    r = []
                    for half, v, u in ((0, V1, U1), (1, V2, U2_)):
                        r += top16(SC[:, 4 * h + 2 * tile + half, :], XT[2 * tile + half], v[:, tile, h, :],
                                   u[:, tile, h, :], tok[f"s{h}"], mixed)
                    yield
                    ca, cb = CA[tile]
                    t = dve.tt(ca.rearrange("p (a b) -> p a b", b=16), V1[:, tile, h, :, None].broadcast_to([128, 16, 16]),
                               V2[:, tile, h, None, :].broadcast_to([128, 16, 16]), ALU.add, r)
                    tok[f"t{h}{tile}"] = top16(ca, cb, TS[:, tile, h, :], UPOS[:, tile, h, :], t)
                    yield
            done = [tok[f"t{h}{tile}"] for h in range(8) for tile in range(2)]
            W = SC.rearrange("p a b -> p (a b)")
            EQS = [W[:, 2048 * i:2048 * i + 2048] for i in range(2)]
            b = dve.do(lambda e: e.tensor_single_scalar(UJ, UPOS, 15, ALU.bitwise_and), [done])
            a = dve.do(lambda e: e.tensor_single_scalar(UPOS, UPOS, 4, ALU.logical_shift_right), [b])
            f = [dve.copy(FP, UPOS, a), dve.copy(FJ, UJ, b), dve.copy(F1, U1), dve.copy(F2, U2_)]
            yield
            g = dve.copy(R8, TS[:, :, :, 0], done)
            g = dve.tt(TS, TS, R8[:, :, :, None].broadcast_to([128, 2, 8, 16]), ALU.subtract, g)
            g = act.act(TS, TS, AF.Exp, g)
            s = dve.reduce(S8, TS, ALU.add, g)
            s = dve.recip(R8, S8, s)
            g = dve.tt(TS, TS, R8[:, :, :, None].broadcast_to([128, 2, 8, 16]), ALU.mult, s)
            yield
            picked = []
            k = 0
            for tile in range(2):
                for pos, idx in ((FP, F1), (FJ, F2)):
                    e = EQS[k % 2]
                    free = picked[-2:] if k >= 2 else None
                    m = dve.tt(e.rearrange("p (a b) -> p a b", b=16),
                               pos[:, tile, :, :].rearrange("p h k -> p (h k)")[:, :, None].broadcast_to([128, 128, 16]),
                               I16[:, None, :].broadcast_to([128, 128, 16]), ALU.is_equal, f, l3_ok, free)
                    e4 = e.rearrange("p (h k i) -> p h k i", k=16, i=16)
                    m = pool.tt(e4, e4, idx[:, tile, :, None, :].broadcast_to([128, 8, 16, 16]), ALU.mult, m)
                    picked.append(dve.reduce(pos[:, tile, :, :].rearrange("p h k -> p (h k)"),
                                             e.rearrange("p (a b) -> p a b", b=16), ALU.add, m))
                    k += 1
                    yield
            i, b, free = 3, *take_bank(3)
            for tile in range(2):
                for n, src in enumerate((FP, FJ)):
                    t = pe.tr(b[:, 256 * n + 128 * tile:256 * n + 128 * tile + 128],
                              src[:, tile, :, :].rearrange("p h k -> p (h k)"), ident[:, :], free, picked,
                              signal=n == 1 and tile == 1)
            a = act.act(ET.rearrange("p n t -> p n t"), b[:, :].rearrange("p (n t) -> p n t", n=2), AF.Copy, t)
            idle[3] = [a]
            b, free = take_bank(4)
            for tile in range(2):
                t = pe.tr(b[:, 128 * tile:128 * tile + 128], TS[:, tile, :, :].rearrange("p h k -> p (h k)"),
                          ident[:, :], free, g, signal=tile == 1)
            g = act.act(GATE, b[:, 0:256], AF.Copy, t)
            idle[4] = [g]
            tok["chosen"] = [a, g]

        sides.append(topk_side())
        tok["xs"] = None
        for u in range(16):
            def f(ps, t, u=u):
                tok[f"q{u}"] = act.act(QP[:, u, :], ps, AF.Copy, t, mixed)
                if u % 2:
                    later(1, lambda: scores(u // 2))
                return tok[f"q{u}"]
            if u == 0:
                sides.insert(0, clock)
            proj_unit(f, X)

        IOTA = ones
        iota_ok = [None]
        progress = [0]
        built = [0]
        last = {"act": None, "dve": None}
        onehot = GH[:, :, :].rearrange("p a b -> p (a b)").rearrange("p (r t n i) -> p r t n i", r=2, n=2, i=128)
        oh_free = [[], []]
        vg_free = [None] * 4
        stats_read = tok.get("stats")

        def build_side():
            while "chosen" not in tok:
                yield
            iota = pool.dma(IOTA[:, :], I["iota"], s_l3, X, st.done[st.v - 1])
            for g in range(T // 4):
                t0 = 4 * g
                r = g % 2
                oh = onehot[:, r]
                m = dve.tt(oh, IOTA[:, None, None, :].broadcast_to([128, 4, 2, 128]),
                           ET[:, :, t0:t0 + 4].rearrange("p n t -> p t n")[:, :, :, None].broadcast_to([128, 4, 2, 128]),
                           ALU.is_equal, iota, tok["chosen"], oh_free[r])
                i = 3 + g % 2
                b, free = take_bank(i)
                yield
                for j in range(4):
                    v = act.act(VG[:, j, :], oh[:, j, 1, :].bitcast(F32), AF.Copy, m, vg_free[j],
                                scale=GATE[:, t0 + j:t0 + j + 1])
                    vg_free[j] = pe.mm(b[:, 128 * j:128 * j + 128], oh[:, j, 0, :].bitcast(F32), VG[:, j, :],
                                       True, True, free, v, signal=True)
                oh_free[r] = vg_free[3]
                n = progress[0]
                g4 = b[:, :].rearrange("p (t e) -> p e t", e=128)
                x = ACTS[:, 0:n, t0:t0 + 4]
                a = dve.tt(x, x, g4[:, 0:n, :], ALU.mult, vg_free[3], last["act"], last["dve"])
                c = a
                if n < 128:
                    c = act.act(ACTS[:, n:128, t0:t0 + 4], g4[:, n:128, :], AF.Copy, a)
                    last["act"] = c
                last["dve"] = a
                idle[i] = [c]
                built[0] = t0 + 4
                if g % 3 != 2:
                    yield
            tok["built"] = True

        sides.append(build_side())

        def ev_down(n):
            def f(ps, t):
                while built[0] == 0 and n == 63:
                    tick()
                m = built[0]
                r = t
                done = []
                if m < T:
                    r = act.act(ACTS[:, n, m:T], ps[:, m:T], AF.Gelu, t, mixed if n < 21 else None,
                                tok["h_saved"], tok["temps"] if n >= 64 else None)
                    last["act"] = r
                if m > 0:
                    r = act.act(TG, ps[:, 0:m], AF.Gelu, t, tok.get("tg")) if m == T else \
                        act.act(TG[:, 0:m], ps[:, 0:m], AF.Gelu, t, tok.get("tg"))
                    x = ACTS[:, n, 0:m]
                    tok["tg"] = last["dve"] = dve.tt(x, x, TG[:, 0:m], ALU.mult, r, last["act"], last["dve"])
                progress[0] = n + 1
                return r
            return f

        tok["temps"] = None
        tok["h_saved"] = None
        for n in range(DOWN):
            proj_unit(ev_down(n), X)
        flush()
        while "built" not in tok:
            tick()
        sides.remove(clock)

        ready = list(last.values())
        W_AHEAD = 3
        parts = {}
        used = {}
        x_done = st.done[st.v]

        def cut(n):
            if n < UP:
                h, l = GH[:, n % 8, :], GL[:, n % 8, :]
                parts[n] = split_into(h, l, ACTS[:, n, :], ready, used.get(n - 8), oh_free[0], oh_free[1])

        accs = [take_bank(3 + i) for i in range(4)]
        for n in range(W_AHEAD):
            cut(n)
        for n in range(UP):
            def mm(n=n):
                wh, wl, h_ok, l_ok = st.take()
                for tile in range(2):
                    a = GH[:, n % 8, 128 * tile:128 * tile + 128]
                    b = GL[:, n % 8, 128 * tile:128 * tile + 128]
                    for half in range(2):
                        o, free = accs[2 * tile + half]
                        w = slice(512 * half, 512 * half + 512)
                        pe.mm(o[:, :], a, wh[:, w], n == 0, False, free if n == 0 else None, h_ok, parts[n])
                        pe.mm(o[:, :], a, wl[:, w], False, False, l_ok)
                    for half in range(2):
                        o, free = accs[2 * tile + half]
                        w = slice(512 * half, 512 * half + 512)
                        t = pe.mm(o[:, :], b, wh[:, w], False, n == UP - 1, signal=half == 1)
                    if n == UP - 1:
                        out_ok.append(t)
                st.release(t)
                used[n] = t
                return t

            out_ok = []
            unit(mm, lambda t: None)
            cut(n + W_AHEAD)
        flush()

        R = big[:, 0:2048].rearrange("p (t d) -> p t d", t=2)
        FW = big[:, 2048:3072]
        O = big[:, 3072:5120].rearrange("p (t d) -> p t d", t=2)
        JUNK = big[:, 5120:6144]
        FS = big[:, 6144:6152]
        s_fin, s_out = sem("fin"), sem("out")
        w = parts[63]
        for tile in range(2):
            pool.dma(R[:, tile, :], hscr[128 * tile:128 * tile + 128, :], s_fin, w, tok["h_scr"])
        fin_ok = pool.dma(FW, I["fnw"], s_fin)
        for tile in range(2):
            r = []
            for half in range(2):
                w = slice(512 * half, 512 * half + 512)
                o, _ = accs[2 * tile + half]
                a = dve.tt(O[:, tile, w], R[:, tile, w], o[:, :], ALU.add, out_ok[tile], fin_ok, parts[63])
                r.append(act.act(JUNK[:, w], O[:, tile, w], AF.Square, a, parts[63],
                                 accum_out=FS[:, 2 * tile + half:2 * tile + half + 1]))
            s = dve.tt(FS[:, 4 + tile:5 + tile], FS[:, 2 * tile:2 * tile + 1], FS[:, 2 * tile + 1:2 * tile + 2],
                       ALU.add, r)
            s = act.act(FS[:, 6 + tile:7 + tile], FS[:, 4 + tile:5 + tile], AF.Sqrt, s, scale=1.0 / D, bias=EPS)
            s = dve.recip(FS[:, 6 + tile:7 + tile], FS[:, 6 + tile:7 + tile], s)
            for half in range(2):
                w = slice(512 * half, 512 * half + 512)
                a = dve.stt(O[:, tile, w], O[:, tile, w], FS[:, 6 + tile:7 + tile], FW[:, w], ALU.mult, ALU.mult, s)
                end = sp.dma(out[0, 128 * tile:128 * tile + 128, w], O[:, tile, w], s_out, a)
        sp.wait(end)

        with nc.Block() as block:
            @block.sync
            def _(e):
                sp.emit(e)

            @block.gpsimd
            def _(e):
                pool.emit(e)

            @block.tensor
            def _(e):
                pe.emit(e)

            @block.scalar
            def _(e):
                act.emit(e)

            @block.vector
            def _(e):
                dve.emit(e)


def prepare(inputs):
    import numpy as np
    f = np.float32
    x = {k: np.asarray(v) for k, v in inputs.items()}
    tiles = []

    def feature_tiles(w):
        n = w.shape[1] // 128
        tiles.append(w.reshape(8, 128, n, 128).transpose(2, 1, 0, 3).reshape(n, 128, 1024))

    def half_tiles(w):
        return w.reshape(4, 128, 4, 2, 128).transpose(2, 1, 0, 3, 4).reshape(4, 128, 1024)

    w = x["w_in"][0]
    o = np.cumsum([0, 512, 128, 128, 128, 128, 128, 128, 24, 512, 128, 128, 1024, 1024])
    part = [w[:, o[i]:o[i + 1]] for i in range(13)]
    qn, kc, vc, ks, vs, kw, vw, gn, qs, kk, vv, ga, gb = part

    def pairs(q):
        return q.reshape(1024, 2, 4, 64).transpose(0, 2, 1, 3).reshape(1024, 512)

    gates = gn.reshape(1024, 2, 4, 3).transpose(0, 3, 2, 1).reshape(1024, 24)
    feature_tiles(np.concatenate([kc, vc, ks, kw, pairs(qn), kk, pairs(qs)], 1))
    tm = np.concatenate([vs, vw, vv, gates, np.zeros((1024, 104), f)], 1)
    tiles.append(tm.reshape(4, 2, 128, 512).transpose(0, 2, 1, 3).reshape(4, 128, 1024))
    feature_tiles(np.concatenate([ga, gb], 1))
    ups = []
    for k in ("w_up_nsa", "w_up_swa"):
        ups.append(half_tiles(x[k][0].reshape(2, 4, 64, 1024).transpose(1, 0, 2, 3).reshape(512, 1024)))
    tiles.append(np.stack(ups, 1).reshape(8, 128, 1024))
    feature_tiles(x["w_out"][0])
    w1, w2 = x["w_mlp_in"][0], x["w_mlp_out"][0]
    for q in range(9):
        if q < 8:
            feature_tiles(w1[:, 512 * q:512 * q + 512])
        if q > 0:
            tiles.append(half_tiles(w2[512 * q - 512:512 * q]))
    w = x["w_in_2"][0]
    xa, qkv, z, ba, ga, gb = np.split(w, [512, 3584, 4608, 4624, 5648], axis=1)
    feature_tiles(qkv.reshape(1024, 3, 8, 128).transpose(0, 2, 1, 3).reshape(1024, 3072))
    feature_tiles(np.concatenate([z, xa, ga, gb], 1))
    tiles.append(half_tiles(x["w_pool_up_2"][0]))
    feature_tiles(x["w_dn_up_2"][0])
    feature_tiles(x["w_mix_out_2"][0])
    feature_tiles(x["peer_w_query_2"][0])
    tiles.append(x["peer_down_2"][0].reshape(128, 128, 8, 128).transpose(1, 3, 2, 0).reshape(128, 128, 1024))
    tiles.append(x["peer_up_2"][0].reshape(128, 128, 1024).transpose(1, 0, 2))
    wst = np.concatenate(tiles, 0)

    cols = [x[k].reshape(-1, 128).T for k in ("norm_mix_pre", "norm_mix_post", "norm_mlp_pre", "norm_mlp_post",
                                              "mix_norm_w_2", "ffn_norm_w_2", "pool_scale_2")]
    cols.append(x["conv_w_2"][0].reshape(4, 24, 128).transpose(2, 1, 0).reshape(128, 96))
    cols.append(x["dn_norm_w_2"].reshape(128, 1))
    cols.append(np.full((128, 1), 1e-6, f))

    dist = 255 - np.arange(384)
    start = np.array([*range(17), 21, 27, 35, 46, 59, 77, 99, 128, 166, 216])
    bucket = np.searchsorted(start, dist, side="right") - 1
    oneh = np.zeros((32, 384), f)
    oneh[bucket[dist >= 0], np.arange(384)[dist >= 0]] = 8.0
    bmask = np.zeros((16, 384), f)
    bmask[:, dist < 0] = -1e30
    bmask[8:, dist >= 128] = -1e30
    relb = x["rel_bias"].reshape(32, 2, 2, 4).transpose(0, 1, 3, 2).reshape(32, 16)
    t = np.arange(256).reshape(2, 128).T
    end = np.arange(15) * 16 + 31
    ok = (end <= t[:, :, None])
    cmask = np.concatenate([np.where(ok, 0, -1e30), ok], 2).astype(f)
    rows = np.arange(128)
    bdmask = (rows[:, None] // 16 == np.arange(8)).astype(f)
    sel = np.zeros((30, 128), f)
    for r in range(128):
        if r % 16 < 15:
            sel[(r // 16 % 2) * 15 + r % 16, r] = 1
    i = np.arange(128)
    tri = (i[:, None] <= i).astype(f)
    lmask = np.stack([(i[:, None] // (2 * n) == i // (2 * n)) & (i // n % 2 == 1) & (i[:, None] // n % 2 == 0)
                      for n in (16, 32, 64)], 1).astype(f)
    inv = 1.0 / np.minimum(np.arange(1, 257), np.array([[2], [4], [8], [16]]))
    keys = np.stack([x["peer_keys_1_2"][0], x["peer_keys_2_2"][0]], 1)
    d = {
        "keys": keys.transpose(3, 0, 1, 2).reshape(128, 16, 128),
        "iota16": np.broadcast_to(np.arange(16, dtype=f), (128, 16)),
        "iota": np.broadcast_to(np.arange(128, dtype=f), (128, 128)),
        "fnw": np.broadcast_to(x["final_norm_w_2"][None], (128, 1024)),
        "tri": tri, "suf": (i[:, None] > i).astype(f), "negm": np.where(i[:, None] <= i, 0, -1e30).astype(f),
        "lmask": lmask, "baw": ba.reshape(8, 128, 16).transpose(1, 0, 2).reshape(128, 128),
        "alog": np.broadcast_to(x["a_log_2"].reshape(1, 8), (128, 8)),
        "dtb": np.broadcast_to(x["dt_bias_2"].reshape(1, 8), (128, 8)),
        "poolw": x["pool_w_2"][0].transpose(1, 0, 2),
        "inv": np.broadcast_to(inv.astype(f)[None], (128, 4, 256)),
        "wst": wst,
        "xT": x["x"][0].T.reshape(8, 128, 256).transpose(1, 0, 2),
        "cols": np.concatenate(cols, 1),
        "ident": np.eye(128, dtype=f),
        "relb": relb, "oneh": oneh, "bmask": bmask,
        "pos": np.concatenate([x[k][0].reshape(16, 128).T for k in ("cmp_pos_k", "cmp_pos_v")], 1),
        "w1k": x["cmp_w1_k"][0].reshape(16, 128, 256).transpose(1, 0, 2),
        "w1v": x["cmp_w1_v"][0].reshape(16, 128, 256).transpose(1, 0, 2),
        "w2k": np.concatenate([x["cmp_w2_k"][0]] * 2, 1).reshape(2, 128, 128).transpose(1, 0, 2),
        "w2v": x["cmp_w2_v"][0].reshape(2, 128, 64).transpose(1, 0, 2),
        "sinks": np.broadcast_to(x["attn_sinks"].reshape(2, 4).T.reshape(1, 8), (128, 8)),
        "cmask": cmask, "bdmask": bdmask, "sel": sel,
    }
    return {k: np.ascontiguousarray(v) for k, v in d.items()}


def kernel(**inputs):
    from concourse import bacc
    from concourse.bass_utils import run_bass_kernel_spmd

    arrays = prepare(inputs)
    nc = bacc.Bacc("TRN2", target_bir_lowering=False, num_devices=1)
    operands = {name: nc.dram_tensor(f"in_{name}", a.shape, mybir.dt.from_np(a.dtype), kind="ExternalInput").ap()
                for name, a in arrays.items()}
    out = nc.dram_tensor("out_0", (1, T, D), mybir.dt.float32, kind="ExternalOutput").ap()
    program(nc, operands, out)
    result = run_bass_kernel_spmd(nc, [{f"in_{name}": a for name, a in arrays.items()}], core_ids=[0])
    return result.results[0]["out_0"]
```

```python
import concourse.bass as bass
from concourse import mybir
from contextlib import ExitStack

T = 256
D = 1024
UNITS = 457


class Sem:

    def __init__(self, handle):
        self.handle = handle
        self.value = 0

    def add(self, n):
        self.value += n
        return (self, self.value)


class Lane:

    def __init__(self, sem):
        self.sem = sem
        self.queue = []
        self.passed = {}

    def wait(self, *after):
        for a in after:
            if a is None:
                continue
            if isinstance(a, list):
                self.wait(*a)
                continue
            sem, value = a
            if self.passed.get(id(sem), 0) < value:
                self.passed[id(sem)] = value
                self.queue.append(lambda e, s=sem, v=value: e.wait_ge(s.handle, v))

    def do(self, fn, after=(), signal=True):
        self.wait(*after)
        if not signal:
            self.queue.append(fn)
            return None
        self.queue.append(lambda e: fn(e).then_inc(self.sem.handle, 1))
        return self.sem.add(1)

    def dma(self, out, in_, sem, *after, **kw):
        self.wait(*after)
        self.queue.append(lambda e: e.dma_start(out, in_, **kw).then_inc(sem.handle, 16))
        return sem.add(16)

    def emit(self, engine):
        for fn in self.queue:
            fn(engine)


class Vec(Lane):
    def tt(self, out, in0, in1, op, *after):
        return self.do(lambda e: e.tensor_tensor(out, in0, in1, op), after)

    def ts(self, out, in0, s1, s2, op0, op1, *after):
        if s2 is None:
            return self.do(lambda e: e.tensor_scalar(out, in0, s1, None, op0), after)
        return self.do(lambda e: e.tensor_scalar(out, in0, s1, s2, op0, op1), after)

    def stt(self, out, in0, s, in1, op0, op1, *after):
        return self.do(lambda e: e.scalar_tensor_tensor(out, in0, s, in1, op0, op1), after)

    def copy(self, out, in_, *after):
        return self.do(lambda e: e.tensor_copy(out, in_), after)

    def recip(self, out, in_, *after):
        return self.do(lambda e: e.reciprocal(out, in_), after)

    def memset(self, out, v, *after):
        return self.do(lambda e: e.memset(out, v), after)

    def reduce(self, out, in_, op, *after):
        return self.do(lambda e: e.tensor_reduce(out, in_, mybir.AxisListType.X, op), after)


class Act(Lane):
    def act(self, out, in_, func, *after, **kw):
        return self.do(lambda e: e.activation(out, in_, func, **kw), after)


class Pe(Lane):
    def mm(self, out, lhsT, rhs, start, stop, *after, signal=False):
        return self.do(lambda e: e.matmul(out, lhsT, rhs, start=start, stop=stop, skip_group_check=True),
                       after, signal)

    def tr(self, out, in_, ident, *after, signal=False):
        return self.do(lambda e: e.transpose(out, in_, ident), after, signal)


def program(nc, I, out):
    F32 = mybir.dt.float32
    F32R = mybir.dt.float32r
    U32 = mybir.dt.uint32
    ALU = mybir.AluOpType
    AF = mybir.ActivationFunctionType

    RR, RW = 4, 3
    LS = RW - 1
    LD = LS + RR

    ctx = ExitStack()
    with ctx:
        sb = lambda name, shape, dt: ctx.enter_context(nc.sbuf_tensor(name, shape, dt))
        sem = lambda name: Sem(ctx.enter_context(nc.semaphore(name)))

        pe, act, dve, pool, sp = Pe(sem("pe")), Act(sem("act")), Vec(sem("dve")), Vec(sem("pool")), Lane(sem("sp"))
        big = sb("big", [128, 32768], F32)
        XH = sb("xh", [128, 8, T], F32R)
        XL = sb("xl", [128, 8, T], F32R)
        GH = sb("gh", [128, 8, T], F32R)
        GL = sb("gl", [128, 8, T], F32R)
        raw = sb("raw", [128, RR, 1024], F32)
        WH = sb("wh", [128, RW, 1024], F32R)
        WL = sb("wl", [128, RW, 1024], F32R)
        ident = sb("ident", [128, 128], F32)
        ones = sb("ones", [128, 128], F32)
        misc = sb("misc", [128, 1412], F32)
        ET = misc[:, 0:512].rearrange("p (n t) -> p n t", n=2)
        GATE = misc[:, 512:768]
        IOTA = misc[:, 768:896]
        RS2 = misc[:, 896:900]
        VG = [misc[:, 900:1028], misc[:, 1028:1156], ones[:, :], ident[:, :]]
        TG = misc[:, 1156:1412]
        cols = sb("cols", [128, I["cols"].shape[1]], F32)
        banks = [ctx.enter_context(nc.psum_tensor(f"bank{i}", [128, 512], F32)) for i in range(8)]
        idle = [[] for _ in range(8)]

        class Arena:
            def __init__(self, at, end):
                self.at, self.end = at, end

            def take(self, n, m=None):
                a = big[:, self.at:self.at + n]
                self.at += n
                assert self.at <= self.end, (self.at, self.end)
                return a if m is None else a.rearrange("p (a b) -> p a b", b=m)

        def take_bank(i):
            free = idle[i]
            assert free is not None, f"bank {i} is in use"
            idle[i] = None
            return banks[i], free

        def quad(x):
            return x[:, :].rearrange("p (a b) -> p a b", b=128)

        def flat(x):
            return x.rearrange("p a b -> p (a b)")

        s_const = sem("const")
        sp.dma(cols[:, :], I["cols"], s_const)
        c_ready = sp.dma(ident[:, :], I["ident"], s_const)
        ones_ready = dve.memset(ones[:, :], 1.0)
        COL = {}
        n = 0
        for name, w in (("mix_pre", 8), ("mix_post", 8), ("mlp_pre", 8), ("mlp_post", 8), ("mix2", 8), ("ffn", 8),
                        ("pool_scale", 4), ("conv", 96), ("dn", 1), ("eps", 1), ("mhalf", 1), ("bd", 8)):
            COL[name] = cols[:, n:n + w]
            n += w
        EPS = COL["eps"]
        MHALF = COL["mhalf"]
        EPS_ = 1e-6
        BD = COL["bd"]

        class Stream:

            def __init__(self):
                self.used = self.cut = self.got = 0
                self.load_sem = [sem(f"load{i}") for i in range(RR)]
                self.load, self.hi, self.lo, self.done = {}, {}, {}, {}

            def fetch(self, upto):
                while self.got < min(upto, UNITS) and (self.got < RR or self.got - RR in self.lo):
                    v = self.got
                    self.load[v] = sp.dma(raw[:, v % RR, :], I["wst"][v], self.load_sem[v % RR],
                                          self.lo.get(v - RR))
                    self.got += 1

            def split(self, upto):
                while self.cut < min(upto, UNITS) and (self.cut < RW or self.cut - RW in self.done):
                    v = self.cut
                    w_free = self.done.get(v - RW)
                    self.hi[v] = act.act(WH[:, v % RW, :], raw[:, v % RR, :], AF.Copy, self.load[v], w_free)
                    self.lo[v] = dve.tt(WL[:, v % RW, :], raw[:, v % RR, :],
                                        WH[:, v % RW, :].bitcast(F32), ALU.subtract, self.load[v], self.hi[v],
                                        w_free)
                    self.cut += 1

            def take(self):
                v = self.used
                self.used += 1
                self.fetch(v + LD + 1)
                self.split(v + LS + 1)
                self.fetch(v + LD + 1)
                assert v < self.cut
                self.v = v
                return v, WH[:, v % RW, :], WL[:, v % RW, :], self.hi[v], self.lo[v]

        st = Stream()

        sides = []
        soon = []
        pending = []
        turns = [1]
        mains = [[0, 1, 2], 0]

        def tick():
            for s in list(sides):
                if next(s, "end") == "end":
                    sides.remove(s)

        def later(n, fn):
            soon.append([n, fn])

        def flush():
            while pending:
                pending.pop(0)()

        def run_soon():
            for job in soon:
                job[0] -= 1
            while soon and soon[0][0] <= 0:
                soon.pop(0)[1]()

        def unit(parts, evac, hooks=None, at=0):
            n = 0
            if at == 0:
                run_soon()
                flush()
            for _ in parts:
                n += 1
                if hooks and n in hooks:
                    hooks[n]()
                if n == at:
                    run_soon()
                    flush()
                if n <= turns[0]:
                    tick()
            for _ in range(n, turns[0]):
                tick()
            flush()
            pending.append(evac)

        def settle(*names):
            while sides and (not names or any(x not in tok for x in names)):
                run_soon()
                tick()

        def main_bank():
            which, at = mains
            i = which[at % len(which)]
            mains[1] += 1
            return i

        def xs(k):
            return XH[:, k, :], XL[:, k, :]

        def gs(k):
            return GH[:, k, :], GL[:, k, :]

        def products(outs, free, x, ready, nk=8, k0=0, first=True, last=True, end=None):
            v, wh, wl, h_ok, l_ok = st.take()
            groups = len(outs)
            for g, o in enumerate(outs):
                for k in range(nk):
                    c = k * groups + g
                    xh, xl = x(k0 + k)
                    a = wh[:, c * 128:(c + 1) * 128]
                    b = wl[:, c * 128:(c + 1) * 128]
                    pe.mm(o, a, xh, first and k == 0 and g == 0, False, free, h_ok, ready[k0 + k])
                    pe.mm(o, a, xl, False, False)
                    t = pe.mm(o, b, xh, False, last and k == nk - 1, l_ok, signal=k == nk - 1 and g == groups - 1)
                    if c % 2:
                        if t:
                            st.done[v] = end["t"] = t
                        yield

        def two_products(oa, ob, free, x, ready, end):
            two = [(o, st.take()) for o in (oa, ob)]
            for k in range(8):
                xh, xl = x(k)
                c = slice(k * 128, k * 128 + 128)
                for o, (v, wh, wl, h_ok, l_ok) in two:
                    pe.mm(o, wh[:, c], xh, k == 0, False, free, h_ok, ready[k])
                    pe.mm(o, wh[:, c], xl, False, False)
                    t = pe.mm(o, wl[:, c], xh, False, k == 7, l_ok, signal=k == 7)
                    if t:
                        st.done[v] = t
                        end.append(t)
                if k % 2:
                    yield

        def tile(evac, x, ready, **kw):
            i = main_bank()
            b, free = take_bank(i)
            end = {}

            def ev():
                idle[i] = [evac(b[:, 0:T], end["t"])]
            unit(products([b[:, 0:T]], free, x, ready, end=end), ev, **kw)

        def tiles(evacs, x, ready, pair=True, stat=None, name=None):
            kw = {}
            if stat:
                def spread():
                    tok[name] = stat.into(RSB)
                kw = {"hooks": {1: stat.sums, 3: spread}, "at": 4}
            if pair:
                ia, ib = main_bank(), main_bank()
                (ba, fa), (bb, fb) = take_bank(ia), take_bank(ib)
                end = []

                def ev():
                    idle[ia] = [evacs[0](ba[:, 0:T], end[0])]
                    idle[ib] = [evacs[1](bb[:, 0:T], end[1])]
                unit(two_products(ba[:, 0:T], bb[:, 0:T], fa + fb, x, ready, end), ev)
            for e in evacs[2 if pair else 0:]:
                tile(e, x, ready, **kw)
                kw = {}

        def split_into(h, l, src, *after):
            a = act.act(h, src, AF.Copy, *after)
            b = dve.tt(l, src, h.bitcast(F32), ALU.subtract, a, *after)
            return [a, b]

        SQN = 3

        class Stat:

            def __init__(self, bank, n, *free, lane=None):
                self.bank, self.n, self.free, self.c = bank, n, list(free), 0
                self.lane = lane or pool
                self.read = {}

            def add(self, src, *after):
                c = self.c
                self.c += 1
                s = SQ[:, c % SQN, :]
                a = act.act(s, src, AF.Square, self.read.get(c - SQN), self.free, *after)
                if c == 0:
                    self.prev = a
                elif c == 1:
                    self.sum = self.read[0] = self.read[1] = self.lane.tt(ACC, SQ[:, 0, :], s, ALU.add, self.prev, a,
                                                                          self.free)
                elif c < self.n - 1:
                    self.sum = self.read[c] = self.lane.tt(ACC, ACC, s, ALU.add, self.sum, a)
                self.last = a
                return a

            def sums(self):
                b, free = take_bank(self.bank)
                for tile in range(2):
                    ts = slice(128 * tile, 128 * tile + 128)
                    o = b[:, tile:tile + 1]
                    pe.mm(o, ACC[:, ts], ones[:, 0:1], True, False, free, self.sum, ones_ready)
                    t = pe.mm(o, SQ[:, (self.n - 1) % SQN, ts], ones[:, 0:1], False, True, self.last, signal=True)
                self.used = t
                t = dve.ts(RS2[:, 0:2], b[:, 0:2], 1.0 / D, EPS_, ALU.mult, ALU.add, t)
                self.t = pool.tt(RS2[:, 2:4], RS2[:, 0:2], MHALF.broadcast_to([128, 2]), ALU.pow, t, c_ready)

            def spread(self):
                b = banks[self.bank]
                for tile in range(2):
                    t = pe.mm(b[:, T + 128 * tile:T + 128 * tile + 128],
                              RS2[:, 2 + tile:3 + tile].broadcast_to([128, 128]), ident[:, :], True, True, self.t,
                              c_ready, signal=True)
                return b[:, T:2 * T], t

            def into(self, dst, *after):
                rs, t = self.spread()
                a = act.act(dst, rs, AF.Copy, t, *after)
                idle[self.bank] = [a]
                return a

        tok = {}
        A = Arena(0, 32768)
        H = A.take(2048, T)
        RSA, RSB, RTMP, ACC = A.take(T), A.take(T), A.take(T), A.take(T)
        SQ4 = big[:, A.at - T:A.at + 3 * T].rearrange("p (a b) -> p a b", b=T)
        SQ = A.take(SQN * T, T)
        TMP = A.take(1024, T)
        BASE = A.at

        def unscaled(c, gain, ok, *free):
            g = gain[:, c:c + 1]
            h = act.act(XH[:, c, :], H[:, c, :], AF.Copy, ok, c_ready, *free, scale=g)
            l = dve.stt(XL[:, c, :], H[:, c, :], g, XH[:, c, :].bitcast(F32), ALU.mult, ALU.subtract, h, *free)
            return [h, l]

        def scaled_side(gain, rs_name, name, free):
            got = tok[name] = {}
            m = {}
            while rs_name not in tok:
                yield
            for c in range(9):
                if c < 8:
                    m[c] = dve.stt(TMP[:, c % 2, :], H[:, c, :], gain[:, c:c + 1], RSB, ALU.mult, ALU.mult,
                                   tok[rs_name], got.get(c - 2))
                if c:
                    got[c - 1] = split_into(GH[:, c - 1, :], GL[:, c - 1, :], TMP[:, (c - 1) % 2, :], m[c - 1], *free)
                yield
            tok[name + "_all"] = True

        s_x = [sem(f"x{i}") for i in range(4)]
        x_ok = []
        for i in range(4):
            x_ok += [sp.dma(H[:, 2 * i:2 * i + 2, :], I["xT"][:, 2 * i:2 * i + 2, :], s_x[i])] * 2
            if i % 2:
                st.fetch(i)

        QN_QS = A.take(2048, T)
        QN, QS = QN_QS[:, 0:4, :], QN_QS[:, 4:8, :]
        KS, KW, KK = A.take(T), A.take(T), A.take(T)
        V = A.take(2 * 384, 384)
        GT = A.take(48, 24)
        SA, SB = A.take(2048, T), A.take(2048, T)
        BT = A.take(4096, T)
        KC2, VC2 = A.take(2 * 258, 258), A.take(2 * 258, 258)
        CX, CV = A.take(480, 30), A.take(480, 30)
        W1K, W1V = A.take(4096, 256), A.take(4096, 256)
        MIS = A.take(1560)
        s_l1 = sem("l1")
        POS = MIS[:, 0:32]
        W2K = MIS[:, 32:288].rearrange("p (a b) -> p a b", b=128)
        W2V = MIS[:, 288:416].rearrange("p (a b) -> p a b", b=64)
        RELB = MIS[0:32, 416:432]
        ONEH = MIS[0:32, 432:816]
        BMASK = MIS[0:16, 816:1200]
        SINK = MIS[:, 1200:1208]
        CM = MIS[:, 1208:1268].rearrange("p (a b) -> p a b", b=30)
        SEL = MIS[0:30, 1268:1396]
        HID = MIS[:, 1396:1516].rearrange("p (a b) -> p a b", b=30)
        KCT = MIS[:, 1516:1546]
        for a, b in ((RELB, I["relb"]), (ONEH, I["oneh"]), (BMASK, I["bmask"]), (POS, I["pos"]), (W2K, I["w2k"]),
                     (W2V, I["w2v"]), (SINK, I["sinks"]), (CM, I["cmask"]), (SEL, I["sel"])):
            l1_ok = pool.dma(a, b, s_l1)
        s_w1k, s_w1v = sem("w1k"), sem("w1v")

        Z = W1K.rearrange("p a b -> p (a b)")
        BDV = Z[:, 0:512].rearrange("p (a b) -> p a b", b=64)
        OA = Z[:, 512:1536].rearrange("p (t a b) -> p t a b", t=2, b=64)
        OB = Z[:, 1536:2560].rearrange("p (t a b) -> p t a b", t=2, b=64)
        TMPO = Z[:, 2560:3072].rearrange("p (a b) -> p a b", b=64)
        VCS = Z[0:30, 3072:3136]
        PCT = [Z[:, 3136 + 128 * i:3264 + 128 * i] for i in range(2)]
        Z = W1V.rearrange("p a b -> p (a b)")
        NS_ = 4
        S = [Z[:, 512 * i:512 * i + 512].rearrange("p (a b) -> p a b", b=T) for i in range(NS_)]
        NP_ = 4
        PTS = [Z[:, 2048 + 512 * i:2560 + 512 * i] for i in range(NP_)]
        Z = A.take(512)
        ST = Z[:, 0:128].rearrange("p (t a b) -> p t a b", t=2, b=8)
        NM = Z[:, 128:192].rearrange("p (a b) -> p a b", b=8)
        SUM = Z[:, 192:256].rearrange("p (a b) -> p a b", b=8)
        GS = Z[:, 256:304].rearrange("p (a b) -> p a b", b=24)
        NS = Z[:, 304:312]
        W8 = Z[:, 312:328].rearrange("p (a b) -> p a b", b=8)
        Z = A.take(256)
        SC = Z.rearrange("p (t a b) -> p t a b", t=2, b=16)
        pad_ok = dve.memset(SC[:, :, :, 15:16], 0.0)

        stat = Stat(7, 8)
        X = {}
        for c in range(8):
            X[c] = unscaled(c, COL["mix_pre"], x_ok[c])
            if c == 3:
                st.fetch(3)
                st.split(2)
        for c in range(8):
            stat.add(H[:, c, :], x_ok[c])

        def bias_side():
            VB = flat(QS)[0:16, 0:384]
            b, free = take_bank(6)
            t = pe.mm(b[0:16, 0:384], RELB, ONEH, True, True, free, l1_ok, signal=True)
            t = dve.tt(VB, b[0:16, 0:384], BMASK, ALU.add, t)
            idle[6] = [t]
            s_w, s_r = sem("toep_w"), sem("toep_r")
            scr = nc.dram_tensor("toeplitz", [16, 16, 384], F32).ap()
            t = pool.dma(scr, VB[:, None, :].broadcast_to([16, 16, 384]), s_w, t)
            tok["vb"] = t
            yield
            for a in range(8):
                src = bass.AP(scr.tensor, 127 - 16 * a, [[383, 16], [6144, 16], [1, 256]])
                r = pool.dma(BT[16 * a:16 * a + 16, :, :], src, s_r, t)
            tok["bt"] = r

        def ev_kc(dst, name):
            def f(ps, t):
                a = dve.tt(dst[0:64, 0, 1:257], ps[0:64, :], RSB[0:64, :], ALU.mult, t, tok["rs1"])
                b = dve.tt(dst[64:128, 1, 0:256], ps[64:128, :], RSB[64:128, :], ALU.mult, t)
                s = sem("sw_" + name)
                sp.dma(dst[64:128, 0, 0:256], dst[0:64, 0, 1:257], s, a)
                d = sp.dma(dst[0:64, 1, 1:257], dst[64:128, 1, 0:256], s, b)
                tok[name] = [b, d]
                return b
            return f

        def ev_scale(dst, name, rs):
            def f(ps, t):
                tok[name] = dve.tt(dst, ps, RSB, ALU.mult, t, tok[rs])
                return tok[name]
            return f

        def ev_act(dst, name, func, *after, **kw):
            def f(ps, t):
                tok[name] = act.act(dst, ps, func, t, *after, **kw)
                return tok[name]
            return f

        def compress_side():
            while "vc" not in tok:
                yield
            yield
            for src, dst, col, name in ((KC2, CX, 0, "kc"), (VC2, CV, 16, "vc")):
                v = src[:, :, 1:257].rearrange("p g (n j two) -> p g j n two", j=8, two=2)
                o = dst.rearrange("p j (g n) -> p g j n", n=15)
                for half in range(2):
                    p = POS[:, col + 8 * half:col + 8 * half + 8]
                    for g in range(2):
                        ready = dve.tt(o[:, g, 8 * half:8 * half + 8, :], v[:, g, :, half:half + 15, 0],
                                       p[:, :, None].broadcast_to([128, 8, 15]), ALU.add, tok[name], l1_ok)
                tok["x" + name] = ready
            yield
            b, free = take_bank(7)
            hid = b[:, 0:128].rearrange("p (a b) -> p a b", b=32)[:, :, 0:30]
            for i, (w, x, w_ok, ok) in enumerate(((W1K, CX, w1k_ok, "xkc"), (W1K, CX, w1k_ok, "xkc"),
                                                  (W1V, CV, w1v_ok, "xvc"), (W1V, CV, w1v_ok, "xvc"))):
                for j in range(16):
                    t = pe.mm(hid[:, i, :], w[:, j, 128 * (i % 2):128 * (i % 2) + 128], x[:, j, :], j == 0, j == 15,
                              free, tok[ok], w_ok, signal=j == 15)
                    if j == 7:
                        yield
                yield
            tok["w1"] = t
            t = act.act(HID, hid, AF.Gelu_apprx_tanh, t)
            yield
            for i in range(2):
                k = pe.mm(b[:, 128:158], W2K[:, i, :], HID[:, i, :], i == 0, i == 1, t, l1_ok, signal=True)
            for i in range(2):
                v = pe.mm(b[0:30, 160:224], HID[:, 2 + i, :], W2V[:, i, :], i == 0, i == 1, signal=True)
            yield
            tok["kct"] = act.act(KCT, b[:, 128:158], AF.Copy, k, v)
            v = act.act(VCS, b[0:30, 160:224], AF.Copy, v)
            tok["ns"] = dve.ts(NS, SINK, -1.0, None, ALU.mult, None, l1_ok)
            v = pe.mm(b[:, 256:320], SEL, VCS, True, True, v, signal=True)
            yield
            t = dve.tt(BDV, b[:, None, 256:320].broadcast_to([128, 8, 64]), BD[:, :, None].broadcast_to([128, 8, 64]),
                       ALU.mult, v, tok["w1"], c_ready)
            tok["bdv"] = t
            idle[7] = [t, tok["kct"]]

        o_ok = [None, None]

        def compressed_side():
            while "bdv" not in tok or "qn3" not in tok:
                yield
            masked, t1, sc_ok = {}, {}, {}
            for tile in range(2):
                ts = slice(128 * tile, 128 * tile + 128)
                x = SC[:, tile, :, 0:15]
                m = CM[:, tile:tile + 1, :]
                for g in range(2):
                    bank, free = take_bank(6 + g)
                    r = slice(64 * g, 64 * g + 64)
                    sc = bank[:, 0:64].rearrange("p (a b) -> p a b", b=16)[:, :, 0:15]
                    for c in range(4):
                        t = pe.mm(sc[:, c, :], QN[r, c, ts], KCT[r, 15 * g:15 * g + 15], True, True, free,
                                  tok["kct"], tok[f"qn{c}"], signal=c == 3)
                    masked[g] = dve.tt(SC[:, tile, :, :].rearrange("p (c g) n -> p g c n", g=2)[:, g, :, 0:15], sc,
                                       m[:, :, 0:15].broadcast_to([128, 4, 15]), ALU.add, t)
                    idle[6 + g] = [masked[g]]
                yield
                t = dve.reduce(ST[:, tile, 0, :], x, ALU.max, list(masked.values()))
                t = dve.tt(x, x, ST[:, tile, 0, :, None].broadcast_to([128, 8, 15]), ALU.subtract, t)
                t = act.act(x, x, AF.Exp, t, scale=0.125)
                t1[tile] = dve.tt(x, x, m[:, :, 15:30].broadcast_to([128, 8, 15]), ALU.mult, t)
            while "gs" not in tok or "bdv" not in tok:
                yield
            for tile in range(2):
                s = dve.reduce(ST[:, tile, 1, :], SC[:, tile, :, 0:15], ALU.add, t1[tile])
                s = dve.ts(ST[:, tile, 1, :], ST[:, tile, 1, :], 1e-30, None, ALU.max, None, s)
                s = dve.recip(ST[:, tile, 2, :], ST[:, tile, 1, :], s)
                sc_ok[tile] = dve.tt(ST[:, tile, 3, :], ST[:, tile, 2, :], GS[:, tile, 0:8], ALU.mult, s, tok["gs"])
            yield
            done = []
            for tile in range(2):
                b, free = take_bank(6 + tile)
                t = pe.tr(b[:, 0:128], SC[:, tile, :, :].rearrange("p a b -> p (a b)"), ident[:, :], t1[tile],
                          pad_ok, c_ready, free, signal=True)
                done.append(act.act(PCT[tile], b[:, 0:128], AF.Copy, t, tok["w1"]))
            yield
            for tile in range(2):
                b = banks[6 + tile]
                t = pe.mm(b[:, :], PCT[tile], BDV.rearrange("p a b -> p (a b)"), True, True, done[tile], tok["bdv"],
                          signal=True)
                done[tile] = dve.tt(OA[:, tile, :, :], b[:, :].rearrange("p (a b) -> p a b", b=64),
                                    ST[:, tile, 3, :, None].broadcast_to([128, 8, 64]), ALU.mult, t, sc_ok[tile])
                idle[6 + tile] = [done[tile]]
            o_ok[0] = done
            tok["oc"] = True

        steps = [(tile, kind, c) for kinds in ((0, 1), (2,)) for tile in range(2) for kind in kinds for c in range(4)]
        exps, pts, pv, freed = {}, {}, {}, {}

        def geometry(s):
            tile, kind, c = steps[s]
            q, k, v0 = ((QN, KS, 0), (QN, KW, 128), (QS, KK, 256))[kind]
            g = c % 2
            heads = [c // 2 * 4 + 2 * i + g for i in range(2)]
            return tile, kind, c, g, heads, q, k, v0 + 64 * g, 128 * (tile + 1), s // 4

        def a_scores(s):
            tile, kind, c, g, heads, q, k, v, n, run = geometry(s)
            b, free = take_bank(3 + s % 2)
            r = slice(64 * g, 64 * g + 64)
            for i in range(2):
                cc = c // 2 * 2 + i
                t = pe.mm(b[:, T * i:T * i + n], q[r, cc, 128 * tile:128 * tile + 128], k[r, 0:n], True, True, free,
                          tok[("qn", "qn", "qs")[kind] + str(cc)], tok[("ks", "kw", "kk")[kind]], signal=i == 1)
            exps[s] = t

        def a_bias(s):
            tile, kind, c, g, heads, q, k, v, n, run = geometry(s)
            b = banks[3 + s % 2]
            for i, h in enumerate(heads):
                init = NS[:, h:h + 1] if kind == 2 else 3e38
                t = dve.do(lambda e, o=S[s % NS_][:, i, 0:n], i0=b[:, T * i:T * i + n],
                           i1=BT[:, (8 if kind == 2 else 0) + h, T - n:T], init=init, nm=NM[:, run, h:h + 1]:
                           e.tensor_tensor_reduce(o, i0, i1, -0.125, init, ALU.add, ALU.min, nm),
                           [exps[s], tok["bt"], freed.get(s - NS_), tok["w1"], tok["ns"]])
            idle[3 + s % 2] = [t]
            exps[s] = t

        def a_exp(s):
            tile, kind, c, g, heads, q, k, v, n, run = geometry(s)
            for i, h in enumerate(heads):
                x = S[s % NS_][:, i, 0:n]
                t = act.act(x, x, AF.Exp, exps[s], scale=-1.0, bias=NM[:, run, h:h + 1], accum_out=SUM[:, run, h:h + 1])
            exps[s] = t

        def a_transpose(s):
            tile, kind, c, g, heads, q, k, v, n, run = geometry(s)
            i = (5, 2)[s % 2]
            b, free = take_bank(i)
            for m in range(2 * (tile + 1)):
                t = pe.tr(b[:, 128 * m:128 * m + 128], S[s % NS_][:, m // (tile + 1), 128 * (m % (tile + 1)):
                                                                 128 * (m % (tile + 1)) + 128],
                          ident[:, :], free, exps[s], c_ready, signal=m == 2 * tile + 1)
            freed[s] = t
            pts[s] = t

        def a_evac(s):
            tile = steps[s][0]
            i = (5, 2)[s % 2]
            w = 256 * (tile + 1)
            t = act.act(PTS[s % NP_][:, 0:w], banks[i][:, 0:w], AF.Copy, pts[s], pv.get(s - NP_), tok["w1"])
            idle[i] = [t]
            pts[s] = t

        def a_values(s):
            tile, kind, c, g, heads, q, k, v, n, run = geometry(s)
            nb = tile + 1
            i = 6 + run % 2
            free = None
            if c == 0:
                _, free = take_bank(i)
            for m, h in enumerate(heads):
                for j in range(nb):
                    t = pe.mm(banks[i][:, 64 * h:64 * h + 64], PTS[s % NP_][:, (m * nb + j) * 128:(m * nb + j) * 128 + 128],
                              V[:, j, v:v + 64], j == 0, j == nb - 1, free, pts[s], tok["v"],
                              signal=m == 1 and j == nb - 1)
            pv[s] = t

        def a_finish(s):
            tile, kind, c, g, heads, q, k, v, n, run = geometry(s)
            if c < 3:
                return
            i = 6 + run % 2
            r = ST[:, tile, 4 + kind, :]
            if kind == 2:
                e = dve.tt(W8[:, tile, :], NM[:, run, :], NS, ALU.subtract, exps[s])
                e = act.act(W8[:, tile, :], W8[:, tile, :], AF.Exp, e)
                e = dve.tt(SUM[:, run, :], SUM[:, run, :], W8[:, tile, :], ALU.add, e)
                e = dve.recip(r, SUM[:, run, :], e)
            else:
                e = dve.recip(r, SUM[:, run, :], exps[s])
                e = dve.tt(r, r, GS[:, tile, 8 + 8 * kind:16 + 8 * kind], ALU.mult, e, tok["gs"])
            o = banks[i][:, :].rearrange("p (a b) -> p a b", b=64)
            sc = r[:, :, None].broadcast_to([128, 8, 64])
            if kind == 2:
                o_ok[1] = dve.tt(OB[:, tile, :, :], o, sc, ALU.mult, pv[s], e)
                idle[i] = [o_ok[1]]
            else:
                t = dve.tt(TMPO, o, sc, ALU.mult, pv[s], e, o_ok[0])
                idle[i] = [t]
                o_ok[0] = dve.tt(OA[:, tile, :, :], OA[:, tile, :, :], TMPO, ALU.add, t)
                if kind == 0:
                    return
            later(1, lambda: to_features((OA, OB)[kind // 2], 4 * (kind // 2), tile, o_ok[kind // 2], i))

        up_in = {}

        def to_features(src, chunk0, tile, ok, i):
            b, free = take_bank(i)
            for c in range(4):
                t = pe.tr(b[:, 128 * c:128 * c + 128], src[:, tile, 2 * c:2 * c + 2, :].rearrange("p a b -> p (a b)"),
                          ident[:, :], free, ok, signal=c == 3)
            ps = b[:, :].rearrange("p (a b) -> p a b", b=128)
            ts = slice(128 * tile, 128 * tile + 128)
            r = split_into(XH[:, chunk0:chunk0 + 4, ts], XL[:, chunk0:chunk0 + 4, ts], ps, t, tok["x_read"])
            idle[i] = list(r)
            for c in range(4):
                up_in.setdefault(chunk0 + c, []).extend(r)

        turn_list = []
        s = 0
        while s < len(steps):
            m = 2 if steps[s][0] == 0 else 1
            turn_list.append(list(range(s, s + m)))
            s += m
        stages = [a_scores, a_bias, a_exp, a_transpose, a_evac, a_values, a_finish]

        def attention_side():
            while "oc" not in tok and not ("kct" in tok and "qn3" in tok):
                yield
            n = len(turn_list)
            for turn in range(n + len(stages) - 1):
                while (turn >= 3 and "v" not in tok) or (turn >= 5 and "oc" not in tok) or (turn >= 12 and "qs3" not in tok):
                    yield
                for k in reversed(range(len(stages))):
                    if 0 <= turn - k < n:
                        for s in turn_list[turn - k]:
                            stages[k](s)
                yield
            tok["attn"] = True

        sides.append(scaled_side(COL["mix_pre"], "rs1", "xs1", []))
        w1k_ok = pool.dma(W1K, I["w1k"], s_w1k)
        sides.append(bias_side())
        tiles([ev_kc(KC2, "kc"), ev_kc(VC2, "vc"), ev_scale(KS, "ks", "rs1"), ev_scale(KW, "kw", "rs1")], xs, X,
              stat=stat, name="rs1")
        w1v_ok = pool.dma(W1V, I["w1v"], s_w1v)
        sides.append(compress_side())
        sides.append(compressed_side())
        sides.append(attention_side())
        settle("xs1_all")
        G = tok["xs1"]
        tok["x_read"] = st.done[3]
        mains[:] = [[0, 1], 1]
        for c in range(4):
            tile(ev_act(QN[:, c, :], f"qn{c}", AF.Copy), gs, G)

        i0, i1 = 2, main_bank()
        (b0, f0), (b1, f1) = take_bank(i0), take_bank(i1)
        for u in range(4):
            def parts(u=u):
                v, wh, wl, h_ok, l_ok = st.take()
                for kk in range(2):
                    k = 2 * u + kk
                    w = slice(512 * kk, 512 * kk + 512)
                    for b, f, ts in ((b0, f0, slice(0, 128)), (b1, f1, slice(128, 256))):
                        pe.mm(b[:, :], GH[:, k, ts], wh[:, w], k == 0, False, f if u == 0 else None, h_ok, G[k])
                        pe.mm(b[:, :], GL[:, k, ts], wh[:, w], False, False)
                        t = pe.mm(b[:, :], GH[:, k, ts], wl[:, w], False, k == 7, l_ok, signal=kk == 1)
                    yield
                st.done[v] = tok["tm"] = t

            def ev(u=u):
                if u < 3:
                    return
                r = []
                for tile, (b, i) in enumerate(((b0, i0), (b1, i1))):
                    r += [act.act(V[:, tile, :], b[:, 0:384], AF.Copy, tok["tm"]),
                          act.act(GT[:, tile, :], b[:, 384:408], AF.Tanh, tok["tm"], scale=0.5)]
                    idle[i] = r[-2:]
                tok["gs"] = dve.ts(GS, GT, 1.0, 0.5, ALU.add, ALU.mult, r)
                tok["v"] = r
            unit(parts(), ev)

        tile(ev_act(KK, "kk", AF.Copy), gs, G)
        for c in range(4):
            tile(ev_act(QS[:, c, :], f"qs{c}", AF.Copy, tok["vb"]), gs, G)
        for c in range(8):
            tile(ev_act(SA[:, c, :], f"ga{c}", AF.Tanh, scale=0.5), gs, G)
        for c in range(8):
            tile(ev_act(SB[:, c, :], f"gb{c}", AF.Tanh, scale=0.5), gs, G)
        flush()
        tok["g_read"] = st.done[st.v]
        settle()
        while soon:
            run_soon()
        mains[:] = [[0, 1, 2], 0]
        Y = QN_QS
        YA, YB_ = flat(TMP[:, 0:2, :]), flat(TMP[:, 2:4, :])
        y_ok = {}
        hold = {}

        def up_pair(i):
            ends = [{}, {}]
            ids = [main_bank(), main_bank()]
            bs = [take_bank(j) for j in ids]
            for n, (gate, chunk0, name) in enumerate(((SA, 0, "ga"), (SB, 4, "gb"))):
                b, free = bs[n]

                def ev(n=n, gate=gate, name=name, b=b):
                    g = flat(gate[:, 2 * i:2 * i + 2, :])
                    a = dve.stt((YA, YB_)[n], g, 1.0, b[:, :], ALU.add, ALU.mult, ends[n]["t"],
                                [tok[name + str(c)] for c in (2 * i, 2 * i + 1)], hold.get("y"))
                    idle[ids[n]] = [a]
                    if n == 0:
                        hold["a"] = a
                        return
                    s = dve.tt(YA, YA, YB_, ALU.add, a, hold["a"])

                    def parts_of_y(s=s):
                        src = YA
                        h = act.act(flat(GH[:, 2 * i:2 * i + 2, :]), src, AF.Copy, s, tok["g_read"], scale=0.5)
                        l = dve.stt(flat(GL[:, 2 * i:2 * i + 2, :]), src, 0.5,
                                    flat(GH[:, 2 * i:2 * i + 2, :]).bitcast(F32), ALU.mult, ALU.subtract, h,
                                    tok["g_read"])
                        y_ok[2 * i] = y_ok[2 * i + 1] = [h, l]
                        hold["y"] = l
                    parts_of_y()
                unit(products([b[:, 0:T], b[:, T:2 * T]], free, xs, up_in, nk=4, k0=chunk0, end=ends[n]), ev)

        for i in range(4):
            up_pair(i)
        tok["x_read"] = st.done[st.v]
        flush()
        stat = Stat(7, 8)

        def ev_y(c):
            def f(ps, t):
                a = act.act(Y[:, c, :], ps, AF.Copy, t)
                stat.add(Y[:, c, :], a)
                return a
            return f

        def turn(y, gain, gain_next, x_free, stats_next=True):
            nonlocal stat
            stat.sums()
            rs, t = stat.spread()
            old, stat = stat, Stat(6, 8, stat.used, lane=dve)
            m, a, got = {}, {}, {}
            for c in range(9):
                if c < 8:
                    m[c] = dve.stt(y[:, c, :], y[:, c, :], gain[:, c:c + 1], rs, ALU.mult, ALU.mult, t)
                    a[c] = pool.tt(H[:, c, :], H[:, c, :], y[:, c, :], ALU.add, m[c])
                if c:
                    got[c - 1] = unscaled(c - 1, gain_next, a[c - 1], x_free)
            idle[old.bank] = [m[7]]
            for c in range(8):
                stat.add(H[:, c, :], a[c])
            return got, list(a.values())

        tiles([ev_y(c) for c in range(8)], gs, y_ok)
        flush()
        g_free = st.done[st.v]
        X, h_ok = turn(Y, COL["mix_post"], COL["mlp_pre"], tok["x_read"])
        A = Arena(BASE, 32768)
        QKV = A.take(24 * T, T)
        Q, K, VF = QKV[:, 0:8, :], QKV[:, 8:16, :], QKV[:, 16:24, :]
        SZ = A.take(2048, T)
        GA, GB = A.take(2048, T), A.take(2048, T)
        XA = A.take(1024, T)
        KB = A.take(2048, T)
        DC = A.take(2048, 128)
        LT = A.take(2048, 128)
        TT_AT = A.at
        TT = A.take(2048, 128)
        VB = A.take(2048, 128)
        KD = A.take(1024, 128)
        CT = [A.take(T) for _ in range(3)]
        SM = Arena(A.at, 32768)
        TRI, SUF, NEGM = SM.take(128), SM.take(128), SM.take(128)
        LM = SM.take(384, 128)
        BAW, BAWH, BAWL = SM.take(128), XH[:, 7, 0:128], XL[:, 7, 0:128]
        PW = SM.take(512, 128)
        JUNK = SM.take(128)
        ALOG, DTB = SM.take(8), SM.take(8)
        B2, G2, E2, U2, W2, NGC, EGC, ESF, RQ, RK, BRK, SS, BE = (SM.take(16, 8) for _ in range(13))
        INV = SM.take(68, 17)
        R16 = SM.take(64).rearrange("p (g k c) -> p g k c", g=4, k=2)
        T0 = flat(KB).rearrange("p (a b) -> p a b", b=128)
        VN = flat(VF).rearrange("p (a b) -> p a b", b=128)
        BAT = CT[2][0:16, :]
        s_l2 = sem("l2")
        for a, b in ((TRI, I["tri"]), (SUF, I["suf"]), (NEGM, I["negm"]), (LM, I["lmask"]), (BAW, I["baw"]),
                     (ALOG, I["alog"]), (DTB, I["dtb"]), (PW, I["poolw"]), (INV, I["inv"])):
            l2_ok = sp.dma(a, b, s_l2, hold["y"], [t for v in y_ok.values() for t in v])

        hid_ok, hid_free = {}, {}
        HT = [TMP[:, i, :] for i in range(3)]
        ht_free = [None] * 3

        def ev_hidden(n):
            def f(ps, t):
                ht = HT[n % 3]
                e = act.act(ht, ps, AF.Relu, t, ht_free[n % 3], hold.get("y"))
                r = dve.tt(ht, ht, ht, ALU.mult, e)
                later(1, lambda: rest(n, ht, r))
                return e
            return f

        def rest(n, ht, r):
            free = [hid_free.get(n - 8), g_free]
            a = act.act(GH[:, n % 8, :], ht, AF.Copy, r, *free)
            b = dve.tt(GL[:, n % 8, :], ht, GH[:, n % 8, :].bitcast(F32), ALU.subtract, a, *free)
            ht_free[n % 3] = b
            hid_ok[n % 8] = [a, b]

        f_end = [{} for _ in range(4)]
        f_stat = []

        def evac_f(i):
            for c in range(2):
                n = 2 * i + c
                r = dve.tt(Y[:, n, :], banks[3 + i][:, T * c:T * c + T], RSA, ALU.mult, f_end[i]["t"], tok["rs2"])
                f_stat[0].add(Y[:, n, :], r)
            idle[3 + i] = [r]

        def mlp_out(q):
            for i in range(4):
                b, free = take_bank(3 + i) if q == 0 else (banks[3 + i], None)

                def ev(q=q, i=i):
                    for k in range(4):
                        hid_free[4 * q + k] = f_end[i]["t"]
                    if q == 7:
                        evac_f(i)
                unit(products([b[:, 0:T], b[:, T:2 * T]], free, gs, hid_ok, nk=4, k0=4 * (q % 2), first=q == 0,
                              last=q == 7, end=f_end[i]), ev)

        tiles([ev_hidden(n) for n in range(4)], xs, X)
        stat.sums()
        r = stat.into(RSB)
        tok["rs2"] = dve.tt(RSA, RSB, RSB, ALU.mult, r)
        for q in range(1, 8):
            tiles([ev_hidden(4 * q + i) for i in range(4)], xs, X, pair=False)
            if q == 7:
                x_free = st.done[st.v]
            mlp_out(q - 1)
        flush()
        run_soon()
        f_stat.append(Stat(7, 8, stat.used))
        stat = f_stat[0]
        mlp_out(7)
        g_free = st.done[st.v]
        flush()
        X, h_ok = turn(Y, COL["mlp_post"], COL["mix2"], x_free)
        g_read2 = g_free
        side_at = [0]

        def side_bank():
            n = 3 + side_at[0] % 4
            side_at[0] += 1
            b, free = take_bank(n)
            return n, b, free

        def quads(lhs, rhs, *after, tr=False):
            n, b, free = side_bank()
            for j in range(4):
                if tr:
                    t = pe.tr(quad(b)[:, j, :], lhs(j), ident[:, :], free, *after, signal=j == 3)
                else:
                    t = pe.mm(quad(b)[:, j, :], lhs(j), rhs(j), True, True, free, *after, signal=j == 3)
            return n, b, t

        def ev_xa(c):
            def f(ps, t):
                tok[f"xa{c}"] = dve.tt(XA[:, c, :], ps, RSB, ALU.mult, t, tok["rs3"])
                return tok[f"xa{c}"]
            return f

        turns[0] = 4
        mains[:] = [[0, 1, 2], 0]
        sides.append(scaled_side(COL["mix2"], "rs3", "xs3", [g_read2]))
        tiles([ev_xa(c) for c in range(4)], xs, X, stat=stat, name="rs3")
        xa_read = st.done[st.v]
        baw = split_into(BAWH, BAWL, BAW, l2_ok, xa_read)
        settle("xs3_all")
        G = tok["xs3"]
        b7, f7 = take_bank(7)

        def beta_parts():
            for k in range(8):
                w = slice(16 * k, 16 * k + 16)
                pe.mm(b7[0:16, 0:T], BAWH[:, w], GH[:, k, :], k == 0, False, f7, G[k], baw)
                pe.mm(b7[0:16, 0:T], BAWH[:, w], GL[:, k, :], False, False)
                tok["ba"] = pe.mm(b7[0:16, 0:T], BAWL[:, w], GH[:, k, :], False, k == 7, signal=k == 7)
                if k % 2:
                    yield

        def both(x):
            return x[:, None, :].broadcast_to([128, 2, 8])

        def gates_side():
            while "ba" not in tok or tok["ba"] is None:
                yield
            t = act.act(BAT, b7[0:16, 0:T], AF.Copy, tok["ba"])
            yield
            for tile in range(2):
                t = pe.tr(b7[:, T + 16 * tile:T + 16 * tile + 16], BAT[:, 128 * tile:128 * tile + 128],
                          ident[0:16, 0:16], t, signal=True)
            yield
            ba = b7[:, T:T + 32].rearrange("p (a b) -> p a b", b=16)
            e = act.act(B2, ba[:, :, 0:8], AF.Exp, t, scale=-1.0)
            c = dve.tt(G2, ba[:, :, 8:16], both(DTB), ALU.add, t, l2_ok, e)
            e = dve.ts(B2, B2, 1.0, None, ALU.add, None, e)
            tok["beta"] = dve.recip(B2, B2, e)
            a = act.act(ALOG, ALOG, AF.Exp, l2_ok)
            u = act.act(U2, G2, AF.Abs, c)
            u = act.act(E2, U2, AF.Exp, u, scale=-1.0)
            yield
            r = dve.ts(U2, E2, 2.0, None, ALU.add, None, u)
            r = dve.recip(U2, U2, r)
            z = dve.tt(E2, E2, U2, ALU.mult, r)
            r = dve.tt(U2, E2, E2, ALU.mult, z)
            w = dve.ts(W2, U2, 1.0 / 19, 1.0 / 17, ALU.mult, ALU.add, r)
            for n in (15, 13, 11, 9, 7, 5, 3, 1):
                w = dve.tt(W2, W2, U2, ALU.mult, w)
                w = dve.ts(W2, W2, 1.0 / n, None, ALU.add, None, w)
                if n % 4 == 3:
                    yield
            w = dve.tt(W2, W2, E2, ALU.mult, w)
            w = dve.ts(W2, W2, 2.0, None, ALU.mult, None, w)
            g = dve.stt(G2, G2, 0.0, W2, ALU.max, ALU.add, w)
            g = dve.tt(G2, G2, both(ALOG), ALU.mult, g, a)
            g = dve.ts(G2, G2, -1.0, None, ALU.mult, None, g)
            tok["g"] = g
            yield
            for tile in range(2):
                pe.mm(b7[:, 8 * tile:8 * tile + 8], TRI, G2[:, tile, :], True, True, g)
                d = pe.mm(b7[:, 16 + 8 * tile:24 + 8 * tile], SUF, G2[:, tile, :], True, True, signal=True)
            yield
            gc = b7[:, 0:16].rearrange("p (a b) -> p a b", b=8)
            sf = b7[:, 16:32].rearrange("p (a b) -> p a b", b=8)
            n = dve.ts(NGC, gc, -1.0, None, ALU.mult, None, d)
            x = act.act(EGC, gc, AF.Exp, n)
            y = act.act(ESF, sf, AF.Exp)
            tok["be"] = dve.tt(BE, B2, EGC, ALU.mult, x, tok["beta"])
            tok["gc"] = [n, x, y]
            idle[7] = [n, y]
            yield
            for i in range(4):
                d = DC[:, 4 * i:4 * i + 4, :]
                n, b, t = quads(lambda j: G2[:, j % 2, 2 * i + j // 2:2 * i + j // 2 + 1].broadcast_to([128, 128]),
                                lambda j: TRI, tok["g"])
                yield
                t = dve.tt(d, quad(b), NEGM[:, None, :].broadcast_to([128, 4, 128]), ALU.add, t)
                idle[n] = [t]
                yield
                for j in range(4):
                    h, tile = 2 * i + j // 2, j % 2
                    e = act.act(d[:, j, :], d[:, j, :], AF.Exp, t, tok["gc"], bias=NGC[:, tile, h:h + 1])
                tok[f"dc{i}"] = e
            yield

        def ev_conv(u):
            def f(ps, t):
                r = u % 3
                w = COL["conv"][:, 4 * u:4 * u + 4]
                c = CT[seq[u] % 3]
                t = act.act(c, ps, AF.Copy, t, tok.get(f"ct{seq[u] % 3}"), scale=w[:, 3:4])
                for j, n in ((2, 1), (1, 2), (0, 3)):
                    t = dve.stt(c[:, n:T], ps[:, 0:T - n], w[:, j:j + 1], c[:, n:T], ALU.mult, ALU.add, t)
                later(1, lambda: conv_silu(u, c, t))
                return t
            return f

        sums_read = [None] * 4

        def conv_silu(u, c, t):
            a = act.act(QKV[:, u, :], c, AF.Silu, t)
            tok[f"ct{seq[u] % 3}"] = tok[f"c{u}"] = a
            if u < 16:
                i = u // 8 * 2 + u % 2
                tok[f"s{u}"] = act.act(SQ4[:, i, :], QKV[:, u, :], AF.Square, a, tok["rs3"], sums_read[u % 8 // 2 - 1])

        order = []
        for h in range(8):
            order += [h, 8 + h, 16 + h]
        seq = {u: n for n, u in enumerate(order)}

        agenda = {}

        def at(n, fn):
            agenda.setdefault(n, []).append(fn)

        def delta_side():
            for n in range(max(agenda) + 1):
                for fn in agenda.get(n, ()):
                    fn()
                yield
            tok["delta"] = True

        def step(n, mm, evac, lag=1):
            got = {}

            def first():
                got["x"] = mm()

            def second():
                k, b, t = got["x"]
                idle[k] = evac(b, t)
            at(n, first)
            at(n + lag, second)

        hd = lambda i, j: (2 * i + j // 2, j % 2)
        half = lambda tile: slice(128 * tile, 128 * tile + 128)

        def group_sums(i):
            n, b, free = side_bank()
            for k in range(4):
                for tile in range(2):
                    u = (8 if k > 1 else 0) + 2 * i + k % 2
                    t = pe.mm(b[:, 4 * tile + k:4 * tile + k + 1], SQ4[:, k, half(tile)], ones[:, 0:1], True, True,
                              free, tok[f"s{u}"], signal=tile == 1)
            sums_read[i] = t
            return n, b, t

        def group_norms(i, b, t):
            s = R16[:, i, 0, :]
            a = dve.ts(s, b[:, 0:8], EPS_, None, ALU.add, None, t)
            r = R16[:, i, 1, :]
            p = pool.tt(r, s, MHALF.broadcast_to([128, 8]), ALU.pow, a, c_ready)
            r = r.rearrange("p (t k h) -> p t k h", t=2, k=2)
            hs = slice(2 * i, 2 * i + 2)
            tok[f"rq{i}"] = dve.ts(RQ[:, :, hs], r[:, :, 0, :], 128 ** -0.5, None, ALU.mult, None, p)
            k = dve.copy(RK[:, :, hs], r[:, :, 1, :], p)
            tok[f"brk{i}"] = dve.tt(BRK[:, :, hs], B2[:, :, hs], RK[:, :, hs], ALU.mult, k, tok["beta"])
            e = dve.tt(ESF[:, :, hs], ESF[:, :, hs], RK[:, :, hs], ALU.mult, k, tok["gc"])
            tok[f"bek{i}"] = dve.tt(BE[:, :, hs], BE[:, :, hs], RK[:, :, hs], ALU.mult, k, tok["be"])
            tok[f"esf{i}"] = e
            rk = RK[:, :, hs].rearrange("p t h -> p h t")[:, :, :, None].broadcast_to([128, 2, 2, 128])
            d = DC[:, 4 * i:4 * i + 4, :].rearrange("p (h t) e -> p h t e", t=2)
            tok[f"dk{i}"] = pool.tt(d, d, rk, ALU.mult, tok[f"dc{i}"], k)
            return [a]

        def kb_mm(i):
            return quads(lambda j: BRK[:, j % 2, 2 * i + j // 2:2 * i + j // 2 + 1].broadcast_to([128, 128]),
                         lambda j: ident[:, :], tok[f"brk{i}"])

        def kb_evac(i, b, t):
            k = slice(2 * i, 2 * i + 2)
            tok[f"kb{i}"] = dve.tt(KB[:, k, :], K[:, k, :], b[:, :].rearrange("p (a b) -> p a b", b=T), ALU.mult, t,
                                   [tok[f"c{8 + h}"] for h in (2 * i, 2 * i + 1)])
            return [tok[f"kb{i}"]]

        def kk_mm(i):
            return quads(lambda j: K[:, 2 * i + j // 2, half(j % 2)], lambda j: KB[:, 2 * i + j // 2, half(j % 2)],
                         tok[f"kb{i}"])

        def kk_evac(i, b, t):
            tok[f"lt{i}"] = dve.tt(LT[:, 4 * i:4 * i + 4, :], quad(b), DC[:, 4 * i:4 * i + 4, :], ALU.mult, t,
                                   tok[f"dk{i}"])
            return [tok[f"lt{i}"]]

        def kq_mm(i):
            return quads(lambda j: K[:, 2 * i + j // 2, half(j % 2)], lambda j: Q[:, 2 * i + j // 2, half(j % 2)],
                         [tok[f"c{h}"] for h in (2 * i, 2 * i + 1)])

        def kq_evac(i, b, t):
            d = DC[:, 4 * i:4 * i + 4, :]
            tok[f"kq{i}"] = t
            tok[f"at{i}"] = dve.tt(d, quad(b), d, ALU.mult, t, tok[f"lt{i}"])
            return [tok[f"at{i}"]]

        def v_mm(i):
            n, b, t = quads(lambda j: VF[:, 2 * i + j // 2, half(j % 2)], None,
                            [tok[f"c{16 + h}"] for h in (2 * i, 2 * i + 1)], tr=True)
            tok[f"vr{i}"] = t
            return n, b, t

        def v_evac(i, b, t):
            beta = B2[:, :, 2 * i:2 * i + 2].rearrange("p t h -> p h t")[:, :, :, None].broadcast_to([128, 2, 2, 128])
            tok[f"vb{i}"] = dve.tt(VB[:, 4 * i:4 * i + 4, :].rearrange("p (h t) e -> p h t e", t=2),
                                   quad(b).rearrange("p (h t) e -> p h t e", t=2), beta, ALU.mult, t, tok["beta"])
            return [tok[f"vb{i}"]]

        def kd_mm(i):
            n, b, t = quads(lambda j: K[:, 4 * i + j, 0:128], None, tr=True)
            tok[f"kr{i}"] = t
            return n, b, t

        def kd_evac(i, b, t):
            tok[f"kd{i}"] = dve.tt(KD[:, 4 * i:4 * i + 4, :], quad(b),
                                   ESF[:, 0, 4 * i:4 * i + 4, None].broadcast_to([128, 4, 128]), ALU.mult, t,
                                   tok[f"esf{2 * i}"], tok[f"esf{2 * i + 1}"])
            return [tok[f"kd{i}"]]

        for i in range(4):
            n = 24 * i + 29
            step(n, lambda i=i: group_sums(i), lambda b, t, i=i: group_norms(i, b, t), lag=2)
            step(n + 4, lambda i=i: kb_mm(i), lambda b, t, i=i: kb_evac(i, b, t))
            step(n + 7, lambda i=i: kk_mm(i), lambda b, t, i=i: kk_evac(i, b, t))
            step(n + 9, lambda i=i: v_mm(i), lambda b, t, i=i: v_evac(i, b, t))
            step(n + 11, lambda i=i: kq_mm(i), lambda b, t, i=i: kq_evac(i, b, t))
            if i % 2:
                step(n + 13, lambda i=i // 2: kd_mm(i), lambda b, t, i=i // 2: kd_evac(i, b, t))
        n += 9

        s_d1, s_d2, s_d3, s_d4, s_d5 = (sem(f"diag{i}") for i in range(5))
        scr1 = nc.dram_tensor("diag_in", [16, 8, 16, 16], F32).ap()
        scr2 = nc.dram_tensor("diag_out", [2, 16, 8, 16, 16], F32).ap()
        BL = CT[0].rearrange("p (a b) -> p a b", b=16)
        BI = CT[1].rearrange("p (a b) -> p a b", b=16)
        C2 = [TMP[:, i, :].rearrange("p (a b) -> p a b", b=16) for i in range(2)]

        def diag_out():
            lt_ok = [tok[f"lt{i}"] for i in range(4)]
            ct_free = [tok[f"ct{i}"] for i in range(3)]
            for i in range(8):
                p = slice(16 * i, 16 * i + 16)
                t = sp.dma(scr1[:, i, :, :].rearrange("a j i -> j a i"), LT[p, :, p], s_d1, lt_ok)
            tok["bl"] = sp.dma(CT[0], scr1.rearrange("a b j i -> (a b) (j i)"), s_d2, t, ct_free)
            m = dve.memset(CT[1], 0.0, ct_free)
            tok["bi"] = dve.memset(CT[1][:, 0:256:17], 1.0, m)

        def substitute(j0, j1):
            m = tok["bi"]
            for j in range(j0, j1):
                k = 15 - j
                o = CT[2][:, 0:k * (j + 1)].rearrange("p (a b) -> p a b", b=j + 1)
                p = dve.tt(o, BL[:, j, j + 1:16, None].broadcast_to([128, k, j + 1]),
                           BI[:, j:j + 1, 0:j + 1].broadcast_to([128, k, j + 1]), ALU.mult, tok["bl"], m)
                x = BI[:, j + 1:16, 0:j + 1]
                m = dve.tt(x, x, o, ALU.subtract, p)
            tok["bi"] = m

        def diag_in():
            r = dve.copy(BL, BI.rearrange("p i c -> p c i"), tok["bi"])
            w = sp.dma(scr2[0].rearrange("a b i c -> (a b) (i c)"), CT[1], s_d3, tok["bi"])
            v = sp.dma(scr2[1].rearrange("a b i c -> (a b) (i c)"), CT[0], s_d3, r)
            for k in range(2):
                tok[f"c2{k}"] = (sp, pool)[k].dma(C2[k], scr2[k].rearrange("a b i c -> (b i) a c"), (s_d4, s_d5)[k], v,
                                                  list(G.values()))

        def expand(i):
            for k, dst in ((0, T0), (1, TT)):
                o = dst[:, 4 * i:4 * i + 4, :].rearrange("p a (b c) -> p a b c", c=16)
                t = dve.tt(o, C2[k][:, 4 * i:4 * i + 4, None, :].broadcast_to([128, 4, 8, 16]),
                           BD[:, None, :, None].broadcast_to([128, 4, 8, 16]), ALU.mult, tok[f"c2{k}"],
                           [tok[f"lt{x}"] for x in range(4)])
            tok[f"t{i}"] = t

        at(n, diag_out)
        n += 8
        for k in range(5):
            at(n + k, lambda k=k: substitute(3 * k, 3 * k + 3))
        n += 5
        at(n, diag_in)
        n += 10

        def mask(level, i):
            s4 = slice(4 * i, 4 * i + 4)
            tok[f"m{i}"] = pool.tt(VN[:, s4, :], LT[:, s4, :], LM[:, level:level + 1, :].broadcast_to([128, 4, 128]),
                                   ALU.mult, tok.get(f"y{i}"), tok[f"vr{i}"], tok[f"lt{i}"])

        def y_mm(level, i):
            n, b, t = quads(lambda j: VN[:, 4 * i + j, :], lambda j: T0[:, 4 * i + j, :], tok[f"m{i}"], tok[f"t{i}"])
            tok[f"y{i}"] = t
            if level < 2:
                mask(level + 1, i)
            return n, b, t

        def y_evac(i, b, t):
            hs = slice(2 * i, 2 * i + 2)
            x = quad(b).rearrange("p (h t) e -> p h t e", t=2)
            r = [act.act(Q[:, hs, 0:128], x[:, :, 0, :], AF.Copy, t, tok[f"kq{i}"], tok.get(f"z{i}r")),
                 act.act(K[:, hs, 0:128], x[:, :, 1, :], AF.Copy, t, tok[f"kr{i // 2}"])]
            tok[f"ye{i}"] = r[1]
            return [r[1]]

        def yv(i, j):
            h, tile = hd(i, j)
            return (Q, K)[tile][:, h, 0:128]

        def z_mm(i, which):
            if which == 0:
                return quads(lambda j: TT[:, 4 * i + j, :], lambda j: yv(i, j), tok[f"ye{i}"], tok[f"t{i}"])
            n, b, t = quads(lambda j: yv(i, j), lambda j: TT[:, 4 * i + j, :], tok[f"ye{i}"], tok[f"t{i}"])
            tok[f"z{i}r"] = t
            return n, b, t

        def z_evac(i, which, b, t):
            x = (T0, TT)[which][:, 4 * i:4 * i + 4, :]
            r = dve.tt(x, x, quad(b), ALU.subtract, t, tok[f"z{i}r"])
            tok[f"t{i}"] = r
            return [r]

        for i in range(4):
            at(n - 4 + i, lambda i=i: mask(0, i))
            at(n + i, lambda i=i: expand(i))
        n += 2
        for level in range(3):
            for i in range(4):
                step(n + i, lambda i=i, level=level: y_mm(level, i), lambda b, t, i=i: y_evac(i, b, t))
            n += 4
            w = (0, 1) if level < 2 else (1,)
            for i in range(4):
                for k, which in enumerate(w):
                    step(n + len(w) * i + k, lambda i=i, which=which: z_mm(i, which),
                         lambda b, t, i=i, which=which: z_evac(i, which, b, t), lag=len(w) - k)
            n += 4 * len(w)

        hc = lambda h, tile: 2 * h + tile
        OR = LT
        og_ok = {}

        def rows(x, i, tile):
            return x[:, 8 * i + tile:8 * i + 8:2, :]

        def all_t(i):
            return [tok[f"t{2 * i}"], tok[f"t{2 * i + 1}"]]

        def r_v0(i):
            return quads(lambda j: TT[:, hc(4 * i + j, 0), :], lambda j: VB[:, hc(4 * i + j, 0), :], all_t(i),
                         tok[f"vb{2 * i}"], tok[f"vb{2 * i + 1}"])

        def r_v0e(i, b, t):
            tok[f"v0{i}"] = act.act(rows(VN, i, 0), quad(b), AF.Copy, t, tok[f"y{2 * i}"], tok[f"y{2 * i + 1}"])
            return [tok[f"v0{i}"]]

        def r_s(i):
            return quads(lambda j: KD[:, 4 * i + j, :], lambda j: VN[:, hc(4 * i + j, 0), :], tok[f"v0{i}"],
                         tok[f"kd{i}"])

        def r_se(i, b, t):
            tok[f"st{i}"] = act.act(T0[:, 4 * i:4 * i + 4, :], quad(b), AF.Copy, t, [tok[f"y{k}"] for k in range(4)],
                                    [tok[f"t{k}"] for k in range(4)])
            return [tok[f"st{i}"]]

        def r_o0(i):
            return quads(lambda j: DC[:, hc(4 * i + j, 0), :], lambda j: VN[:, hc(4 * i + j, 0), :],
                         tok[f"at{2 * i}"], tok[f"at{2 * i + 1}"])

        def r_o0e(i, b, t):
            tok[f"o0{i}"] = act.act(rows(OR, i, 0), quad(b), AF.Copy, t, tok[f"m{2 * i}"], tok[f"m{2 * i + 1}"])
            return [tok[f"o0{i}"]]

        def r_w(i):
            return quads(lambda j: K[:, 4 * i + j, 128:256], lambda j: T0[:, 4 * i + j, :], tok[f"st{i}"])

        def r_we(i, b, t):
            tmp = flat(TMP[:, 2 * i:2 * i + 2, :]).rearrange("p (a b) -> p a b", b=128)
            r = dve.tt(tmp, quad(b), BE[:, 1, 4 * i:4 * i + 4, None].broadcast_to([128, 4, 128]), ALU.mult, t,
                       tok[f"bek{2 * i}"], tok[f"bek{2 * i + 1}"], tok["pooled"] if i else None)
            tok[f"vb{i}"] = dve.tt(rows(VB, i, 1), rows(VB, i, 1), tmp, ALU.subtract, r)
            return [r]

        def r_q(i):
            return quads(lambda j: Q[:, 4 * i + j, 128:256], lambda j: T0[:, 4 * i + j, :])

        def r_qe(i, b, t):
            tok[f"o1{i}"] = dve.tt(rows(OR, i, 1), quad(b), EGC[:, 1, 4 * i:4 * i + 4, None].broadcast_to([128, 4, 128]),
                                   ALU.mult, t, tok["gc"], tok[f"m{2 * i}"], tok[f"m{2 * i + 1}"])
            return [tok[f"o1{i}"]]

        def r_v1(i):
            return quads(lambda j: TT[:, hc(4 * i + j, 1), :], lambda j: VB[:, hc(4 * i + j, 1), :], tok[f"vb{i}"],
                         all_t(i))

        def r_v1e(i, b, t):
            tok[f"v1{i}"] = act.act(rows(VN, i, 1), quad(b), AF.Copy, t)
            return [tok[f"v1{i}"]]

        def r_o1(i):
            return quads(lambda j: DC[:, hc(4 * i + j, 1), :], lambda j: VN[:, hc(4 * i + j, 1), :], tok[f"v1{i}"])

        def r_o1e(i, b, t):
            tok[f"o1{i}"] = dve.tt(rows(OR, i, 1), rows(OR, i, 1), quad(b), ALU.add, t, tok[f"o1{i}"])
            return [tok[f"o1{i}"]]

        def squares(i, tile):
            for j in range(4):
                h = 4 * i + j
                t = act.act(JUNK, OR[:, hc(h, tile), :], AF.Square, tok[f"o{tile}{i}"], tok.get("junk"),
                            accum_out=SS[:, tile, h:h + 1])
                tok["junk"] = t
            tok[f"ss{i}"] = t

        def out_norms(i):
            hs = slice(4 * i, 4 * i + 4)
            s, rq = SS[:, :, hs], RQ[:, :, hs]
            r = dve.tt(s, s, rq, ALU.mult, tok[f"ss{i}"], tok[f"rq{2 * i}"], tok[f"rq{2 * i + 1}"])
            r = dve.tt(s, s, rq, ALU.mult, r)
            r = dve.ts(s, s, 1.0 / 128, EPS_, ALU.mult, ALU.add, r)
            r = pool.tt(s, s, MHALF[:, :, None].broadcast_to([128, 2, 4]), ALU.pow, r)
            tok[f"on{i}"] = dve.tt(s, s, rq, ALU.mult, r)

        def o_scale(i):
            x = OR[:, 4 * i:4 * i + 4, :].rearrange("p (h t) e -> p h t e", t=2)
            sc = SS[:, :, 2 * i:2 * i + 2].rearrange("p t h -> p h t")[:, :, :, None].broadcast_to([128, 2, 2, 128])
            tok[f"os{i}"] = dve.tt(x, x, sc, ALU.mult, tok[f"on{i // 2}"])

        def o_tr(i):
            return quads(lambda j: OR[:, 4 * i + j, :], None, tok[f"os{i}"], tr=True)

        def o_evac(i, b, t):
            o = flat(VB[:, 4 * i:4 * i + 4, :])
            k = slice(2 * i, 2 * i + 2)
            m = dve.stt(o, b[:, :], COL["dn"], flat(SZ[:, k, :]), ALU.mult, ALU.mult, t,
                        [tok[f"z{c}"] for c in range(8)], tok["v10"], tok["v11"])
            r = split_into(flat(XH[:, k, :]), flat(XL[:, k, :]), o, m, tok["pool_read"])
            for c in (2 * i, 2 * i + 1):
                og_ok[c] = r
            return [m]

        def both_halves(n, mm, evac, gap=1):
            for i in range(2):
                step(n + gap * i, lambda i=i: mm(i), lambda b, t, i=i: evac(i, b, t))

        both_halves(n, r_v0, r_v0e)
        both_halves(n + 2, r_s, r_se)
        both_halves(n + 4, r_o0, r_o0e)
        both_halves(n + 6, r_w, r_we)
        both_halves(n + 8, r_q, r_qe)
        both_halves(n + 10, r_v1, r_v1e)
        both_halves(n + 12, r_o1, r_o1e)
        for i in range(2):
            at(n + 6 + i, lambda i=i: squares(i, 0))
            at(n + 14 + i, lambda i=i: squares(i, 1))
            at(n + 15 + i, lambda i=i: out_norms(i))
        for i in range(4):
            at(n + 16 + i, lambda i=i: o_scale(i))
            step(n + 17 + i, lambda i=i: o_tr(i), lambda b, t, i=i: o_evac(i, b, t))

        pool_in = {}
        s_inv = sem("inv")

        def pool_side():
            for g in range(4):
                x = XA[:, g, :]
                ring = (TMP[:, 3, :], RTMP)
                prev, t = x, tok[f"xa{g}"]
                for i in range(g + 1):
                    n = 1 << i
                    dst = ring[i % 2]
                    u = [pool.copy(dst[:, 0:n], prev[:, 0:n], t, tok.get("pool_free"), G[7]),
                         pool.tt(dst[:, n:T], prev[:, n:T], prev[:, 0:T - n], ALU.add)]
                    prev, t = dst, u
                    yield
                u = [pool.tt(prev[:, 0:16], prev[:, 0:16], INV[:, g, 0:16], ALU.mult, t, l2_ok),
                     pool.tt(prev[:, 16:T], prev[:, 16:T], INV[:, g, 16:17].broadcast_to([128, T - 16]), ALU.mult, t)]
                t = u
                t = pool.tt(x, prev, x, ALU.subtract, t)
                tok["pool_free"] = t
                for _ in range(4):
                    yield
                i, b, free = side_bank()
                t = pe.mm(b[:, 0:T], PW[:, g, :], x, True, True, free, t, l2_ok, signal=True)
                yield
                sc = COL["pool_scale"][:, g:g + 1]
                h = act.act(XH[:, g, :], b[:, 0:T], AF.Copy, t, xa_read, scale=sc)
                l = dve.stt(XL[:, g, :], b[:, 0:T], sc, XH[:, g, :].bitcast(F32), ALU.mult, ALU.subtract, h)
                idle[i] = [l]
                pool_in[g] = [h, l]
            tok["pooled"] = tok["pool_free"]

        def ev_fn(dst, name, func, **kw):
            def f(ps, t):
                tok[name] = act.act(dst, ps, func, t, **kw)
                return tok[name]
            return f

        sides.append(delta_side())
        sides.append(pool_side())
        for n, u in enumerate(order):
            tile(ev_conv(u), gs, G)
            if n == 0:
                unit(beta_parts(), lambda: None)
                sides.append(gates_side())
        for c in range(8):
            tile(ev_fn(SZ[:, c, :], f"z{c}", AF.Silu), gs, G)
        for c in range(8):
            tile(ev_fn(GA[:, c, :], f"ga{c}", AF.Tanh, scale=0.5), gs, G)
        settle("pooled")
        for i in range(4):
            bi = main_bank()
            b, free = take_bank(bi)
            end = {}

            def ev(i=i, b=b, bi=bi, end=end):
                g = flat(GA[:, 2 * i:2 * i + 2, :])
                a = dve.stt(g, g, 1.0, b[:, :], ALU.add, ALU.mult, end["t"], [tok[f"ga{c}"] for c in range(8)])
                idle[bi] = [a]
                tok[f"ya{i}"] = a
            unit(products([b[:, 0:T], b[:, T:2 * T]], free, xs, pool_in, nk=4, end=end), ev)
        tok["pool_read"] = st.done[st.v]
        for c in range(8):
            tile(ev_fn(GB[:, c, :], f"gb{c}", AF.Tanh, scale=0.5), gs, G)
        g_read2 = st.done[st.v]
        settle("delta")
        y_ok = {}

        def ev_merge(c):
            def f(ps, t):
                g = GB[:, c, :]
                a = dve.stt(g, g, 1.0, ps, ALU.add, ALU.mult, t, tok[f"gb{c}"])
                s = dve.tt(g, g, GA[:, c, :], ALU.add, a, tok[f"ya{c // 2}"])
                h = act.act(GH[:, c, :], g, AF.Copy, s, g_read2, scale=0.5)
                l = dve.stt(GL[:, c, :], g, 0.5, GH[:, c, :].bitcast(F32), ALU.mult, ALU.subtract, h, g_read2)
                y_ok[c] = [h, l]
                return a
            return f

        tiles([ev_merge(c) for c in range(8)], xs, og_ok)
        og_read = st.done[st.v]
        flush()
        h_ok = {}
        X = {}
        stat = Stat(7, 8, og_read, lane=dve)

        def ev_mix(c):
            def f(ps, t):
                h_ok[c] = dve.tt(H[:, c, :], H[:, c, :], ps, ALU.add, t)
                later(1, lambda: mixed_chunk(c))
                return h_ok[c]
            return f

        def mixed_chunk(c):
            X[c] = unscaled(c, COL["ffn"], h_ok[c], og_read)
            stat.add(H[:, c, :], h_ok[c])

        tiles([ev_mix(c) for c in range(8)], gs, y_ok)
        flush()
        run_soon()
        m_read = st.done[st.v]
        ACTS = big[:, :].rearrange("p (e t) -> p e t", t=T)
        A = Arena(32768 - 14848, 32768)
        QP = A.take(4096, T)
        KEYS = A.take(2048, 128)
        SC_AT = A.at // T
        SC = A.take(4096, 128)
        XT = [A.take(128) for _ in range(4)]
        CA = [[A.take(256) for _ in range(2)] for _ in range(2)]
        SMALL = A.take(12 * 256)
        V1, V2, TS, F1, F2, FP, FJ = (SMALL[:, 256 * i:256 * i + 256].rearrange("p (t h k) -> p t h k", t=2, k=16)
                                      for i in range(7))
        U1, U2_, UPOS, UJ = (SMALL[:, 256 * (7 + i):256 * (8 + i)].bitcast(U32).rearrange("p (t h k) -> p t h k", t=2,
                                                                                          k=16) for i in range(4))
        S8 = SMALL[:, 2816:2832].rearrange("p (t h) -> p t h", t=2)
        R8 = SMALL[:, 2832:2848].rearrange("p (t h) -> p t h", t=2)
        I16 = SMALL[:, 2848:2864]
        s_l3 = sem("l3")
        mixed = [t for v in og_ok.values() for t in v] + [t for v in y_ok.values() for t in v]
        sp.dma(KEYS, I["keys"], s_l3, mixed)
        sp.dma(IOTA, I["iota"], s_l3)
        l3_ok = sp.dma(I16, I["iota16"], s_l3)

        accs = [take_bank(3 + i) for i in range(4)]

        def residual_side():
            while "rs4" not in tok:
                yield
            for tile in range(2):
                for half_ in range(2):
                    b, free = accs[2 * tile + half_]
                    for c in range(4):
                        t = pe.mm(b[:, 128 * c:128 * c + 128], H[:, 4 * half_ + c, 128 * tile:128 * tile + 128],
                                  ident[:, :], c == 0, False, free, list(h_ok.values()), signal=c == 3)
                    yield
                    yield
            tok["h_saved"] = t

        pair_at = [0]

        def pair_bank():
            i = (2, 7)[pair_at[0] % 2]
            pair_at[0] += 1
            b, free = take_bank(i)
            return i, b, free

        def scores(h):
            i, b, free = pair_bank()
            for tile in range(2):
                for k in range(2):
                    t = pe.mm(b[:, 256 * tile + 128 * k:256 * tile + 128 * k + 128],
                              QP[:, 2 * h + k, 128 * tile:128 * tile + 128], KEYS[:, 2 * h + k, :], True, True,
                              free, tok[f"q{2 * h}"], tok[f"q{2 * h + 1}"], l3_ok, signal=tile == 1 and k == 1)
            tok["qp_read"] = t

            def out():
                a = act.act(flat(SC[:, 4 * h:4 * h + 4, :]), b[:, :], AF.Copy, t, mixed)
                idle[i] = [a]
                tok[f"sc{h}"] = a
            later(1, out)

        def top16(jobs):
            a = [dve.do(lambda e, v=v, s=s: e.max(v[:, 0:8], s), after) for s, x, v, i, after in jobs]
            yield
            b = [dve.do(lambda e, v=v, s=s, x=x: e.match_replace(x, v[:, 0:8], s, -3.0e38), [k])
                 for k, (s, x, v, i, after) in zip(a, jobs)]
            yield
            c = [dve.do(lambda e, v=v, x=x: e.max(v[:, 8:16], x), [k]) for k, (s, x, v, i, after) in zip(b, jobs)]
            yield
            d = [dve.do(lambda e, v=v, s=s, i=i: e.max_index(i[:, 0:8], v[:, 0:8], s), [k])
                 for k, (s, x, v, i, after) in zip(a, jobs)]
            yield
            f = [dve.do(lambda e, v=v, x=x, i=i: e.max_index(i[:, 8:16], v[:, 8:16], x), [k])
                 for k, (s, x, v, i, after) in zip(c, jobs)]
            yield
            return a + c + d + f

        def topk_side():
            for h in range(8):
                while f"sc{h}" not in tok:
                    yield
                for tile in range(2):
                    r = yield from top16([(SC[:, 4 * h + 2 * tile + k, :], XT[2 * tile + k], v[:, tile, h, :],
                                           u[:, tile, h, :], [tok[f"sc{h}"], mixed])
                                          for k, v, u in ((0, V1, U1), (1, V2, U2_))])
                    ca, cb = CA[tile]
                    t = dve.tt(ca.rearrange("p (a b) -> p a b", b=16), V1[:, tile, h, :, None].broadcast_to([128, 16, 16]),
                               V2[:, tile, h, None, :].broadcast_to([128, 16, 16]), ALU.add, r)
                    yield
                    tok[f"t{h}{tile}"] = yield from top16([(ca, cb, TS[:, tile, h, :], UPOS[:, tile, h, :], [t])])
            done = [tok[f"t{h}{tile}"] for h in range(8) for tile in range(2)]
            W = flat(SC)
            EQS = [W[:, 2048 * i:2048 * i + 2048] for i in range(2)]
            b = dve.do(lambda e: e.tensor_single_scalar(UJ, UPOS, 15, ALU.bitwise_and), [done])
            a = dve.do(lambda e: e.tensor_single_scalar(UPOS, UPOS, 4, ALU.logical_shift_right), [b])
            f = [dve.copy(FP, UPOS, a), dve.copy(FJ, UJ, b), dve.copy(F1, U1), dve.copy(F2, U2_)]
            yield
            g = dve.copy(R8, TS[:, :, :, 0], done)
            g = dve.tt(TS, TS, R8[:, :, :, None].broadcast_to([128, 2, 8, 16]), ALU.subtract, g)
            g = act.act(TS, TS, AF.Exp, g)
            yield
            yield
            s = dve.reduce(S8, TS, ALU.add, g)
            s = dve.recip(R8, S8, s)
            g = dve.tt(TS, TS, R8[:, :, :, None].broadcast_to([128, 2, 8, 16]), ALU.mult, s)
            yield
            picked, m = {}, {}
            work = [(tile, pos, idx) for tile in range(2) for pos, idx in ((FP, F1), (FJ, F2))]

            def equal(k):
                tile, pos, idx = work[k]
                e = EQS[k % 2]
                m[k] = dve.tt(e.rearrange("p (a b) -> p a b", b=16),
                              pos[:, tile, :, :].rearrange("p h k -> p (h k)")[:, :, None].broadcast_to([128, 128, 16]),
                              I16[:, None, :].broadcast_to([128, 128, 16]), ALU.is_equal, f, l3_ok, picked.get(k - 2))
                e4 = e.rearrange("p (h k i) -> p h k i", k=16, i=16)
                m[k] = pool.tt(e4, e4, idx[:, tile, :, None, :].broadcast_to([128, 8, 16, 16]), ALU.mult, m[k], f)

            def pick(k):
                tile, pos, idx = work[k]
                picked[k] = dve.reduce(pos[:, tile, :, :].rearrange("p h k -> p (h k)"),
                                       EQS[k % 2].rearrange("p (a b) -> p a b", b=16), ALU.add, m[k])

            for fn, k, ticks in ((equal, 0, 4), (equal, 1, 6), (pick, 0, 3), (equal, 2, 3), (pick, 1, 3), (equal, 3, 6),
                                 (pick, 2, 6), (pick, 3, 1)):
                fn(k)
                for _ in range(ticks):
                    yield
            i, b, free = pair_bank()
            for tile in range(2):
                for n, src in enumerate((FP, FJ)):
                    t = pe.tr(b[:, 256 * n + 128 * tile:256 * n + 128 * tile + 128],
                              src[:, tile, :, :].rearrange("p h k -> p (h k)"), ident[:, :], free,
                              list(picked.values()), signal=n == 1 and tile == 1)
            yield
            a = act.act(ET, b[:, :].rearrange("p (n t) -> p n t", n=2), AF.Copy, t)
            idle[i] = [a]
            i, b, free = pair_bank()
            for tile in range(2):
                t = pe.tr(b[:, 128 * tile:128 * tile + 128], TS[:, tile, :, :].rearrange("p h k -> p (h k)"),
                          ident[:, :], free, g, signal=tile == 1)
            yield
            g = act.act(GATE, b[:, 0:256], AF.Copy, t)
            idle[i] = [g]
            tok["chosen"] = [a, g]
            turns[0] = 4

        def ev_query(u):
            def f(ps, t):
                tok[f"q{u}"] = dve.tt(QP[:, u, :], ps, RSB, ALU.mult, t, tok["rs4"], mixed)
                if u % 2:
                    later(2, lambda: scores(u // 2))
                return tok[f"q{u}"]
            return f

        sides.append(scaled_side(COL["ffn"], "rs4", "xs4", [m_read]))
        sides.append(residual_side())
        sides.append(topk_side())
        turns[0] = 2
        tiles([ev_query(u) for u in range(3)], xs, X, stat=stat, name="rs4")
        mains[:] = [[0, 1], 1]
        for u in range(3, 16):
            tile(ev_query(u), xs, X)
        q_read = st.done[st.v]
        G = tok["xs4"]
        g_all = [t for v in G.values() for t in v]
        progress = [0]
        built = [0]
        last = {"act": None, "dve": None, "pool": None}
        onehot = [flat(x[:, 4 * k:4 * k + 4, :]).rearrange("p (t n i) -> p t n i", n=2, i=128)
                  for k in range(2) for x in (XH, XL)]
        oh_free = [None] * 4
        vg_free = [None] * 4

        def build_side():
            while "chosen" not in tok:
                yield
            flats, table = {}, {}

            def hot(g):
                r = g % 4
                flats[g] = dve.tt(onehot[r], IOTA[:, None, None, :].broadcast_to([128, 4, 2, 128]),
                                  ET[:, :, 4 * g:4 * g + 4].rearrange("p n t -> p t n")[:, :, :, None].broadcast_to(
                                      [128, 4, 2, 128]), ALU.is_equal, l3_ok, tok["chosen"], oh_free[r], q_read)

            def scale(g):
                for j in range(4):
                    v = act.act(VG[j], onehot[g % 4][:, j, 1, :].bitcast(F32), AF.Copy, flats[g], vg_free[j],
                                scale=GATE[:, 4 * g + j:4 * g + j + 1])
                    flats[g, j] = v

            def multiply(g):
                i, b, free = pair_bank()
                for j in range(4):
                    vg_free[j] = pe.mm(b[:, 128 * j:128 * j + 128], onehot[g % 4][:, j, 0, :].bitcast(F32), VG[j],
                                       True, True, free, flats[g, j], signal=True)
                oh_free[g % 4] = vg_free[3]
                table[g] = (i, b, vg_free[3])

            def fold(g):
                t0 = 4 * g
                i, b, t = table[g]
                n = progress[0]
                g4 = b[:, :].rearrange("p (t e) -> p e t", e=128)
                a = None
                if n:
                    x = ACTS[:, 0:n, t0:t0 + 4]
                    a = last["dve"] = dve.tt(x, x, g4[:, 0:n, :], ALU.mult, t, last["act"], last["pool"])
                table[g] += (g4, a, n)

            def fill(g):
                i, b, t, g4, a, n = table[g]
                t0 = 4 * g
                idle[i] = [a]
                assert n == progress[0]
                if n < 128:
                    last["act"] = act.act(ACTS[:, n:128, t0:t0 + 4], g4[:, n:128, :], AF.Copy, t, a, tok["chosen"])
                    idle[i] = [last["act"]]
                built[0] = t0 + 4

            n = T // 4
            for g in range(n + 2):
                yield
                if g > 1:
                    multiply(g - 2)
                yield
                if g > 1:
                    fold(g - 2)
                if g < n:
                    hot(g)
                if 0 < g <= n:
                    scale(g - 1)
                yield
                if g > 1:
                    fill(g - 2)
                yield
            tok["built"] = True

        def ev_down(n):
            def f(ps, t):
                m = built[0]
                r = t
                free = [mixed, tok["h_saved"], g_all]
                if 70 <= n:
                    free += [tok["qp_read"]]
                if m < T:
                    r = last["act"] = act.act(ACTS[:, n, m:T], ps[:, m:T], AF.Gelu, t, free,
                                              tok["chosen"] if n >= SC_AT else None)
                if m > 0:
                    r = act.act(TG[:, 0:m], ps[:, 0:m], AF.Gelu, t, last["pool"])
                    x = ACTS[:, n, 0:m]
                    last["pool"] = pool.tt(x, x, TG[:, 0:m], ALU.mult, r, last["act"], last["dve"])
                progress[0] = n + 1
                return r
            return f

        turns[0] = 3
        sides.append(build_side())
        for n in range(128):
            tile(ev_down(n), gs, G)
        flush()
        settle("built")
        ready = list(last.values())
        W_AHEAD = 3
        parts = {}
        used = {}

        def cut(n):
            if n < 128:
                s = (n + 4) % 8
                parts[n] = split_into(XH[:, s, :], XL[:, s, :], ACTS[:, n, :], ready, used.get(n - 8), oh_free)

        for n in range(W_AHEAD):
            cut(n)
        out_ok = []
        for n in range(128):
            def up_parts(n=n):
                v, wh, wl, h_ok_, l_ok = st.take()
                s = (n + 4) % 8
                for tile in range(2):
                    a = XH[:, s, 128 * tile:128 * tile + 128]
                    b = XL[:, s, 128 * tile:128 * tile + 128]
                    for half_ in range(2):
                        o, _ = accs[2 * tile + half_]
                        w = slice(512 * half_, 512 * half_ + 512)
                        pe.mm(o[:, :], a, wh[:, w], False, False, h_ok_, parts[n])
                        pe.mm(o[:, :], a, wl[:, w], False, False, l_ok)
                    for half_ in range(2):
                        o, _ = accs[2 * tile + half_]
                        w = slice(512 * half_, 512 * half_ + 512)
                        t = pe.mm(o[:, :], b, wh[:, w], False, n == 127, signal=half_ == 1)
                    if n == 127:
                        out_ok.append(t)
                    yield
                st.done[v] = used[n] = t

            unit(up_parts(), lambda: None)
            cut(n + W_AHEAD)
        flush()

        FW = big[:, 0:1024]
        O = big[:, 1024:3072].rearrange("p (t d) -> p t d", t=2)
        FS = big[:, 3072:3080]
        s_fin, s_out = sem("fin"), sem("out")
        fin_ok = sp.dma(FW, I["fnw"], s_fin, parts[63])
        for tile in range(2):
            r = []
            for half_ in range(2):
                w = slice(512 * half_, 512 * half_ + 512)
                o, _ = accs[2 * tile + half_]
                r.append(act.act(O[:, tile, w], o[:, :], AF.Square, out_ok[tile], parts[63],
                                 accum_out=FS[:, 2 * tile + half_:2 * tile + half_ + 1]))
            s = dve.tt(FS[:, 4 + tile:5 + tile], FS[:, 2 * tile:2 * tile + 1], FS[:, 2 * tile + 1:2 * tile + 2],
                       ALU.add, r)
            s = dve.ts(FS[:, 4 + tile:5 + tile], FS[:, 4 + tile:5 + tile], 1.0 / D, EPS_, ALU.mult, ALU.add, s)
            s = pool.tt(FS[:, 6 + tile:7 + tile], FS[:, 4 + tile:5 + tile], MHALF, ALU.pow, s)
            for half_ in range(2):
                w = slice(512 * half_, 512 * half_ + 512)
                o, _ = accs[2 * tile + half_]
                a = dve.stt(O[:, tile, w], o[:, :], FS[:, 6 + tile:7 + tile], FW[:, w], ALU.mult, ALU.mult, s, r, fin_ok)
                end = sp.dma(out[0, 128 * tile:128 * tile + 128, w], O[:, tile, w], s_out, a)
        sp.wait(end)
        with nc.Block() as block:
            @block.sync
            def _(e):
                sp.emit(e)

            @block.gpsimd
            def _(e):
                pool.emit(e)

            @block.tensor
            def _(e):
                pe.emit(e)

            @block.scalar
            def _(e):
                act.emit(e)

            @block.vector
            def _(e):
                dve.emit(e)


def prepare(inputs):
    import numpy as np
    f = np.float32
    x = {k: np.asarray(v) for k, v in inputs.items()}
    tiles = []

    def feature_tiles(w):
        n = w.shape[1] // 128
        tiles.append(w.reshape(8, 128, n, 128).transpose(2, 1, 0, 3).reshape(n, 128, 1024))

    def half_tiles(w):
        return w.reshape(4, 128, 4, 2, 128).transpose(2, 1, 0, 3, 4).reshape(4, 128, 1024)

    w = x["w_in"][0]
    o = np.cumsum([0, 512, 128, 128, 128, 128, 128, 128, 24, 512, 128, 128, 1024, 1024])
    part = [w[:, o[i]:o[i + 1]] for i in range(13)]
    qn, kc, vc, ks, vs, kw, vw, gn, qs, kk, vv, ga, gb = part

    def pairs(q):
        return q.reshape(1024, 2, 4, 64).transpose(0, 2, 1, 3).reshape(1024, 512)

    gates = gn.reshape(1024, 2, 4, 3).transpose(0, 3, 2, 1).reshape(1024, 24)
    feature_tiles(np.concatenate([kc, vc, ks, kw, pairs(qn)], 1))
    tm = np.concatenate([vs, vw, vv, gates, np.zeros((1024, 104), f)], 1)
    tiles.append(tm.reshape(4, 2, 128, 512).transpose(0, 2, 1, 3).reshape(4, 128, 1024))
    feature_tiles(np.concatenate([kk, pairs(qs), ga, gb], 1))
    ups = []
    for k in ("w_up_nsa", "w_up_swa"):
        ups.append(half_tiles(x[k][0].reshape(2, 4, 64, 1024).transpose(1, 0, 2, 3).reshape(512, 1024)))
    tiles.append(np.stack(ups, 1).reshape(8, 128, 1024))
    feature_tiles(x["w_out"][0])
    w1, w2 = x["w_mlp_in"][0], x["w_mlp_out"][0]
    for q in range(9):
        if q < 8:
            feature_tiles(w1[:, 512 * q:512 * q + 512])
        if q > 0:
            tiles.append(half_tiles(w2[512 * q - 512:512 * q]))
    w = x["w_in_2"][0]
    xa, qkv, z, ba, ga, gb = np.split(w, [512, 3584, 4608, 4624, 5648], axis=1)
    qkv = qkv.reshape(1024, 3, 8, 128).transpose(0, 2, 1, 3).reshape(1024, 3072)
    feature_tiles(np.concatenate([xa, qkv, z, ga], 1))
    tiles.append(half_tiles(x["w_pool_up_2"][0]))
    feature_tiles(np.concatenate([gb, x["w_dn_up_2"][0]], 1))
    feature_tiles(x["w_mix_out_2"][0])
    feature_tiles(x["peer_w_query_2"][0])
    tiles.append(x["peer_down_2"][0].reshape(128, 128, 8, 128).transpose(1, 3, 2, 0).reshape(128, 128, 1024))
    tiles.append(x["peer_up_2"][0].reshape(128, 128, 1024).transpose(1, 0, 2))
    wst = np.concatenate(tiles, 0)

    cols = [x[k].reshape(-1, 128).T for k in ("norm_mix_pre", "norm_mix_post", "norm_mlp_pre", "norm_mlp_post",
                                              "mix_norm_w_2", "ffn_norm_w_2", "pool_scale_2")]
    cols.append(x["conv_w_2"][0].reshape(4, 24, 128).transpose(2, 1, 0).reshape(128, 96))
    cols.append(x["dn_norm_w_2"].reshape(128, 1))
    cols.append(np.full((128, 1), 1e-6, f))
    cols.append(np.full((128, 1), -0.5, f))
    cols.append((np.arange(128)[:, None] // 16 == np.arange(8)).astype(f))

    dist = 255 - np.arange(384)
    start = np.array([*range(17), 21, 27, 35, 46, 59, 77, 99, 128, 166, 216])
    bucket = np.searchsorted(start, dist, side="right") - 1
    oneh = np.zeros((32, 384), f)
    oneh[bucket[dist >= 0], np.arange(384)[dist >= 0]] = 8.0
    bmask = np.zeros((16, 384), f)
    bmask[:, dist < 0] = -1e30
    bmask[8:, dist >= 128] = -1e30
    relb = x["rel_bias"].reshape(32, 2, 2, 4).transpose(0, 1, 3, 2).reshape(32, 16)
    t = np.arange(256).reshape(2, 128).T
    end = np.arange(15) * 16 + 31
    ok = (end <= t[:, :, None])
    cmask = np.concatenate([np.where(ok, 0, -1e30), ok], 2).astype(f)
    sel = np.zeros((30, 128), f)
    for r in range(128):
        if r % 16 < 15:
            sel[(r // 16 % 2) * 15 + r % 16, r] = 1
    i = np.arange(128)
    tri = (i[:, None] <= i).astype(f)
    lmask = np.stack([(i[:, None] // (2 * n) == i // (2 * n)) & (i // n % 2 == 1) & (i[:, None] // n % 2 == 0)
                      for n in (16, 32, 64)], 1).astype(f)
    inv = 1.0 / np.minimum(np.arange(1, 18), np.array([[2], [4], [8], [16]]))
    keys = np.stack([x["peer_keys_1_2"][0], x["peer_keys_2_2"][0]], 1)
    d = {
        "keys": keys.transpose(3, 0, 1, 2).reshape(128, 16, 128),
        "iota16": np.broadcast_to(np.arange(16, dtype=f), (128, 16)),
        "iota": np.broadcast_to(np.arange(128, dtype=f), (128, 128)),
        "fnw": np.broadcast_to(x["final_norm_w_2"][None], (128, 1024)),
        "tri": tri, "suf": (i[:, None] > i).astype(f), "negm": np.where(i[:, None] <= i, 0, -1e30).astype(f),
        "lmask": lmask, "baw": ba.reshape(8, 128, 16).transpose(1, 0, 2).reshape(128, 128),
        "alog": np.broadcast_to(x["a_log_2"].reshape(1, 8), (128, 8)),
        "dtb": np.broadcast_to(x["dt_bias_2"].reshape(1, 8), (128, 8)),
        "poolw": x["pool_w_2"][0].transpose(1, 0, 2),
        "inv": np.broadcast_to(inv.astype(f)[None], (128, 4, 17)),
        "wst": wst,
        "xT": x["x"][0].T.reshape(8, 128, 256).transpose(1, 0, 2),
        "cols": np.concatenate(cols, 1),
        "ident": np.eye(128, dtype=f),
        "relb": relb, "oneh": oneh, "bmask": bmask,
        "pos": np.concatenate([x[k][0].reshape(16, 128).T for k in ("cmp_pos_k", "cmp_pos_v")], 1),
        "w1k": x["cmp_w1_k"][0].reshape(16, 128, 256).transpose(1, 0, 2),
        "w1v": x["cmp_w1_v"][0].reshape(16, 128, 256).transpose(1, 0, 2),
        "w2k": np.concatenate([x["cmp_w2_k"][0]] * 2, 1).reshape(2, 128, 128).transpose(1, 0, 2),
        "w2v": x["cmp_w2_v"][0].reshape(2, 128, 64).transpose(1, 0, 2),
        "sinks": np.broadcast_to(x["attn_sinks"].reshape(2, 4).T.reshape(1, 8), (128, 8)),
        "cmask": cmask, "sel": sel,
    }
    return {k: np.ascontiguousarray(v) for k, v in d.items()}


def kernel(**inputs):
    from concourse import bacc
    from concourse.bass_utils import run_bass_kernel_spmd

    arrays = prepare(inputs)
    nc = bacc.Bacc("TRN2", target_bir_lowering=False, num_devices=1)
    operands = {name: nc.dram_tensor(f"in_{name}", a.shape, mybir.dt.from_np(a.dtype), kind="ExternalInput").ap()
                for name, a in arrays.items()}
    out = nc.dram_tensor("out_0", (1, T, D), mybir.dt.float32, kind="ExternalOutput").ap()
    program(nc, operands, out)
    result = run_bass_kernel_spmd(nc, [{f"in_{name}": a for name, a in arrays.items()}], core_ids=[0])
    return result.results[0]["out_0"]
```

```python
import concourse.bass as bass
from concourse import mybir
from contextlib import ExitStack

T = 256
D = 1024
UNITS = 457


class Sem:

    def __init__(self, handle):
        self.handle = handle
        self.value = 0

    def add(self, n):
        self.value += n
        return (self, self.value)


class Lane:

    def __init__(self, sem):
        self.sem = sem
        self.queue = []
        self.passed = {}

    def wait(self, *after):
        for a in after:
            if a is None:
                continue
            if isinstance(a, list):
                self.wait(*a)
                continue
            sem, value = a
            if self.passed.get(id(sem), 0) < value:
                self.passed[id(sem)] = value
                self.queue.append(lambda e, s=sem, v=value: e.wait_ge(s.handle, v))

    def do(self, fn, after=(), signal=True):
        self.wait(*after)
        if not signal:
            self.queue.append(fn)
            return None
        self.queue.append(lambda e: fn(e).then_inc(self.sem.handle, 1))
        return self.sem.add(1)

    def dma(self, out, in_, sem, *after, **kw):
        self.wait(*after)
        self.queue.append(lambda e: e.dma_start(out, in_, **kw).then_inc(sem.handle, 16))
        return sem.add(16)

    def emit(self, engine):
        for fn in self.queue:
            fn(engine)


class Vec(Lane):
    def tt(self, out, in0, in1, op, *after):
        return self.do(lambda e: e.tensor_tensor(out, in0, in1, op), after)

    def ts(self, out, in0, s1, s2, op0, op1, *after):
        if s2 is None:
            return self.do(lambda e: e.tensor_scalar(out, in0, s1, None, op0), after)
        return self.do(lambda e: e.tensor_scalar(out, in0, s1, s2, op0, op1), after)

    def stt(self, out, in0, s, in1, op0, op1, *after):
        return self.do(lambda e: e.scalar_tensor_tensor(out, in0, s, in1, op0, op1), after)

    def copy(self, out, in_, *after):
        return self.do(lambda e: e.tensor_copy(out, in_), after)

    def recip(self, out, in_, *after):
        return self.do(lambda e: e.reciprocal(out, in_), after)

    def memset(self, out, v, *after):
        return self.do(lambda e: e.memset(out, v), after)

    def reduce(self, out, in_, op, *after):
        return self.do(lambda e: e.tensor_reduce(out, in_, mybir.AxisListType.X, op), after)


class Act(Lane):
    def act(self, out, in_, func, *after, **kw):
        return self.do(lambda e: e.activation(out, in_, func, **kw), after)


class Pe(Lane):
    def mm(self, out, lhsT, rhs, start, stop, *after, signal=False):
        return self.do(lambda e: e.matmul(out, lhsT, rhs, start=start, stop=stop, skip_group_check=True),
                       after, signal)

    def tr(self, out, in_, ident, *after, signal=False):
        return self.do(lambda e: e.transpose(out, in_, ident), after, signal)


def program(nc, I, out):
    F32 = mybir.dt.float32
    F32R = mybir.dt.float32r
    U32 = mybir.dt.uint32
    ALU = mybir.AluOpType
    AF = mybir.ActivationFunctionType

    RR, RW = 4, 3
    LS = RW - 1
    LD = LS + RR

    ctx = ExitStack()
    with ctx:
        sb = lambda name, shape, dt: ctx.enter_context(nc.sbuf_tensor(name, shape, dt))
        sem = lambda name: Sem(ctx.enter_context(nc.semaphore(name)))

        pe, act, dve, pool, sp = Pe(sem("pe")), Act(sem("act")), Vec(sem("dve")), Vec(sem("pool")), Lane(sem("sp"))
        big = sb("big", [128, 32768], F32)
        XH = sb("xh", [128, 8, T], F32R)
        XL = sb("xl", [128, 8, T], F32R)
        GH = sb("gh", [128, 8, T], F32R)
        GL = sb("gl", [128, 8, T], F32R)
        raw = sb("raw", [128, RR, 1024], F32)
        WH = sb("wh", [128, RW, 1024], F32R)
        WL = sb("wl", [128, RW, 1024], F32R)
        ident = sb("ident", [128, 128], F32)
        ones = sb("ones", [128, 128], F32)
        misc = sb("misc", [128, 1412], F32)
        ET = misc[:, 0:512].rearrange("p (n t) -> p n t", n=2)
        GATE = misc[:, 512:768]
        IOTA = misc[:, 768:896]
        RS2 = misc[:, 896:900]
        RS4 = misc[:, 900:902]
        VG = [misc[:, 900:1028], misc[:, 1028:1156], ones[:, :], ident[:, :]]
        TG = misc[:, 1156:1412]
        cols = sb("cols", [128, I["cols"].shape[1]], F32)
        banks = [ctx.enter_context(nc.psum_tensor(f"bank{i}", [128, 512], F32)) for i in range(8)]
        idle = [[] for _ in range(8)]

        class Arena:
            def __init__(self, at, end):
                self.at, self.end = at, end

            def take(self, n, m=None):
                a = big[:, self.at:self.at + n]
                self.at += n
                assert self.at <= self.end, (self.at, self.end)
                return a if m is None else a.rearrange("p (a b) -> p a b", b=m)

        def take_bank(i):
            free = idle[i]
            assert free is not None, f"bank {i} is in use"
            idle[i] = None
            return banks[i], free

        def quad(x):
            return x[:, :].rearrange("p (a b) -> p a b", b=128)

        def flat(x):
            return x.rearrange("p a b -> p (a b)")

        s_const = sem("const")
        s_ident = sem("ident")
        c_ready = sp.dma(cols[:, :], I["cols"], s_const)
        ones_ready = dve.memset(ones[:, :], 1.0)
        act.act(misc[:, 0:1], ones[:, 0:1], AF.Copy, ones_ready)
        COL = {}
        n = 0
        for name, w in (("mix_pre", 8), ("mix_post", 8), ("mlp_pre", 8), ("mlp_post", 8), ("mix2", 8), ("ffn", 8),
                        ("pool_scale", 4), ("conv", 96), ("dn", 1), ("eps", 1), ("mhalf", 1), ("bd", 8), ("atanh", 10)):
            COL[name] = cols[:, n:n + w]
            n += w
        MHALF = COL["mhalf"]
        EPS_ = 1e-6
        BD = COL["bd"]

        def keep_warm(i, n):
            b, free = take_bank(i)
            for k in range(n):
                t = pe.mm(b[:, 0:128], ones[:, :], ones[:, :], True, True, free, ones_ready, signal=k == n - 1)
            idle[i] = [t]

        class Stream:

            def __init__(self):
                self.used = self.cut = self.got = 0
                self.ahead = LS
                self.share = 0
                self.early = [sem("early0"), sem("early1")]
                self.load_sem = [sem(f"load{i}") for i in range(RR)]
                self.load, self.hi, self.lo, self.done = {}, {}, {}, {}

            def fetch(self, upto):
                while self.got < min(upto, UNITS) and (self.got < RR or self.got - RR in self.lo):
                    v = self.got
                    self.load[v] = []
                    for w in self.cuts(v):
                        s = self.load_sem[v % RR] if w.stop == 1024 else self.early[v]
                        self.load[v].append(sp.dma(raw[:, v % RR, w], I["wst"][v][:, w], s, self.lo.get(v - RR)))
                    self.got += 1

            def split(self, upto):
                while self.cut < min(upto, UNITS) and (self.cut < RW or self.cut - RW in self.done):
                    v = self.cut
                    w_free = self.done.get(v - RW)
                    self.hi[v], self.lo[v] = [], []
                    for n, w in enumerate(self.cuts(v)):
                        x, h = raw[:, v % RR, w], WH[:, v % RW, w]
                        self.hi[v].append(act.act(h, x, AF.Copy, self.load[v][n], w_free))
                        own = w.stop - w.start - self.share
                        for lane, c in ((dve, slice(0, own)), (pool, slice(own, own + self.share))):
                            if c.start < c.stop:
                                self.lo[v].append(lane.tt(WL[:, v % RW, w][:, c], x[:, c], h[:, c].bitcast(F32),
                                                          ALU.subtract, self.load[v][n], self.hi[v][n], w_free))
                    self.cut += 1

            def cuts(self, v):
                return [slice(0, 512), slice(512, 1024)] if v < 2 else [slice(0, 1024)]

            def take(self):
                v = self.used
                self.used += 1
                self.fetch(v + LD + 1)
                self.split(v + self.ahead + 1)
                self.fetch(v + LD + 1)
                assert v < self.cut
                self.v = v
                return v, WH[:, v % RW, :], WL[:, v % RW, :], self.hi[v], self.lo[v]

        st = Stream()

        sides = []
        soon = []
        pending = []
        turns = [1]
        mains = [[0, 1, 2], 0]
        current = [None]

        place = [0]

        def tick():
            place[0] += 1
            for s in list(sides):
                if next(s, "end") == "end":
                    sides.remove(s)

        def later(n, fn):
            soon.append([n, fn])

        def flush():
            while pending:
                pending.pop(0)()

        def run_soon():
            for job in soon:
                job[0] -= 1
            while soon and soon[0][0] <= 0:
                soon.pop(0)[1]()

        def unit(parts, evac, hooks=None, at=0, hold=False):
            n = place[0] = 0
            if at == 0 and not hold:
                run_soon()
                flush()
            for _ in parts:
                n += 1
                if hooks and n in hooks:
                    hooks[n]()
                if n == at:
                    run_soon()
                    flush()
                if n <= turns[0]:
                    tick()
            for _ in range(n, turns[0]):
                tick()
            if not hold:
                flush()
            pending.append(evac)

        def settle(*names):
            while sides and (not names or any(x not in tok for x in names)):
                run_soon()
                tick()

        def main_bank():
            which, at = mains
            i = which[at % len(which)]
            mains[1] += 1
            current[0] = i
            return i

        def use_mains(which):
            mains[:] = [which, next(k for k, i in enumerate(which) if i != current[0])]

        def xs(k):
            return XH[:, k, :], XL[:, k, :]

        def gs(k):
            return GH[:, k, :], GL[:, k, :]

        def high(parts):
            return parts[:1] if len(parts) == 2 else parts

        def products(outs, free, x, ready, nk=8, k0=0, first=True, last=True, end=None):
            v, wh, wl, h_ok, l_ok = st.take()
            groups = len(outs)
            for g, o in enumerate(outs):
                for k in range(nk):
                    c = k * groups + g
                    xh, xl = x(k0 + k)
                    a = wh[:, c * 128:(c + 1) * 128]
                    b = wl[:, c * 128:(c + 1) * 128]
                    pe.mm(o, a, xh, first and k == 0 and g == 0, False, free, h_ok, high(ready[k0 + k]))
                    pe.mm(o, a, xl, False, False, ready[k0 + k])
                    t = pe.mm(o, b, xh, False, last and k == nk - 1, l_ok, signal=k == nk - 1 and g == groups - 1)
                    if c % 2:
                        if t:
                            st.done[v] = end["t"] = t
                        yield

        def two_products(oa, ob, free, x, ready, end):
            two = [(o, st.take()) for o in (oa, ob)]
            for k in range(8):
                xh, xl = x(k)
                c = slice(k * 128, k * 128 + 128)
                for o, (v, wh, wl, h_ok, l_ok) in two:
                    if v < 2:
                        h_ok, l_ok = h_ok[k // 4], l_ok[k // 4]
                    pe.mm(o, wh[:, c], xh, k == 0, False, free, h_ok, high(ready[k]))
                    pe.mm(o, wh[:, c], xl, False, False, ready[k])
                    t = pe.mm(o, wl[:, c], xh, False, k == 7, l_ok, signal=k == 7)
                    if t:
                        st.done[v] = t
                        end.append(t)
                if k % 2:
                    yield

        def tile(evac, x, ready, **kw):
            i = main_bank()
            b, free = take_bank(i)
            end = {}

            def ev():
                idle[i] = [evac(b[:, 0:T], end["t"])]
            unit(products([b[:, 0:T]], free, x, ready, end=end), ev, **kw)

        def scaled_by(stat, name):
            def spread():
                tok[name] = stat.into(RSB)
            return {"hooks": {1: stat.sums, 4: spread}, "at": 4}

        def tiles(evacs, x, ready, pair=True, stat=None, name=None):
            kw = scaled_by(stat, name) if stat else {}
            if pair:
                ia, ib = main_bank(), main_bank()
                (ba, fa), (bb, fb) = take_bank(ia), take_bank(ib)
                end = []

                def ev():
                    idle[ia] = [evacs[0](ba[:, 0:T], end[0])]
                    idle[ib] = [evacs[1](bb[:, 0:T], end[1])]
                unit(two_products(ba[:, 0:T], bb[:, 0:T], fa + fb, x, ready, end), ev)
            for e in evacs[2 if pair else 0:]:
                tile(e, x, ready, **kw)
                kw = {}

        def split_into(h, l, src, *after):
            a = act.act(h, src, AF.Copy, *after)
            b = dve.tt(l, src, h.bitcast(F32), ALU.subtract, a, *after)
            return [a, b]

        SQN = 3

        class Stat:

            def __init__(self, bank, n, *free, lane=None, ring=None, alone=1):
                self.alone, self.own = alone, []
                self.ring = ring or [SQ[:, i, :] for i in range(SQN)]
                self.bank, self.n, self.free, self.c = bank, n, list(free), 0
                self.lane = lane or pool
                self.read = {}

            def add(self, src, *after):
                c = self.c
                self.c += 1
                r = self.ring
                s = r[c % len(r)]
                a = act.act(s, src, AF.Square, self.read.get(c - len(r)), self.free, *after)
                if c == 0:
                    self.prev = a
                elif c == 1:
                    self.sum = self.read[0] = self.read[1] = self.lane.tt(ACC, r[0], s, ALU.add, self.prev, a, self.free)
                elif c < self.n - self.alone:
                    self.sum = self.read[c] = self.lane.tt(ACC, ACC, s, ALU.add, self.sum, a)
                else:
                    self.own.append((s, a))
                return a

            def sums(self, scale=None):
                b, free = take_bank(self.bank)
                for tile in range(2):
                    ts = slice(128 * tile, 128 * tile + 128)
                    o = b[:, tile:tile + 1]
                    pe.mm(o, ACC[:, ts], ones[:, 0:1], True, False, free, self.sum, ones_ready)
                    for n, (s, a) in enumerate(self.own):
                        t = pe.mm(o, s[:, ts], ones[:, 0:1], False, n == len(self.own) - 1, a,
                                  signal=n == len(self.own) - 1)
                self.used = t
                if scale is None:
                    t = dve.ts(RS2[:, 0:2], b[:, 0:2], 1.0 / D, EPS_, ALU.mult, ALU.add, t)
                else:
                    t = [dve.ts(RS2[:, n:n + 1], b[:, n:n + 1], scale[:, n:n + 1], EPS_, ALU.mult, ALU.add, t)
                         for n in range(2)]
                self.t = pool.tt(RS2[:, 2:4], RS2[:, 0:2], MHALF.broadcast_to([128, 2]), ALU.pow, t, c_ready)

            def spread(self):
                b = banks[self.bank]
                for tile in range(2):
                    t = pe.mm(b[:, T + 128 * tile:T + 128 * tile + 128],
                              RS2[:, 2 + tile:3 + tile].broadcast_to([128, 128]), ident[:, :], True, True, self.t,
                              tok["ident"], signal=True)
                return b[:, T:2 * T], t

            def into(self, dst, *after):
                rs, t = self.spread()
                a = act.act(dst, rs, AF.Copy, t, *after)
                idle[self.bank] = [a]
                return a

        tok = {}
        A = Arena(0, 32768)
        H = A.take(2048, T)
        RSA, RSB, RTMP, ACC = A.take(T), A.take(T), A.take(T), A.take(T)
        SQ4 = big[:, A.at - T:A.at + 3 * T].rearrange("p (a b) -> p a b", b=T)
        SQ = A.take(SQN * T, T)
        TMP = A.take(1024, T)
        BASE = A.at

        def unscaled(c, gain, ok, *free):
            g = gain[:, c:c + 1]
            h = act.act(XH[:, c, :], H[:, c, :], AF.Copy, ok, c_ready, *free, scale=g)
            l = dve.stt(XL[:, c, :], H[:, c, :], g, XH[:, c, :].bitcast(F32), ALU.mult, ALU.subtract, h, *free)
            return [h, l]

        def scaled_side(gain, rs_name, name, free, last=None, pace=1):
            got = tok[name] = {}
            m = {}
            free = list(free)
            while rs_name not in tok:
                yield
            for c in range(9):
                while c == 8 and last and not tok.get(last):
                    yield
                if c < 8:
                    m[c] = dve.stt(TMP[:, c % 2, :], H[:, c, :], gain[:, c:c + 1], RSB, ALU.mult, ALU.mult,
                                   tok[rs_name], got.get(c - 2))
                if c:
                    got[c - 1] = split_into(GH[:, c - 1, :], GL[:, c - 1, :], TMP[:, (c - 1) % 2, :], m[c - 1], *free,
                                            tok.get(last))
                for _ in range(pace):
                    yield
            tok[name + "_all"] = True

        s_x = [sem(f"x{i}") for i in range(4)]
        x_ok = []
        for i in range(4):
            x_ok += [sp.dma(H[:, 2 * i:2 * i + 2, :], I["xT"][:, 2 * i:2 * i + 2, :], s_x[i])] * 2
            if i < 2:
                st.fetch(i + 1)
        tok["ident"] = sp.dma(ident[:, :], I["ident"], s_ident)

        QN_QS = A.take(2048, T)
        QN, QS = QN_QS[:, 0:4, :], QN_QS[:, 4:8, :]
        KS, KW, KK = A.take(T), A.take(T), A.take(T)
        V = A.take(2 * 384, 384)
        GT = A.take(48, 24)
        SA, SB = A.take(2048, T), A.take(2048, T)
        BT = A.take(4096, T)
        KC2, VC2 = A.take(2 * 258, 258), A.take(2 * 258, 258)
        CX, CV = A.take(480, 30), A.take(480, 30)
        W1K, W1V = A.take(4096, 256), A.take(4096, 256)
        MIS = A.take(1560)
        s_l1 = sem("l1")
        POS = MIS[:, 0:32]
        W2K = MIS[:, 32:288].rearrange("p (a b) -> p a b", b=128)
        W2V = MIS[:, 288:416].rearrange("p (a b) -> p a b", b=64)
        RELB = MIS[0:32, 416:432]
        ONEH = MIS[0:32, 432:816]
        BMASK = MIS[0:16, 816:1200]
        SINK = MIS[:, 1200:1208]
        CM = MIS[:, 1208:1268].rearrange("p (a b) -> p a b", b=30)
        SEL = MIS[0:30, 1268:1396]
        HID = MIS[:, 1396:1516].rearrange("p (a b) -> p a b", b=30)
        KCT = MIS[:, 1516:1548]
        s_bias = sem("bias")
        for a, b in ((RELB, I["relb"]), (ONEH, I["oneh"]), (BMASK, I["bmask"])):
            bias_ok = sp.dma(a, b, s_bias)
        s_w1k, s_w1v = ([sem(f"{x}{j}") for j in range(4)] for x in ("w1k", "w1v"))

        Z = W1K.rearrange("p a b -> p (a b)")
        BDV = Z[:, 0:512].rearrange("p (a b) -> p a b", b=64)
        OA = Z[:, 512:1536].rearrange("p (t a b) -> p t a b", t=2, b=64)
        OB = Z[:, 1536:2560].rearrange("p (t a b) -> p t a b", t=2, b=64)
        TMPO = Z[:, 2560:3072].rearrange("p (a b) -> p a b", b=64)
        VCS = Z[0:30, 3072:3136]
        HTM = Z[0:30, 512:1024]
        PCT = [Z[:, 3136 + 128 * i:3264 + 128 * i] for i in range(2)]
        Z = W1V.rearrange("p a b -> p (a b)")
        NS_ = 6
        S = [A.take(512, T) for i in range(NS_)]
        NP_ = 4
        PTS = [Z[:, 512 * i:512 * i + 512] for i in range(NP_)]
        Z = A.take(512)
        ST = Z[:, 0:128].rearrange("p (t a b) -> p t a b", t=2, b=8)
        NM = Z[:, 128:192].rearrange("p (a b) -> p a b", b=8)
        SUM = Z[:, 192:256].rearrange("p (a b) -> p a b", b=8)
        GS = Z[:, 256:304].rearrange("p (a b) -> p a b", b=24)
        NS = Z[:, 304:312]
        HRS = Z[:, 328:330]
        W8 = Z[:, 312:328].rearrange("p (a b) -> p a b", b=8)
        Z = A.take(256)
        SC = Z.rearrange("p (t a b) -> p t a b", t=2, b=16)
        pad_ok = [dve.memset(SC[:, :, :, 15:16], 0.0), dve.memset(KCT, 0.0)]

        stat = Stat(7, 8, ring=[SQ[:, i, :] for i in range(3)] + [TMP[:, i, :] for i in range(4)])
        X = {}
        for c in range(8):
            X[c] = unscaled(c, COL["mix_pre"], x_ok[c])
            if c == 1:
                st.split(1)
            if c == 3:
                st.split(2)
                st.fetch(4)
                for a, b in ((POS, I["pos"]), (W2K, I["w2k"]), (W2V, I["w2v"]), (SINK, I["sinks"]), (CM, I["cmask"]),
                             (SEL, I["sel"])):
                    l1_ok = sp.dma(a, b, s_l1)
        st.split(3)
        for c in range(8):
            stat.add(H[:, c, :], x_ok[c])

        def bias_side():
            VB = flat(QS)[0:16, 0:384]
            b, free = take_bank(6)
            t = pe.mm(b[0:16, 0:384], RELB, ONEH, True, True, free, bias_ok, signal=True)
            t = dve.tt(VB, b[0:16, 0:384], BMASK, ALU.add, t, bias_ok)
            idle[6] = [t]
            s_w, s_r = sem("toep_w"), sem("toep_r")
            scr = nc.dram_tensor("toeplitz", [16, 16, 384], F32).ap()
            t = sp.dma(scr, VB[:, None, :].broadcast_to([16, 16, 384]), s_w, t)
            tok["vb"] = t
            for a in range(8):
                yield
                src = bass.AP(scr.tensor, 127 - 16 * a, [[383, 16], [6144, 16], [1, 256]])
                r = sp.dma(BT[16 * a:16 * a + 16, :, :], src, s_r, t)
            tok["bt"] = r
            for which, w, src, s in (("w1k", W1K, I["w1k"], s_w1k), ("w1v", W1V, I["w1v"], s_w1v)):
                for j in range(4):
                    yield
                    tok[which, j] = sp.dma(w[:, 4 * j:4 * j + 4, :], src[:, 4 * j:4 * j + 4, :], s[j])
                    yield

        def ev_kc(dst, name):
            def f(ps, t):
                a = dve.tt(dst[0:64, 0, 1:257], ps[0:64, :], RSB[0:64, :], ALU.mult, t, tok["rs1"])
                b = dve.tt(dst[64:128, 1, 0:256], ps[64:128, :], RSB[64:128, :], ALU.mult, t)
                s = sem("sw_" + name)
                sp.dma(dst[64:128, 0, 0:256], dst[0:64, 0, 1:257], s, a)
                d = sp.dma(dst[0:64, 1, 1:257], dst[64:128, 1, 0:256], s, b)
                tok[name] = [b, d]
                return b
            return f

        def ev_scale(dst, name, *after):
            def f(ps, t):
                tok[name] = dve.tt(dst, ps, RSB, ALU.mult, t, [tok[a] for a in after])
                return tok[name]
            return f

        def ev_act(dst, name, func, *after, **kw):
            def f(ps, t):
                tok[name] = act.act(dst, ps, func, t, *after, **kw)
                return tok[name]
            return f

        def compress_side():
            while "vc" not in tok:
                yield
            yield
            for src, dst, col, name in ((KC2, CX, 0, "kc"), (VC2, CV, 16, "vc")):
                v = src[:, :, 1:257].rearrange("p g (n j two) -> p g j n two", j=8, two=2)
                o = dst.rearrange("p j (g n) -> p g j n", n=15)
                for half in range(2):
                    p = POS[:, col + 8 * half:col + 8 * half + 8]
                    for g in range(2):
                        ready = dve.tt(o[:, g, 8 * half:8 * half + 8, :], v[:, g, :, half:half + 15, 0],
                                       p[:, :, None].broadcast_to([128, 8, 15]), ALU.add, tok[name], l1_ok)
                tok["x" + name] = ready
            for _ in range(5):
                yield
            b, free = take_bank(7)
            for i, (w, x, which, ok) in enumerate(((W1K, CX, "w1k", "xkc"), (W1V, CV, "w1v", "xvc"))):
                for j in range(16):
                    while (which, j // 4) not in tok:
                        yield
                    t = pe.mm(b[0:30, T * i:T * i + T], x[:, j, :], w[:, j, :], j == 0, j == 15, free, tok[ok],
                              tok[which, j // 4], signal=j == 15)
                    if j % 2:
                        yield
            tok["w1"] = t
            yield
            t = act.act(HTM, b[0:30, :], AF.Gelu_apprx_tanh, t)
            yield
            yield
            for i in range(4):
                t = pe.tr(b[:, 32 * i:32 * i + 30], HTM[:, 128 * i:128 * i + 128], ident[0:30, 0:30], t, tok["ident"],
                          signal=i == 3)
            yield
            t = act.act(HID, b[:, 0:128].rearrange("p (a b) -> p a b", b=32)[:, :, 0:30], AF.Copy, t)
            yield
            for i in range(2):
                k = pe.mm(b[:, 128:158], W2K[:, i, :], HID[:, i, :], i == 0, i == 1, t, l1_ok, signal=True)
            for i in range(2):
                v = pe.mm(b[0:30, 160:224], HID[:, 2 + i, :], W2V[:, i, :], i == 0, i == 1, signal=True)
            yield
            tok["kct"] = [act.act(KCT[64 * g:64 * g + 64, 16 * g:16 * g + 15], b[64 * g:64 * g + 64,
                                  128 + 15 * g:143 + 15 * g], AF.Copy, k, v, pad_ok) for g in range(2)]
            v = act.act(VCS, b[0:30, 160:224], AF.Copy, v)
            yield
            yield
            tok["ns"] = dve.ts(NS, SINK, -1.0, None, ALU.mult, None, l1_ok)
            v = pe.mm(b[:, 256:320], SEL, VCS, True, True, v, signal=True)
            yield
            t = dve.tt(BDV, b[:, None, 256:320].broadcast_to([128, 8, 64]), BD[:, :, None].broadcast_to([128, 8, 64]),
                       ALU.mult, v, tok["w1"], c_ready)
            tok["bdv"] = t
            idle[7] = [t] + tok["kct"]

        o_ok = [None, None]

        def compressed_side():
            while "bdv" not in tok or "qn3" not in tok:
                yield
            got = []
            for tile in range(2):
                bank, free = take_bank(6 + tile)
                for c in range(4):
                    t = pe.mm(bank[:, 32 * c:32 * c + 32], QN[:, c, 128 * tile:128 * tile + 128], KCT, True, True, free,
                              tok["kct"], tok[f"qn{c}"], signal=c == 3)
                got.append(t)
                yield
            for tile in range(2):
                got[tile] = dve.tt(SC[:, tile, :, 0:15],
                                   banks[6 + tile][:, 0:128].rearrange("p (a b) -> p a b", b=16)[:, :, 0:15],
                                   CM[:, tile:tile + 1, 0:15].broadcast_to([128, 8, 15]), ALU.add, got[tile], l1_ok)
                idle[6 + tile] = [got[tile]]
            x = SC[:, :, :, 0:15]

            def by_head(k):
                return ST[:, :, k, :, None].broadcast_to([128, 2, 8, 15])

            t = dve.reduce(ST[:, :, 0, :], x, ALU.max, got)
            yield
            t = dve.tt(x, x, by_head(0), ALU.subtract, t)
            yield
            t = act.act(x, x, AF.Exp, t, scale=0.125)
            yield
            t = dve.tt(x, x, CM[:, :, None, 15:30].broadcast_to([128, 2, 8, 15]), ALU.mult, t)
            yield
            tok["pc"] = t
            s = dve.reduce(ST[:, :, 1, :], x, ALU.add, t)
            while "gs" not in tok:
                yield
            s = dve.ts(ST[:, :, 1, :], ST[:, :, 1, :], 1e-30, None, ALU.max, None, s)
            yield
            s = dve.recip(ST[:, :, 2, :], ST[:, :, 1, :], s)
            yield
            sc_ok = dve.tt(ST[:, :, 3, :], ST[:, :, 2, :], GS[:, :, 0:8], ALU.mult, s, tok["gs"])
            yield
            done = []
            for tile in range(2):
                b, free = take_bank(6 + tile)
                t = pe.tr(b[:, 0:128], SC[:, tile, :, :].rearrange("p a b -> p (a b)"), ident[:, :], tok["pc"],
                          pad_ok, tok["ident"], free, signal=True)
                done.append(act.act(PCT[tile], b[:, 0:128], AF.Copy, t, tok["w1"]))
            yield
            for tile in range(2):
                b = banks[6 + tile]
                t = pe.mm(b[:, :], PCT[tile], BDV.rearrange("p a b -> p (a b)"), True, True, done[tile], tok["bdv"],
                          signal=True)
                done[tile] = dve.tt(OA[:, tile, :, :], b[:, :].rearrange("p (a b) -> p a b", b=64),
                                    ST[:, tile, 3, :, None].broadcast_to([128, 8, 64]), ALU.mult, t, sc_ok)
                idle[6 + tile] = [done[tile]]
            o_ok[0] = done
            tok["oc"] = True

        steps = [(tile, kind, c) for kinds in ((0, 1), (2,)) for tile in range(2) for kind in kinds for c in range(4)]
        exps, pts, pv, freed = {}, {}, {}, {}

        def geometry(s):
            tile, kind, c = steps[s]
            q, k, v0 = ((QN, KS, 0), (QN, KW, 128), (QS, KK, 256))[kind]
            g = c % 2
            heads = [c // 2 * 4 + 2 * i + g for i in range(2)]
            return tile, kind, c, g, heads, q, k, v0 + 64 * g, 128 * (tile + 1), s // 4

        def a_scores(s):
            tile, kind, c, g, heads, q, k, v, n, run = geometry(s)
            b, free = take_bank(3 + s % 2)
            r = slice(64 * g, 64 * g + 64)
            for i in range(2):
                cc = c // 2 * 2 + i
                t = pe.mm(b[:, T * i:T * i + n], q[r, cc, 128 * tile:128 * tile + 128], k[r, 0:n], True, True, free,
                          tok[("qn", "qn", "qs")[kind] + str(cc)], tok[("ks", "kw", "kk")[kind]], signal=i == 1)
            exps[s] = t

        def a_bias(s):
            tile, kind, c, g, heads, q, k, v, n, run = geometry(s)
            b = banks[3 + s % 2]
            for i, h in enumerate(heads):
                init = NS[:, h:h + 1] if kind == 2 else 3e38
                t = dve.do(lambda e, o=S[s % NS_][:, i, 0:n], i0=b[:, T * i:T * i + n],
                           i1=BT[:, (8 if kind == 2 else 0) + h, T - n:T], init=init, nm=NM[:, run, h:h + 1]:
                           e.tensor_tensor_reduce(o, i0, i1, -0.125, init, ALU.add, ALU.min, nm),
                           [exps[s], tok["bt"], freed.get(s - NS_), tok["ns"] if kind == 2 else None])
            idle[3 + s % 2] = [t]
            exps[s] = t

        def a_exp(s):
            tile, kind, c, g, heads, q, k, v, n, run = geometry(s)
            for i, h in enumerate(heads):
                x = S[s % NS_][:, i, 0:n]
                t = act.act(x, x, AF.Exp, exps[s], scale=-1.0, bias=NM[:, run, h:h + 1], accum_out=SUM[:, run, h:h + 1])
            exps[s] = t

        def a_transpose(s):
            tile, kind, c, g, heads, q, k, v, n, run = geometry(s)
            i = (5, 2)[s % 2]
            b, free = take_bank(i)
            for m in range(2 * (tile + 1)):
                t = pe.tr(b[:, 128 * m:128 * m + 128], S[s % NS_][:, m // (tile + 1), 128 * (m % (tile + 1)):
                                                                 128 * (m % (tile + 1)) + 128],
                          ident[:, :], free, exps[s], tok["ident"], signal=m == 2 * tile + 1)
            freed[s] = t
            pts[s] = t

        def a_evac(s):
            tile = steps[s][0]
            i = (5, 2)[s % 2]
            w = 256 * (tile + 1)
            t = act.act(PTS[s % NP_][:, 0:w], banks[i][:, 0:w], AF.Copy, pts[s], pv.get(s - NP_), tok["w1"])
            idle[i] = [t]
            pts[s] = t

        def a_values(s):
            tile, kind, c, g, heads, q, k, v, n, run = geometry(s)
            nb = tile + 1
            i = 6 + run % 2
            free = None
            if c == 0:
                _, free = take_bank(i)
            for m, h in enumerate(heads):
                for j in range(nb):
                    t = pe.mm(banks[i][:, 64 * h:64 * h + 64], PTS[s % NP_][:, (m * nb + j) * 128:(m * nb + j) * 128 + 128],
                              V[:, j, v:v + 64], j == 0, j == nb - 1, free, pts[s], tok["v"],
                              signal=m == 1 and j == nb - 1)
            pv[s] = t

        def a_finish(s):
            tile, kind, c, g, heads, q, k, v, n, run = geometry(s)
            if c < 3:
                return
            i = 6 + run % 2
            r = ST[:, tile, 4 + kind, :]
            if kind == 2:
                e = dve.tt(W8[:, tile, :], NM[:, run, :], NS, ALU.subtract, exps[s])
                e = act.act(W8[:, tile, :], W8[:, tile, :], AF.Exp, e)
                e = dve.tt(SUM[:, run, :], SUM[:, run, :], W8[:, tile, :], ALU.add, e)
                e = dve.recip(r, SUM[:, run, :], e)
            else:
                e = dve.recip(r, SUM[:, run, :], exps[s])
                e = dve.tt(r, r, GS[:, tile, 8 + 8 * kind:16 + 8 * kind], ALU.mult, e, tok["gs"])
            o = banks[i][:, :].rearrange("p (a b) -> p a b", b=64)
            sc = r[:, :, None].broadcast_to([128, 8, 64])
            if kind == 2:
                o_ok[1] = dve.tt(OB[:, tile, :, :], o, sc, ALU.mult, pv[s], e)
                idle[i] = [o_ok[1]]
            else:
                t = dve.tt(TMPO, o, sc, ALU.mult, pv[s], e, o_ok[0])
                idle[i] = [t]
                o_ok[0] = dve.tt(OA[:, tile, :, :], OA[:, tile, :, :], TMPO, ALU.add, t)
                if kind == 0:
                    return
            later(1, lambda: to_features((OA, OB)[kind // 2], 4 * (kind // 2), tile, o_ok[kind // 2], i))

        up_in = {}

        def to_features(src, chunk0, tile, ok, i):
            b, free = take_bank(i)
            for c in range(4):
                t = pe.tr(b[:, 128 * c:128 * c + 128], src[:, tile, 2 * c:2 * c + 2, :].rearrange("p a b -> p (a b)"),
                          ident[:, :], free, ok, signal=c == 3)
            ps = b[:, :].rearrange("p (a b) -> p a b", b=128)
            ts = slice(128 * tile, 128 * tile + 128)
            r = split_into(GH[:, chunk0:chunk0 + 4, ts], GL[:, chunk0:chunk0 + 4, ts], ps, t)
            idle[i] = list(r)
            for c in range(4):
                up_in.setdefault(chunk0 + c, []).extend(r)

        turn_list = []
        s = 0
        while s < len(steps):
            m = 2 if steps[s][0] == 0 else 1
            turn_list.append(list(range(s, s + m)))
            s += m
        stages = [[a_scores], [a_bias], [a_exp], [a_transpose], [a_evac], [a_values], [a_finish]]
        spread = ((4, 5), (1,), (2, 3), (6, 0))

        def attention_side():
            while "qn3" not in tok or "kw" not in tok or "bt" not in tok:
                yield
            n = len(turn_list)
            for turn in range(n + len(stages) - 1):
                while (turn >= 3 and "v" not in tok) or (turn >= 5 and "oc" not in tok) or (turn >= 12 and "qs3" not in tok):
                    yield
                for ks in spread:
                    for k in ks:
                        if 0 <= turn - k < n:
                            for s in turn_list[turn - k]:
                                stages[k][0](s)
                    yield
            tok["attn"] = True

        mains[:] = [[0, 1, 2, 3], 0]
        turns[0] = 4
        sides.append(bias_side())
        tiles([ev_kc(KC2, "kc"), ev_kc(VC2, "vc"), ev_scale(KS, "ks", "rs1"), ev_scale(KW, "kw", "rs1")]
              + [ev_scale(QN[:, c, :], f"qn{c}", "rs1") for c in range(2)], xs, X, stat=stat, name="rs1")
        sides.append(compress_side())
        sides.append(compressed_side())
        for c in range(2, 4):
            tile(ev_scale(QN[:, c, :], f"qn{c}", "rs1"), xs, X)
        sides.append(attention_side())

        st.share = 448
        mains[:] = [[0, 1], 1]
        i0, i1 = 2, 0
        (b0, f0), (b1, f1) = take_bank(i0), take_bank(i1)
        half_rs = dve.ts(HRS, RS2[:, 2:4], 0.5, None, ALU.mult, None, stat.t)
        for u in range(4):
            def parts(u=u):
                v, wh, wl, h_ok, l_ok = st.take()
                for kk in range(2):
                    k = 2 * u + kk
                    w = slice(512 * kk, 512 * kk + 512)
                    for b, f, ts in ((b0, f0, slice(0, 128)), (b1, f1, slice(128, 256))):
                        pe.mm(b[:, :], XH[:, k, ts], wh[:, w], k == 0, False, f if u == 0 else None, h_ok, X[k])
                        pe.mm(b[:, :], XL[:, k, ts], wh[:, w], False, False)
                        t = pe.mm(b[:, :], XH[:, k, ts], wl[:, w], False, k == 7, l_ok, signal=kk == 1)
                        yield
                st.done[v] = tok["tm"] = t

            def ev(u=u):
                if u < 3:
                    return
                r = []
                for tile, (b, i) in enumerate(((b0, i0), (b1, i1))):
                    r += [act.act(V[:, tile, :], b[:, 0:384], AF.Copy, tok["tm"], stat.t, scale=RS2[:, 2 + tile:3 + tile]),
                          act.act(GT[:, tile, :], b[:, 384:408], AF.Tanh, tok["tm"], half_rs,
                                  scale=HRS[:, tile:tile + 1])]
                    idle[i] = r[-2:]
                tok["gs"] = dve.ts(GS, GT, 1.0, 0.5, ALU.add, ALU.mult, r)
                tok["v"] = r
            unit(parts(), ev)

        def ev_gate(dst, name):
            def f(ps, t):
                r = dve.tt(dst, ps, RSB, ALU.mult, t)

                def tanh():
                    tok[name] = act.act(dst, dst, AF.Tanh, r, scale=0.5)
                later(1, tanh)
                return r
            return f

        tile(ev_scale(KK, "kk", "rs1"), xs, X)
        for c in range(4):
            tile(ev_scale(QS[:, c, :], f"qs{c}", "rs1", "vb"), xs, X)
        for c in range(8):
            tile(ev_gate(SA[:, c, :], f"ga{c}"), xs, X)
        for c in range(8):
            tile(ev_gate(SB[:, c, :], f"gb{c}"), xs, X)
        flush()
        tok["x_read"] = st.done[st.v]

        Y = QN_QS
        YB = [flat(TMP[:, 2 * n:2 * n + 2, :]) for n in range(2)]
        y_ok, merged = {}, {}

        def up_tile(i, chunk0, evac):
            bi = main_bank()
            b, free = take_bank(bi)
            end = {}

            def ev():
                idle[bi] = [evac(i, b, end["t"])]
            unit(products([b[:, 0:T], b[:, T:2 * T]], free, gs, up_in, nk=4, k0=chunk0, end=end), ev)

        def up_a(i, b, t):
            g = flat(SA[:, 2 * i:2 * i + 2, :])
            merged[i] = dve.stt(g, g, 1.0, b[:, :], ALU.add, ALU.mult, t, [tok[f"ga{c}"] for c in (2 * i, 2 * i + 1)])
            return merged[i]

        def up_b(i, b, t):
            g = flat(SB[:, 2 * i:2 * i + 2, :])
            a = dve.stt(YB[i % 2], g, 1.0, b[:, :], ALU.add, ALU.mult, t,
                        [tok[f"gb{c}"] for c in (2 * i, 2 * i + 1)], merged.get(("b", i - 2)))
            src = flat(SA[:, 2 * i:2 * i + 2, :])
            s = merged["b", i] = dve.tt(src, src, YB[i % 2], ALU.add, a, merged[i])

            def parts_of_y():
                h = act.act(flat(XH[:, 2 * i:2 * i + 2, :]), src, AF.Copy, s, tok["x_read"], scale=0.5)
                l = dve.stt(flat(XL[:, 2 * i:2 * i + 2, :]), src, 0.5,
                            flat(XH[:, 2 * i:2 * i + 2, :]).bitcast(F32), ALU.mult, ALU.subtract, h, tok["x_read"])
                y_ok[2 * i] = y_ok[2 * i + 1] = [h, l]
            later(1, parts_of_y)
            return a

        for i in range(4):
            up_tile(i, 0, up_a)
        st.share = 256
        flush()
        settle()
        while soon:
            run_soon()
        turns[0] = 1
        mains[:] = [[0, 1, 2], 0]
        for i in range(4):
            up_tile(i, 4, up_b)
        st.share = 0
        g_free = st.done[st.v]
        flush()
        run_soon()
        stat = Stat(7, 8)

        def ev_y(c):
            def f(ps, t):
                stat.add(ps, t)
                return act.act(Y[:, c, :], ps, AF.Copy, t)
            return f

        y_end = {}

        def turn(y, gain, gain_next, x_free, soon_=True, scale=None):
            nonlocal stat
            st.ahead = LS
            stat.sums(scale)
            st.split(st.used + RW)
            rs, t = stat.spread()
            keep_warm(5, 6)
            old, stat = stat, Stat(6, 8, stat.used, lane=dve)
            m, a, got = {}, {}, {}
            for c in range(10):
                if c < 8:
                    m[c] = dve.stt(y[:, c, :], y[:, c, :], gain[:, c:c + 1], rs, ALU.mult, ALU.mult, t,
                                   y_end.get(c // 2))
                    a[c] = (pool if c > 1 else dve).tt(H[:, c, :], H[:, c, :], y[:, c, :], ALU.add, m[c])
                if c > 1:
                    got[c - 2] = unscaled(c - 2, gain_next, a[c - 2], x_free)
            idle[old.bank] = [m[7]]

            def squares():
                for c in range(8):
                    stat.add(H[:, c, :], a[c])
                    yield
                tok["squares"] = True
            if soon_:
                list(squares())
            else:
                sides.append(squares())
            return got, list(a.values())

        tiles([ev_y(c) for c in range(8)], xs, y_ok)
        flush()
        X, h_ok = turn(Y, COL["mix_post"], COL["mlp_pre"], st.done[st.v], soon_=False)
        A = Arena(BASE, 32768)
        QKV = A.take(24 * T, T)
        Q, K, VF = QKV[:, 0:8, :], QKV[:, 8:16, :], QKV[:, 16:24, :]
        SZ = A.take(2048, T)
        GA, GB = A.take(2048, T), A.take(2048, T)
        XA = A.take(1024, T)
        KB = A.take(2048, T)
        DC = A.take(2048, 128)
        LT = A.take(2048, 128)
        TT = A.take(2048, 128)
        VB = A.take(2048, 128)
        KD = A.take(1024, 128)
        CT = [A.take(T) for _ in range(3)]
        SM = Arena(A.at, 32768)
        TRI, SUF, NEGM = SM.take(128), SM.take(128), SM.take(128)
        LM = SM.take(384, 128)
        BAW, BAWH, BAWL = SM.take(128), GH[:, 7, 0:128], GL[:, 7, 0:128]
        PW = SM.take(512, 128)
        ALOG, DTB = SM.take(8), SM.take(8)
        B2, G2, E2, U2, V2, NGC, EGC, ESF, RQ, BRK, SS, BE = (SM.take(16, 8) for _ in range(12))
        W2 = SM.take(32, 16)
        INV = SM.take(68, 17)
        R16 = SM.take(64).rearrange("p (g k c) -> p g k c", g=4, k=2)
        T0 = flat(KB).rearrange("p (a b) -> p a b", b=128)
        VN = flat(VF).rearrange("p (a b) -> p a b", b=128)
        BAT = CT[2][0:16, :]
        s_l2 = sem("l2")
        for a, b in ((TRI, I["tri"]), (SUF, I["suf"]), (NEGM, I["negm"]), (LM, I["lmask"]), (BAW, I["baw"]),
                     (ALOG, I["alog"]), (DTB, I["dtb"]), (PW, I["poolw"]), (INV, I["inv"])):
            l2_ok = sp.dma(a, b, s_l2, merged["b", 3], [t for v in y_ok.values() for t in v])

        hid_ok, hid_free = {}, {}
        HT = [TMP[:, i, :] for i in range(3)]
        ht_free = [None] * 3

        def ev_hidden(n):
            def f(ps, t):
                ht = HT[n % 3]
                e = act.act(ht, ps, AF.Relu, t, ht_free[n % 3], merged["b", 3])
                r = dve.tt(ht, ht, ht, ALU.mult, e)
                later(1, lambda: rest(n, ht, r))
                return e
            return f

        def rest(n, ht, r):
            free = [hid_free.get(n - 8), g_free]
            a = act.act(GH[:, n % 8, :], ht, AF.Copy, r, *free)
            b = dve.tt(GL[:, n % 8, :], ht, GH[:, n % 8, :].bitcast(F32), ALU.subtract, a, *free)
            ht_free[n % 3] = b
            hid_ok[n % 8] = [a, b]

        f_end = [{} for _ in range(4)]
        f_stat = []

        def evac_f(i):
            b = banks[3 + i]
            s = [f_stat[0].add(b[:, T * c:T * c + T], f_end[i]["t"]) for c in range(2)]
            y_end[i] = dve.tt(Y[:, 2 * i:2 * i + 2, :], b[:, :].rearrange("p (a b) -> p a b", b=T),
                              RSA[:, None, :].broadcast_to([128, 2, T]), ALU.mult, s, tok["rs2"])
            idle[3 + i] = [y_end[i]]

        def mlp_out(q):
            for i in range(4):
                b, free = take_bank(3 + i) if q == 0 else (banks[3 + i], None)
                st.ahead = LS - 1 if (q, i) == (7, 3) else LS

                def ev(q=q, i=i):
                    for k in range(4):
                        hid_free[4 * q + k] = f_end[i]["t"]
                    if q == 7:
                        evac_f(i)
                unit(products([b[:, 0:T], b[:, T:2 * T]], free, gs, hid_ok, nk=4, k0=4 * (q % 2), first=q == 0,
                              last=q == 7, end=f_end[i]), ev)

        tiles([ev_hidden(n) for n in range(4)], xs, X)
        for i in range(4):
            tile(ev_hidden(4 + i), xs, X)
        settle("squares")

        def rs2_side():
            stat.sums()
            yield
            yield
            tok["rs2"] = dve.tt(RSA, RSB, RSB, ALU.mult, stat.into(RSB))
            r = dve.tt(RS4, RS2[:, 2:4], RS2[:, 2:4], ALU.mult, stat.t)
            r = dve.tt(RS4, RS4, RS4, ALU.mult, r)
            tok["rs2_4"] = dve.ts(RS4, RS4, 1.0 / D, None, ALU.mult, None, r)
        sides.append(rs2_side())
        for q in range(1, 8):
            if q > 1:
                tiles([ev_hidden(4 * q + i) for i in range(4)], xs, X, pair=False)
            if q == 7:
                x_free = st.done[st.v]
            mlp_out(q - 1)
        flush()
        run_soon()
        f_stat.append(Stat(7, 8, stat.used, ht_free, ring=[SQ[:, i, :] for i in range(3)] + [TMP[:, i, :] for i in range(4)],
                           alone=2))
        stat = f_stat[0]
        mlp_out(7)
        g_free = st.done[st.v]
        flush()
        X, h_ok = turn(Y, COL["mlp_post"], COL["mix2"], x_free, scale=RS4)
        g_read2 = g_free
        side_at = [0]

        def side_bank():
            n = 3 + side_at[0] % 4
            side_at[0] += 1
            b, free = take_bank(n)
            return n, b, free

        def quads(lhs, rhs, *after, tr=False):
            n, b, free = side_bank()
            for j in range(4):
                if tr:
                    t = pe.tr(quad(b)[:, j, :], lhs(j), ident[:, :], free, *after, signal=j == 3)
                else:
                    t = pe.mm(quad(b)[:, j, :], lhs(j), rhs(j), True, True, free, *after, signal=j == 3)
            return n, b, t

        def ev_xa(c):
            def f(ps, t):
                tok[f"xa{c}"] = dve.tt(XA[:, c, :], ps, RSB, ALU.mult, t, tok["rs3"])
                return tok[f"xa{c}"]
            return f

        turns[0] = 4
        mains[:] = [[0, 1, 2, 3], 0]
        sides.append(scaled_side(COL["mix2"], "rs3", "xs3", [g_read2], last="ba", pace=3))
        st.share = 320
        tiles([ev_xa(c) for c in range(2)], xs, X)
        tile(ev_xa(2), xs, X, hold=True)
        baw = split_into(BAWH, BAWL, BAW, l2_ok, g_read2)
        tile(ev_xa(3), xs, X, **scaled_by(stat, "rs3"))

        b7, f7 = take_bank(7)

        def beta_parts():
            for k in range(8):
                w = slice(16 * k, 16 * k + 16)
                pe.mm(b7[0:16, 0:T], BAWH[:, w], XH[:, k, :], k == 0, False, f7, X[k], baw)
                pe.mm(b7[0:16, 0:T], BAWH[:, w], XL[:, k, :], False, False)
                tok["ba"] = pe.mm(b7[0:16, 0:T], BAWL[:, w], XH[:, k, :], False, k == 7, signal=k == 7)
                if k % 2:
                    yield

        def both(x):
            return x[:, None, :].broadcast_to([128, 2, 8])

        def gates_side():
            t = dve.tt(BAT, b7[0:16, 0:T], RSB[0:16, :], ALU.mult, tok["ba"], tok["rs3"])
            for _ in range(3):
                yield
            for tile in range(2):
                t = pe.tr(b7[:, T + 16 * tile:T + 16 * tile + 16], BAT[:, 128 * tile:128 * tile + 128],
                          ident[0:16, 0:16], t, signal=True)
            yield
            ba = b7[:, T:T + 32].rearrange("p (a b) -> p a b", b=16)
            e = act.act(B2, ba[:, :, 0:8], AF.Exp, t, scale=-1.0)
            c = dve.tt(G2, ba[:, :, 8:16], both(DTB), ALU.add, t, l2_ok, e)
            e = dve.ts(B2, B2, 1.0, None, ALU.add, None, e)
            tok["beta"] = dve.recip(B2, B2, e)
            a = act.act(ALOG, ALOG, AF.Exp, l2_ok)
            a = dve.ts(ALOG, ALOG, -1.0, None, ALU.mult, None, a)
            u = act.act(U2, G2, AF.Abs, c)
            u = act.act(E2, U2, AF.Exp, u, scale=-1.0)
            yield
            st.share = 0
            r = dve.ts(U2, E2, 2.0, None, ALU.add, None, u)
            r = dve.recip(U2, U2, r)
            z = pool.tt(E2, E2, U2, ALU.mult, r)
            r = pool.tt(U2, E2, E2, ALU.mult, z)
            v = pool.tt(V2, U2, U2, ALU.mult, r)
            g = pool.ts(G2, G2, 0.0, None, ALU.max, None, u)
            vv = V2.rearrange("p a b -> p (a b)")[:, None, :].broadcast_to([128, 2, 16])
            for k in (4, 3, 2, 1, 0):
                ck = COL["atanh"][:, 2 * k:2 * k + 2, None].broadcast_to([128, 2, 16])
                if k == 4:
                    w = pool.tt(W2, vv, ck, ALU.mult, v)
                else:
                    w = pool.tt(W2, W2, ck, ALU.add, w)
                    if k:
                        w = pool.tt(W2, W2, vv, ALU.mult, w)
            e, o = (W2[:, n, :].rearrange("p (a b) -> p a b", b=8) for n in range(2))
            w = pool.tt(o, o, U2, ALU.mult, w)
            w = pool.tt(e, e, o, ALU.add, w)
            w = pool.tt(e, e, E2, ALU.mult, w)
            g = pool.tt(G2, G2, e, ALU.add, w, g)
            g = pool.tt(G2, G2, both(ALOG), ALU.mult, g, a)
            tok["g"] = g
            for k in range(13):
                if k == 4:
                    st.share = 320
                yield
            for tile in range(2):
                pe.mm(b7[:, 8 * tile:8 * tile + 8], TRI, G2[:, tile, :], True, True, g)
                d = pe.mm(b7[:, 16 + 8 * tile:24 + 8 * tile], SUF, G2[:, tile, :], True, True, signal=True)
            yield
            gc = b7[:, 0:16].rearrange("p (a b) -> p a b", b=8)
            sf = b7[:, 16:32].rearrange("p (a b) -> p a b", b=8)
            n = dve.ts(NGC, gc, -1.0, None, ALU.mult, None, d)
            x = act.act(EGC, gc, AF.Exp, n)
            y = act.act(ESF, sf, AF.Exp)
            tok["be"] = dve.tt(BE, B2, EGC, ALU.mult, x, tok["beta"])
            tok["gc"] = [n, x, y]
            idle[7] = [n, y]
            yield
            for i in range(6):
                if i < 4:
                    tok[f"dm{i}"] = quads(lambda j: NGC[:, j % 2, 2 * i + j // 2:2 * i + j // 2 + 1].broadcast_to([128, 128]),
                                          None, tok["gc"], tr=True)
                if 0 < i < 5:
                    n, b, t = tok[f"dm{i - 1}"]
                    t = dve.tt(DC[:, 4 * i - 4:4 * i, :], quad(b), NEGM[:, None, :].broadcast_to([128, 4, 128]), ALU.subtract, t)
                    idle[n] = [t]
                    tok[f"dm{i - 1}"] = t
                if i > 1:
                    k = i - 2
                    for j in range(4):
                        h, tile = 2 * k + j // 2, j % 2
                        d = DC[:, 4 * k + j, :]
                        e = act.act(d, d, AF.Exp, tok[f"dm{k}"], tok["gc"], scale=-1.0, bias=NGC[:, tile, h:h + 1])
                    tok[f"dc{k}"] = e
                yield

        def ev_conv(u):
            def f(ps, t):
                r = u % 3
                w = COL["conv"][:, 4 * u:4 * u + 4]
                c = CT[seq[u] % 3]
                t = act.act(c, ps, AF.Copy, t, tok.get(f"ct{seq[u] % 3}"), scale=w[:, 3:4])
                for j, n in ((2, 1), (1, 2), (0, 3)):
                    t = dve.stt(c[:, n:T], ps[:, 0:T - n], w[:, j:j + 1], c[:, n:T], ALU.mult, ALU.add, t)
                later(1, lambda: conv_silu(u, c, t))
                return t
            return f

        sums_read = {}

        def conv_silu(u, c, t):
            a = act.act(QKV[:, u, :], c, AF.Silu, t)
            tok[f"ct{seq[u] % 3}"] = tok[f"c{u}"] = a
            if u < 16:
                n = (1 - u // 8) * 2 + u % 8 // 4
                tok[f"s{u}"] = act.act(SQ4[:, u % 4, :], QKV[:, u, :], AF.Square, a, tok["rs3"],
                                       sums_read[n - 1] if n else None)

        order = [8 + h for h in range(8)] + [u for h in range(8) for u in (h, 16 + h, 24 + h)]
        seq_all = {u: n for n, u in enumerate(order)}
        seq = {u: n for n, u in enumerate([u for u in order if u < 24])}

        agenda = {}

        def at(n, fn):
            agenda.setdefault(n, []).append(fn)

        def delta_side():
            for n in range(max(agenda) + 1):
                for fn in agenda.get(n, ()):
                    fn()
                yield
            tok["delta"] = True

        def step(n, mm, evac, lag=1):
            got = {}

            def first():
                got["x"] = mm()

            def second():
                k, b, t = got["x"]
                idle[k] = evac(b, t)
            at(n, first)
            at(n + lag, second)

        half = lambda tile: slice(128 * tile, 128 * tile + 128)

        def four_sums(n):
            k, b, free = side_bank()
            for h in range(4):
                for tile in range(2):
                    t = pe.mm(b[:, 4 * tile + h:4 * tile + h + 1], SQ4[:, h, half(tile)], ones[:, 0:1], True, True,
                              free, tok[f"s{(8, 0)[n // 2] + 4 * (n % 2) + h}"], signal=tile == 1)
            sums_read[n] = t
            return k, b, t

        def four_norms(n, b, t):
            s = R16[:, n, 0, :]
            a = dve.ts(s, b[:, 0:8], EPS_, None, ALU.add, None, t)
            r = R16[:, n, 1, :]
            p = pool.tt(r, s, MHALF.broadcast_to([128, 8]), ALU.pow, a, c_ready)
            tok[f"r{n}"] = p
            return [a]

        def key_scales(n):
            hs = slice(4 * n, 4 * n + 4)
            p = tok[f"r{n}"]
            r = R16[:, n, 1, :].rearrange("p (t h) -> p t h", t=2)
            tok[f"brk{n}"] = dve.tt(BRK[:, :, hs], B2[:, :, hs], r, ALU.mult, p, tok["beta"])
            tok[f"esf{n}"] = dve.tt(ESF[:, :, hs], ESF[:, :, hs], r, ALU.mult, p, tok["gc"])
            tok[f"bek{n}"] = dve.tt(BE[:, :, hs], BE[:, :, hs], r, ALU.mult, p, tok["be"])
            for i in (2 * n, 2 * n + 1):
                rk = R16[:, n, 1, :].rearrange("p (t h) -> p h t", t=2)[:, i % 2 * 2:i % 2 * 2 + 2, :, None]
                d = DC[:, 4 * i:4 * i + 4, :].rearrange("p (h t) e -> p h t e", t=2)
                tok[f"dk{i}"] = pool.tt(d, d, rk.broadcast_to([128, 2, 2, 128]), ALU.mult, tok[f"dc{i}"], p)

        def query_scales(n):
            hs = slice(4 * n, 4 * n + 4)
            r = R16[:, 2 + n, 1, :].rearrange("p (t h) -> p t h", t=2)
            tok[f"rq{n}"] = dve.ts(RQ[:, :, hs], r, 128 ** -0.5, None, ALU.mult, None, tok[f"r{2 + n}"])

        def kb_mm(i):
            return quads(lambda j: BRK[:, j % 2, 2 * i + j // 2:2 * i + j // 2 + 1].broadcast_to([128, 128]), None,
                         tok[f"brk{i // 2}"], tr=True)

        def kb_evac(i, b, t):
            k = slice(2 * i, 2 * i + 2)
            tok[f"kb{i}"] = dve.tt(KB[:, k, :], K[:, k, :], b[:, :].rearrange("p (a b) -> p a b", b=T), ALU.mult, t,
                                   [tok[f"c{8 + h}"] for h in (2 * i, 2 * i + 1)])
            return [tok[f"kb{i}"]]

        def kk_mm(i):
            return quads(lambda j: K[:, 2 * i + j // 2, half(j % 2)], lambda j: KB[:, 2 * i + j // 2, half(j % 2)],
                         tok[f"kb{i}"])

        def kk_evac(i, b, t):
            tok[f"lt{i}"] = dve.tt(LT[:, 4 * i:4 * i + 4, :], quad(b), DC[:, 4 * i:4 * i + 4, :], ALU.mult, t,
                                   tok[f"dk{i}"])
            return [tok[f"lt{i}"]]

        def kq_mm(i):
            return quads(lambda j: K[:, 2 * i + j // 2, half(j % 2)], lambda j: Q[:, 2 * i + j // 2, half(j % 2)],
                         [tok[f"c{h}"] for h in (2 * i, 2 * i + 1)])

        def kq_evac(i, b, t):
            d = DC[:, 4 * i:4 * i + 4, :]
            tok[f"at{i}"] = dve.tt(d, quad(b), d, ALU.mult, t, tok[f"lt{i}"])
            return [tok[f"at{i}"]]

        def v_mm(i):
            n, b, t = quads(lambda j: VF[:, 2 * i + j // 2, half(j % 2)], None,
                            [tok[f"c{16 + h}"] for h in (2 * i, 2 * i + 1)], tr=True)
            tok[f"vr{i}"] = t
            return n, b, t

        def v_evac(i, b, t):
            beta = B2[:, :, 2 * i:2 * i + 2].rearrange("p t h -> p h t")[:, :, :, None].broadcast_to([128, 2, 2, 128])
            tok[f"vb{i}"] = dve.tt(VB[:, 4 * i:4 * i + 4, :].rearrange("p (h t) e -> p h t e", t=2),
                                   quad(b).rearrange("p (h t) e -> p h t e", t=2), beta, ALU.mult, t, tok["beta"],
                                   [tok[f"y{k}"] for k in range(4)])
            return [tok[f"vb{i}"]]

        def kd_mm(i):
            return quads(lambda j: K[:, 4 * i + j, 0:128], None, tr=True)

        def kd_evac(i, b, t):
            tok[f"kd{i}"] = dve.tt(KD[:, 4 * i:4 * i + 4, :], quad(b),
                                   ESF[:, 0, 4 * i:4 * i + 4, None].broadcast_to([128, 4, 128]), ALU.mult, t,
                                   tok[f"esf{i}"])
            return [tok[f"kd{i}"]]

        for i in range(2):
            n = 21 + 16 * i
            step(n, lambda i=i: four_sums(i), lambda b, t, i=i: four_norms(i, b, t), lag=2)
            at(n + 6, lambda i=i: key_scales(i))
            for k in (2 * i, 2 * i + 1):
                step(n + 8 + k % 2, lambda i=k: kb_mm(i), lambda b, t, i=k: kb_evac(i, b, t))
                step(n + 12 + k % 2, lambda i=k: kk_mm(i), lambda b, t, i=k: kk_evac(i, b, t))
            step(n + 10, lambda i=i: kd_mm(i), lambda b, t, i=i: kd_evac(i, b, t))
        n += 15
        for i in range(2):
            q3 = 4 * seq_all[4 * i + 3] + 8
            step(q3 + 1, lambda i=i: four_sums(2 + i), lambda b, t, i=i: four_norms(2 + i, b, t), lag=2)
        for i in range(4):
            q = 4 * seq_all[2 * i + 1] + 8
            step(q + 2, lambda i=i: kq_mm(i), lambda b, t, i=i: kq_evac(i, b, t))

        s_d1, s_d2, s_d3, s_d4 = (sem(f"diag{i}") for i in range(4))
        scr1 = nc.dram_tensor("diag_in", [16, 8, 16, 16], F32).ap()
        scr2 = nc.dram_tensor("diag_out", [2, 16, 8, 16, 16], F32).ap()
        BLF, BIF, BOF = (GB[:, i, :] for i in range(3))
        BL = BLF.rearrange("p (a b) -> p a b", b=16)
        BI = BIF.rearrange("p (a b) -> p a b", b=16)
        C2 = [TMP[:, i, :].rearrange("p (a b) -> p a b", b=16) for i in range(2)]

        def diag_out():
            lt_ok = [tok[f"lt{i}"] for i in range(4)]
            for i in range(8):
                p = slice(16 * i, 16 * i + 16)
                t = sp.dma(scr1[:, i, :, :].rearrange("a j i -> j a i"), LT[p, :, p], s_d1, lt_ok)
            tok["d1"] = t

        def substitute():
            bl = pool.dma(BLF, scr1.rearrange("a b j i -> (a b) (j i)"), s_d2, tok["d1"])
            m = pool.memset(BIF, 0.0)
            m = pool.memset(BIF[:, 0:256:17], 1.0, m)
            for j in range(15):
                k = 15 - j
                o = BOF[:, 0:k * (j + 1)].rearrange("p (a b) -> p a b", b=j + 1)
                p = pool.tt(o, BL[:, j, j + 1:16, None].broadcast_to([128, k, j + 1]),
                            BI[:, j:j + 1, 0:j + 1].broadcast_to([128, k, j + 1]), ALU.mult, bl, m)
                x = BI[:, j + 1:16, 0:j + 1]
                m = pool.tt(x, x, o, ALU.subtract, p)
            r = pool.copy(BL, BI.rearrange("p i c -> p c i"), m)
            w = pool.dma(scr2[0].rearrange("a b i c -> (a b) (i c)"), BIF, s_d3, m)
            v = pool.dma(scr2[1].rearrange("a b i c -> (a b) (i c)"), BLF, s_d3, r)
            tok["inverted"] = [r, v]
            for k in range(2):
                tok["blocks"] = pool.dma(C2[k], scr2[k].rearrange("a b i c -> (b i) a c"), s_d4, v, list(G.values()))

        def expand(i):
            for k, dst in ((0, T0), (1, TT)):
                o = dst[:, 4 * i:4 * i + 4, :].rearrange("p a (b c) -> p a b c", c=16)
                t = dve.tt(o, C2[k][:, 4 * i:4 * i + 4, None, :].broadcast_to([128, 4, 8, 16]),
                           BD[:, None, :, None].broadcast_to([128, 4, 8, 16]), ALU.mult, tok["blocks"],
                           [tok[f"lt{x}"] for x in range(4)])
            tok[f"t{i}"] = t

        at(n, diag_out)
        for i in range(4):
            at(n + 1, lambda i=i: mask(0, i))
        at(n + 1, substitute)
        n += 47

        def mask(level, i):
            s4 = slice(4 * i, 4 * i + 4)
            tok[f"m{i}"] = pool.tt(VB[:, s4, :], LT[:, s4, :], LM[:, level:level + 1, :].broadcast_to([128, 4, 128]),
                                   ALU.mult, tok.get(f"y{i}"), tok[f"lt{i}"])

        def y_mm(level, i):
            n, b, t = quads(lambda j: VB[:, 4 * i + j, :], lambda j: T0[:, 4 * i + j, :], tok[f"m{i}"], tok[f"t{i}"])
            tok[f"y{i}"] = t
            if level < 2:
                mask(level + 1, i)
            return n, b, t

        YS = flat(GB).rearrange("p (a b) -> p a b", b=128)

        def y_evac(i, b, t):
            tok[f"ye{i}"] = act.act(YS[:, 4 * i:4 * i + 4, :], quad(b), AF.Copy, t, tok.get(f"zr{i}"), tok["inverted"])
            return [tok[f"ye{i}"]]

        def z_mm(i, which):
            if which == 0:
                return quads(lambda j: TT[:, 4 * i + j, :], lambda j: YS[:, 4 * i + j, :], tok[f"ye{i}"], tok[f"t{i}"])
            n, b, t = quads(lambda j: YS[:, 4 * i + j, :], lambda j: TT[:, 4 * i + j, :], tok[f"ye{i}"], tok[f"t{i}"])
            tok[f"zr{i}"] = t
            return n, b, t

        def z_evac(i, which, b, t):
            x = (T0, TT)[which][:, 4 * i:4 * i + 4, :]
            r = dve.tt(x, x, quad(b), ALU.subtract, t, tok[f"zr{i}"])
            tok[f"t{i}"] = r
            return [r]

        for i in range(4):
            at(n + 2 * i, lambda i=i: expand(i))
        n += 5
        for level in range(3):
            for i in range(4):
                step(n + i, lambda i=i, level=level: y_mm(level, i), lambda b, t, i=i: y_evac(i, b, t))
            n += 4
            w = (0, 1) if level < 2 else (1,)
            for i in range(4):
                for k, which in enumerate(w):
                    step(n + len(w) * i + k, lambda i=i, which=which: z_mm(i, which),
                         lambda b, t, i=i, which=which: z_evac(i, which, b, t), lag=len(w) - k)
            n += 4 * len(w)

        hc = lambda h, tile: 2 * h + tile
        OR = LT
        og_ok = {}

        def rows(x, i, tile):
            return x[:, 8 * i + tile:8 * i + 8:2, :]

        def all_t(i):
            return [tok[f"t{2 * i}"], tok[f"t{2 * i + 1}"]]

        def r_v0(i):
            return quads(lambda j: TT[:, hc(4 * i + j, 0), :], lambda j: VB[:, hc(4 * i + j, 0), :], all_t(i),
                         tok[f"vb{2 * i}"], tok[f"vb{2 * i + 1}"])

        def r_v0e(i, b, t):
            tok[f"v0{i}"] = act.act(rows(VN, i, 0), quad(b), AF.Copy, t, tok[f"vr{2 * i}"], tok[f"vr{2 * i + 1}"])
            return [tok[f"v0{i}"]]

        def r_s(i):
            return quads(lambda j: KD[:, 4 * i + j, :], lambda j: VN[:, hc(4 * i + j, 0), :], tok[f"v0{i}"],
                         tok[f"kd{i}"])

        def r_se(i, b, t):
            tok[f"st{i}"] = act.act(T0[:, 4 * i:4 * i + 4, :], quad(b), AF.Copy, t, [tok[f"y{k}"] for k in range(4)],
                                    [tok[f"t{k}"] for k in range(4)])
            return [tok[f"st{i}"]]

        def r_o0(i):
            return quads(lambda j: DC[:, hc(4 * i + j, 0), :], lambda j: VN[:, hc(4 * i + j, 0), :],
                         tok[f"at{2 * i}"], tok[f"at{2 * i + 1}"])

        def r_o0e(i, b, t):
            tok[f"o0{i}"] = act.act(rows(OR, i, 0), quad(b), AF.Copy, t, tok[f"m{2 * i}"], tok[f"m{2 * i + 1}"])
            return [tok[f"o0{i}"]]

        def r_w(i):
            return quads(lambda j: K[:, 4 * i + j, 128:256], lambda j: T0[:, 4 * i + j, :], tok[f"st{i}"])

        def r_we(i, b, t):
            tmp = flat(TMP[:, 2 * i:2 * i + 2, :]).rearrange("p (a b) -> p a b", b=128)
            r = dve.tt(tmp, quad(b), BE[:, 1, 4 * i:4 * i + 4, None].broadcast_to([128, 4, 128]), ALU.mult, t,
                       tok[f"bek{i}"], tok["pooled"] if i else None)
            tok[f"vb{i}"] = dve.tt(rows(VB, i, 1), rows(VB, i, 1), tmp, ALU.subtract, r)
            return [r]

        def r_q(i):
            return quads(lambda j: Q[:, 4 * i + j, 128:256], lambda j: T0[:, 4 * i + j, :])

        def r_qe(i, b, t):
            tok[f"o1{i}"] = dve.tt(rows(OR, i, 1), quad(b), EGC[:, 1, 4 * i:4 * i + 4, None].broadcast_to([128, 4, 128]),
                                   ALU.mult, t, tok["gc"], tok[f"m{2 * i}"], tok[f"m{2 * i + 1}"])
            return [tok[f"o1{i}"]]

        def r_v1(i):
            return quads(lambda j: TT[:, hc(4 * i + j, 1), :], lambda j: VB[:, hc(4 * i + j, 1), :], tok[f"vb{i}"],
                         all_t(i))

        def r_v1e(i, b, t):
            tok[f"v1{i}"] = act.act(rows(VN, i, 1), quad(b), AF.Copy, t, tok[f"vr{2 * i}"], tok[f"vr{2 * i + 1}"])
            return [tok[f"v1{i}"]]

        def r_o1(i):
            return quads(lambda j: DC[:, hc(4 * i + j, 1), :], lambda j: VN[:, hc(4 * i + j, 1), :], tok[f"v1{i}"])

        def r_o1e(i, b, t):
            tok[f"o1{i}"] = dve.tt(rows(OR, i, 1), rows(OR, i, 1), quad(b), ALU.add, t, tok[f"o1{i}"])
            return [tok[f"o1{i}"]]

        def squares(i, tile):
            for j in range(4):
                h = 4 * i + j
                junk = CT[j // 2][:, 128 * (j % 2):128 * (j % 2) + 128]
                t = act.act(junk, OR[:, hc(h, tile), :], AF.Square, tok[f"o{tile}{i}"], tok.get(f"ct{j // 2}"),
                            tok.get("junk"), accum_out=SS[:, tile, h:h + 1])
            tok["junk"] = t
            tok[f"ss{i}"] = t

        def out_norms(i):
            query_scales(i)
            hs = slice(4 * i, 4 * i + 4)
            s, rq = SS[:, :, hs], RQ[:, :, hs]
            r = dve.tt(s, s, rq, ALU.mult, tok[f"ss{i}"], tok[f"rq{i}"])
            r = dve.tt(s, s, rq, ALU.mult, r)
            r = dve.ts(s, s, 1.0 / 128, EPS_, ALU.mult, ALU.add, r)
            tok[f"on{i}"] = pool.tt(s, s, MHALF[:, :, None].broadcast_to([128, 2, 4]), ALU.pow, r)

        def out_scales(i):
            hs = slice(4 * i, 4 * i + 4)
            tok[f"on{i}"] = dve.tt(SS[:, :, hs], SS[:, :, hs], RQ[:, :, hs], ALU.mult, tok[f"on{i}"])

        def o_scale(i):
            x = OR[:, 4 * i:4 * i + 4, :].rearrange("p (h t) e -> p h t e", t=2)
            sc = SS[:, :, 2 * i:2 * i + 2].rearrange("p t h -> p h t")[:, :, :, None].broadcast_to([128, 2, 2, 128])
            tok[f"os{i}"] = dve.tt(x, x, sc, ALU.mult, tok[f"on{i // 2}"])

        def o_tr(i):
            return quads(lambda j: OR[:, 4 * i + j, :], None, tok[f"os{i}"], tr=True)

        def o_evac(i, b, t):
            o = flat(VB[:, 4 * i:4 * i + 4, :])
            k = slice(2 * i, 2 * i + 2)
            m = dve.stt(o, b[:, :], COL["dn"], flat(SZ[:, k, :]), ALU.mult, ALU.mult, t,
                        [tok[f"z{c}"] for c in (2 * i, 2 * i + 1)], tok[f"v1{i // 2}"])
            tok[f"og{i}"] = m
            return [m]

        def o_parts(i):
            k = slice(2 * i, 2 * i + 2)
            r = split_into(flat(XH[:, k, :]), flat(XL[:, k, :]), flat(VB[:, 4 * i:4 * i + 4, :]), tok[f"og{i}"],
                           tok["pool_read"])
            for c in (2 * i, 2 * i + 1):
                og_ok[c] = r

        for i in range(4):
            v = 4 * seq_all[16 + 2 * i + 1] + 9
            step(max(n + 1 + i, v), lambda i=i: v_mm(i), lambda b, t, i=i: v_evac(i, b, t))
        for i in range(2):
            m = (n + 4, max(n + 6, 4 * len(order) + 4))[i]
            for k, (mm, evac) in enumerate(((r_v0, r_v0e), (r_s, r_se), (r_o0, r_o0e), (r_w, r_we), (r_q, r_qe),
                                            (r_v1, r_v1e), (r_o1, r_o1e))):
                step(m + 3 * k, lambda i=i, mm=mm: mm(i), lambda b, t, i=i, evac=evac: evac(i, b, t))
            at(m + 9, lambda i=i: squares(i, 0))
            at(m + 20, lambda i=i: squares(i, 1))
            at(m + 23, lambda i=i: out_norms(i))
            at(m + 27, lambda i=i: out_scales(i))
            m = max(m + (28, 34)[i], 4 * len(order) + 4 * 7 + 1)
            for k in (2 * i, 2 * i + 1):
                at(m + 2 * (k % 2), lambda i=k: o_scale(i))
                step(m + 3 + 4 * (k % 2), lambda i=k: o_tr(i), lambda b, t, i=k: o_evac(i, b, t))
                at(m + 5 + 4 * (k % 2), lambda i=k: o_parts(i))

        pool_in = {}

        def pool_side():
            for g in range(4):
                x = XA[:, g, :]
                ring = (TMP[:, 3, :], RTMP)
                prev, t = x, tok[f"xa{g}"]
                for i in range(g + 1):
                    n = 1 << i
                    dst = ring[i % 2]
                    u = [pool.copy(dst[:, 0:n], prev[:, 0:n], t, tok.get("pool_free"), G[7]),
                         pool.tt(dst[:, n:T], prev[:, n:T], prev[:, 0:T - n], ALU.add)]
                    prev, t = dst, u
                    yield
                u = [pool.tt(prev[:, 0:16], prev[:, 0:16], INV[:, g, 0:16], ALU.mult, t, l2_ok),
                     pool.tt(prev[:, 16:T], prev[:, 16:T], INV[:, g, 16:17].broadcast_to([128, T - 16]), ALU.mult, t)]
                t = u
                t = pool.tt(x, prev, x, ALU.subtract, t)
                tok["pool_free"] = t
                for _ in range(9):
                    yield
                i, b, free = side_bank()
                t = pe.mm(b[:, 0:T], PW[:, g, :], x, True, True, free, t, l2_ok, signal=True)
                yield
                sc = COL["pool_scale"][:, g:g + 1]
                h = act.act(XH[:, g, :], b[:, 0:T], AF.Copy, t, x_read, scale=sc)
                l = dve.stt(XL[:, g, :], b[:, 0:T], sc, XH[:, g, :].bitcast(F32), ALU.mult, ALU.subtract, h)
                idle[i] = [l]
                pool_in[g] = [h, l]
            tok["pooled"] = tok["pool_free"]

        def ev_fn(dst, name, func, **kw):
            def f(ps, t):
                tok[name] = act.act(dst, ps, func, t, **kw)
                return tok[name]
            return f

        gates = gates_side()
        unit(beta_parts(), lambda: next(gates))
        mains[:] = [[0, 1, 2], 1]
        sides.append(gates)

        def ev_scaled_gate(c):
            def f(ps, t):
                r = dve.tt(GA[:, c, :], ps, RSB, ALU.mult, t)

                def tanh():
                    tok[f"ga{c}"] = act.act(GA[:, c, :], GA[:, c, :], AF.Tanh, r, scale=0.5)
                later(1, tanh)
                return r
            return f

        for c in range(5):
            tile(ev_scaled_gate(c), xs, X)
        x_read = st.done[st.v]
        settle("xs3_all")
        G = tok["xs3"]
        sides.append(pool_side())
        sides.append(delta_side())
        for n, u in enumerate(order):
            st.share = 0 if 4 <= n < 24 else 384
            tile(ev_conv(u) if u < 24 else ev_fn(SZ[:, u - 24, :], f"z{u - 24}", AF.Silu), gs, G)
        for c in range(5, 8):
            tile(ev_fn(GA[:, c, :], f"ga{c}", AF.Tanh, scale=0.5), gs, G)
        settle("pooled")
        for i in range(4):
            bi = main_bank()
            b, free = take_bank(bi)
            end = {}

            def ev(i=i, b=b, bi=bi, end=end):
                g = flat(GA[:, 2 * i:2 * i + 2, :])
                a = dve.stt(g, g, 1.0, b[:, :], ALU.add, ALU.mult, end["t"], [tok[f"ga{c}"] for c in range(8)])
                idle[bi] = [a]
                tok[f"ya{i}"] = a
            unit(products([b[:, 0:T], b[:, T:2 * T]], free, xs, pool_in, nk=4, end=end), ev)
        tok["pool_read"] = st.done[st.v]
        for c in range(8):
            tile(ev_fn(GB[:, c, :], f"gb{c}", AF.Tanh, scale=0.5), gs, G)
        g_read2 = st.done[st.v]
        settle("delta")
        y_ok = {}

        def ev_merge(c):
            def f(ps, t):
                g = GB[:, c, :]
                a = dve.stt(g, g, 1.0, ps, ALU.add, ALU.mult, t, tok[f"gb{c}"])
                s = dve.tt(g, g, GA[:, c, :], ALU.add, a, tok[f"ya{c // 2}"])

                def parts_of_merged():
                    h = act.act(GH[:, c, :], g, AF.Copy, s, g_read2, scale=0.5)
                    l = dve.stt(GL[:, c, :], g, 0.5, GH[:, c, :].bitcast(F32), ALU.mult, ALU.subtract, h, g_read2)
                    y_ok[c] = [h, l]
                later(1, parts_of_merged)
                return a
            return f

        st.share = 0
        tiles([ev_merge(c) for c in range(8)], xs, og_ok)
        og_read = st.done[st.v]
        st.split(st.used + RW)
        flush()
        run_soon()
        h_ok = {}
        X = {}
        stat = Stat(7, 8, og_read, lane=dve)

        def ev_mix(c):
            def f(ps, t):
                h_ok[c] = dve.tt(H[:, c, :], H[:, c, :], ps, ALU.add, t)
                later(1, lambda: mixed_chunk(c))
                return h_ok[c]
            return f

        def mixed_chunk(c):
            X[c] = unscaled(c, COL["ffn"], h_ok[c], og_read)
            stat.add(H[:, c, :], h_ok[c])

        tiles([ev_mix(c) for c in range(8)], gs, y_ok)
        flush()
        run_soon()
        m_read = st.done[st.v]
        ACTS = big[:, :].rearrange("p (e t) -> p e t", t=T)
        A = Arena(32768 - 14848, 32768)
        QP = A.take(4096, T)
        KEYS = A.take(2048, 128)
        SC = A.take(4096, 128)
        XT = [A.take(128) for _ in range(4)]
        CA = [[A.take(256) for _ in range(2)] for _ in range(2)]
        SMALL = A.take(12 * 256)
        V1, V2, TS, F1, F2, FP, FJ = (SMALL[:, 256 * i:256 * i + 256].rearrange("p (t h k) -> p t h k", t=2, k=16)
                                      for i in range(7))
        U1, U2_, UPOS, UJ = (SMALL[:, 256 * (7 + i):256 * (8 + i)].bitcast(U32).rearrange("p (t h k) -> p t h k", t=2,
                                                                                          k=16) for i in range(4))
        S8 = SMALL[:, 2816:2832].rearrange("p (t h) -> p t h", t=2)
        R8 = SMALL[:, 2832:2848].rearrange("p (t h) -> p t h", t=2)
        I16 = SMALL[:, 2848:2864]
        s_l3 = sem("l3")
        mixed = [t for v in og_ok.values() for t in v] + [t for v in y_ok.values() for t in v]
        sp.dma(KEYS, I["keys"], s_l3, mixed)
        sp.dma(IOTA, I["iota"], s_l3)
        l3_ok = sp.dma(I16, I["iota16"], s_l3)

        accs = []

        def residual_side():
            for tile in range(2):
                for half_ in range(2):
                    b, free = accs[2 * tile + half_]
                    for c in range(4):
                        t = pe.mm(b[:, 128 * c:128 * c + 128], H[:, 4 * half_ + c, 128 * tile:128 * tile + 128],
                                  ident[:, :], c == 0, False, free, list(h_ok.values()), signal=c == 3)
                    yield
                    yield
            tok["h_saved"] = t

        pair_at, pairs = [0], [2, 7]

        def pair_bank():
            i = pairs[pair_at[0] % len(pairs)]
            pair_at[0] += 1
            b, free = take_bank(i)
            return i, b, free

        def scores(h):
            i, b, free = pair_bank()
            for tile in range(2):
                for k in range(2):
                    t = pe.mm(b[:, 256 * tile + 128 * k:256 * tile + 128 * k + 128],
                              QP[:, 2 * h + k, 128 * tile:128 * tile + 128], KEYS[:, 2 * h + k, :], True, True,
                              free, tok[f"q{2 * h}"], tok[f"q{2 * h + 1}"], l3_ok, signal=tile == 1 and k == 1)
            tok["qp_read"] = t

            def out():
                a = act.act(flat(SC[:, 4 * h:4 * h + 4, :]), b[:, :], AF.Copy, t, mixed)
                idle[i] = [a]
                tok[f"sc{h}"] = a
            later(1, out)

        def top16(jobs):
            a = [dve.do(lambda e, v=v, s=s: e.max(v[:, 0:8], s), after) for s, x, v, i, after in jobs]
            yield
            b = [dve.do(lambda e, v=v, s=s, x=x: e.match_replace(x, v[:, 0:8], s, -3.0e38), [k])
                 for k, (s, x, v, i, after) in zip(a, jobs)]
            yield
            c = [dve.do(lambda e, v=v, x=x: e.max(v[:, 8:16], x), [k]) for k, (s, x, v, i, after) in zip(b, jobs)]
            yield
            d = [dve.do(lambda e, v=v, s=s, i=i: e.max_index(i[:, 0:8], v[:, 0:8], s), [k])
                 for k, (s, x, v, i, after) in zip(a, jobs)]
            yield
            f = [dve.do(lambda e, v=v, x=x, i=i: e.max_index(i[:, 8:16], v[:, 8:16], x), [k])
                 for k, (s, x, v, i, after) in zip(c, jobs)]
            yield
            return a + c + d + f

        picked, to_pick = [], {}

        def pick(h):
            done = [tok[f"t{h}{tile}"] for tile in range(2)]
            b = dve.do(lambda e: e.tensor_single_scalar(UJ[:, :, h, :], UPOS[:, :, h, :], 15, ALU.bitwise_and), [done])
            a = dve.do(lambda e: e.tensor_single_scalar(UPOS[:, :, h, :], UPOS[:, :, h, :], 4,
                                                        ALU.logical_shift_right), [b])
            if h:
                reduce_picked(h - 1)
            yield
            f = [[pool.copy(FP[:, :, h, :], UPOS[:, :, h, :], a), pool.copy(F1[:, :, h, :], U1[:, :, h, :])],
                 [pool.copy(FJ[:, :, h, :], UJ[:, :, h, :]), pool.copy(F2[:, :, h, :], U2_[:, :, h, :])]]
            yield
            for n, (pos, idx, room) in enumerate(((FP, F1, SC[:, 4 * h:4 * h + 4, :]),
                                                  (FJ, F2, QP[:, 2 * h:2 * h + 2, :]))):
                p, i = pos[:, :, h, :], idx[:, :, h, :]
                e = flat(room).rearrange("p (t k i) -> p t k i", t=2, i=16)
                m = dve.tt(e, p[:, :, :, None].broadcast_to([128, 2, 16, 16]),
                            I16[:, None, None, :].broadcast_to([128, 2, 16, 16]), ALU.is_equal, f[n], l3_ok, tok["qp_read"])
                to_pick[h, n] = p, e, pool.tt(e, e, i[:, :, None, :].broadcast_to([128, 2, 16, 16]), ALU.mult, m)
                yield

        def reduce_picked(h):
            for n in range(2):
                p, e, m = to_pick[h, n]
                picked.append(dve.reduce(p, e, ALU.add, m))

        def topk_side():
            for h in range(8):
                while f"sc{h}" not in tok:
                    yield
                for tile in range(2):
                    r = yield from top16([(SC[:, 4 * h + 2 * tile + k, :], XT[2 * tile + k], v[:, tile, h, :],
                                           u[:, tile, h, :], [tok[f"sc{h}"], mixed])
                                          for k, v, u in ((0, V1, U1), (1, V2, U2_))])
                    ca, cb = CA[tile]
                    t = dve.tt(ca.rearrange("p (a b) -> p a b", b=16), V1[:, tile, h, :, None].broadcast_to([128, 16, 16]),
                               V2[:, tile, h, None, :].broadcast_to([128, 16, 16]), ALU.add, r)
                    yield
                    tok[f"t{h}{tile}"] = yield from top16([(ca, cb, TS[:, tile, h, :], UPOS[:, tile, h, :], [t])])
                yield from pick(h)
            done = [tok[f"t{h}{tile}"] for h in range(8) for tile in range(2)]
            g = dve.copy(R8, TS[:, :, :, 0], done)
            g = dve.tt(TS, TS, R8[:, :, :, None].broadcast_to([128, 2, 8, 16]), ALU.subtract, g)
            for _ in range(4):
                yield
            g = act.act(TS, TS, AF.Exp, g)
            for _ in range(8):
                yield
            reduce_picked(7)
            s = dve.reduce(S8, TS, ALU.add, g)
            s = dve.recip(R8, S8, s)
            g = dve.tt(TS, TS, R8[:, :, :, None].broadcast_to([128, 2, 8, 16]), ALU.mult, s)
            for _ in range(4):
                yield
            i, b, free = pair_bank()
            for tile in range(2):
                for n, src in enumerate((FP, FJ)):
                    t = pe.tr(b[:, 256 * n + 128 * tile:256 * n + 128 * tile + 128],
                              src[:, tile, :, :].rearrange("p h k -> p (h k)"), ident[:, :], free,
                              picked, signal=n == 1 and tile == 1)
            for _ in range(3):
                yield
            a = act.act(ET, b[:, :].rearrange("p (n t) -> p n t", n=2), AF.Copy, t)
            idle[i] = [a]
            i, b, free = pair_bank()
            for tile in range(2):
                t = pe.tr(b[:, 128 * tile:128 * tile + 128], TS[:, tile, :, :].rearrange("p h k -> p (h k)"),
                          ident[:, :], free, g, signal=tile == 1)
            for _ in range(3):
                yield
            g = act.act(GATE, b[:, 0:256], AF.Copy, t)
            idle[i] = [g]
            tok["chosen"] = [a, g]
            st.share = 0
            turns[0] = 4
            use_mains([0, 1])
            for _ in range(8):
                yield
            pairs[:] = [2, 7]

        def ev_query(u):
            def f(ps, t):
                tok[f"q{u}"] = dve.tt(QP[:, u, :], ps, RSB, ALU.mult, t, tok["rs4"], mixed)
                if u % 2:
                    later(2, lambda: scores(u // 2))
                return tok[f"q{u}"]
            return f

        sides.append(scaled_side(COL["ffn"], "rs4", "xs4", [m_read]))
        st.share = 320
        sides.append(topk_side())
        turns[0] = 3
        mains[:] = [[0, 1, 2, 3], 0]
        tiles([ev_query(u) for u in range(4)], xs, X, stat=stat, name="rs4")
        tile(ev_query(4), xs, X)
        accs += [take_bank(3 + i) for i in range(4)]
        sides.append(residual_side())
        mains[:] = [[0, 1], 1]
        for u in range(5, 16):
            tile(ev_query(u), xs, X)
        q_read = st.done[st.v]
        G = tok["xs4"]
        g_all = [t for v in G.values() for t in v]
        progress = [0]
        built = [0]
        last = {"act": None, "dve": None, "pool": None}
        onehot = [flat(x[:, 4 * k:4 * k + 4, :]).rearrange("p (t n i) -> p t n i", n=2, i=128)
                  for k in range(2) for x in (XH, XL)]
        oh_free = [None] * 4
        vg_free = [None] * 4

        def build_side():
            while "chosen" not in tok or len(pairs) < 2 or place[0] < 4:
                yield
            flats, table = {}, {}

            def hot(g):
                r = g % 4
                flats[g] = dve.tt(onehot[r], IOTA[:, None, None, :].broadcast_to([128, 4, 2, 128]),
                                  ET[:, :, 4 * g:4 * g + 4].rearrange("p n t -> p t n")[:, :, :, None].broadcast_to(
                                      [128, 4, 2, 128]), ALU.is_equal, l3_ok, tok["chosen"], oh_free[r], q_read)

            def scale(g):
                for j in range(4):
                    v = act.act(VG[j], onehot[g % 4][:, j, 1, :].bitcast(F32), AF.Copy, flats[g], vg_free[j],
                                scale=GATE[:, 4 * g + j:4 * g + j + 1])
                    flats[g, j] = v

            def multiply(g):
                i, b, free = pair_bank()
                for j in range(4):
                    vg_free[j] = pe.mm(b[:, 128 * j:128 * j + 128], onehot[g % 4][:, j, 0, :].bitcast(F32), VG[j],
                                       True, True, free, flats[g, j], signal=True)
                oh_free[g % 4] = vg_free[3]
                table[g] = (i, b, vg_free[3])

            def fold(g):
                t0 = 4 * g
                i, b, t = table[g]
                n = progress[0]
                g4 = b[:, :].rearrange("p (t e) -> p e t", e=128)
                a = None
                if n:
                    x = ACTS[:, 0:n, t0:t0 + 4]
                    a = last["dve"] = dve.tt(x, x, g4[:, 0:n, :], ALU.mult, t, last["act"], last["pool"])
                table[g] += (g4, a, n)

            def fill(g):
                i, b, t, g4, a, n = table[g]
                t0 = 4 * g
                idle[i] = [a]
                assert n == progress[0]
                if n < 128:
                    last["act"] = act.act(ACTS[:, n:128, t0:t0 + 4], g4[:, n:128, :], AF.Copy, t, a, tok["chosen"])
                    idle[i] = [last["act"]]
                built[0] = t0 + 4

            n = T // 4
            for g in range(n + 2):
                yield
                if g > 1:
                    multiply(g - 2)
                yield
                if g > 1:
                    fold(g - 2)
                if g < n:
                    hot(g)
                if 0 < g <= n:
                    scale(g - 1)
                yield
                if g > 1:
                    fill(g - 2)
                yield
            tok["built"] = True

        def ev_down(n):
            def f(ps, t):
                m = built[0]
                r = t
                free = [mixed, tok["h_saved"], g_all]
                if n >= 70:
                    free += [tok["chosen"]]
                if m < T:
                    r = last["act"] = act.act(ACTS[:, n, m:T], ps[:, m:T], AF.Gelu, t, free)
                if m > 0:
                    r = act.act(TG[:, 0:m], ps[:, 0:m], AF.Gelu, t, last["pool"])
                    x = ACTS[:, n, 0:m]
                    last["pool"] = pool.tt(x, x, TG[:, 0:m], ALU.mult, r, last["act"], last["dve"])
                progress[0] = n + 1
                return r
            return f

        turns[0] = 4
        st.share = 384
        sides.append(build_side())
        W_AHEAD = 3
        parts = {}
        used = {}

        def cut(n):
            if n < 128:
                s = (n + 4) % 8
                parts[n] = split_into(XH[:, s, :], XL[:, s, :], ACTS[:, n, :], list(last.values()), used.get(n - 8),
                                      oh_free)

        for n in range(128):
            if n == 4:
                mains[:] = [[0, 1, 2], 0]
                pairs[:] = [7]
            tile(ev_down(n), gs, G)
            if n >= 128 - W_AHEAD and "built" in tok:
                cut(len(parts))
        flush()
        settle("built")
        while len(parts) < W_AHEAD:
            cut(len(parts))
        FW = big[:, 0:1024]
        O = big[:, 1024:3072].rearrange("p (t d) -> p t d", t=2)
        FS = big[:, 3072:3082]
        s_fin, s_out = sem("fin"), sem("out")
        out_ok = {}
        for n in range(125):
            def up_parts(n=n):
                v, wh, wl, h_ok_, l_ok = st.take()
                s = (n + 4) % 8
                for tile in range(2):
                    a = XH[:, s, 128 * tile:128 * tile + 128]
                    b = XL[:, s, 128 * tile:128 * tile + 128]
                    for half_ in range(2):
                        o, _ = accs[2 * tile + half_]
                        w = slice(512 * half_, 512 * half_ + 512)
                        pe.mm(o[:, :], a, wh[:, w], False, False, h_ok_, parts[n])
                        pe.mm(o[:, :], a, wl[:, w], False, False, l_ok)
                    for half_ in range(2):
                        o, _ = accs[2 * tile + half_]
                        w = slice(512 * half_, 512 * half_ + 512)
                        t = pe.mm(o[:, :], b, wh[:, w], False, False, signal=half_ == 1)
                    yield
                st.done[v] = used[n] = t

            unit(up_parts(), lambda: None)
            cut(n + W_AHEAD)
        fin_ok = sp.dma(FW, I["fnw"], s_fin, parts[63])
        three = {n: st.take() for n in range(125, 128)}
        for tile, half_, n in [(0, 0, 125), (0, 1, 125), (0, 0, 126), (0, 1, 126), (0, 0, 127), (0, 1, 127)] + [
                (1, half_, n) for half_ in range(2) for n in range(125, 128)]:
            v, wh, wl, h_ok_, l_ok = three[n]
            o, _ = accs[2 * tile + half_]
            w = slice(512 * half_, 512 * half_ + 512)
            s = (n + 4) % 8
            a = XH[:, s, 128 * tile:128 * tile + 128]
            b = XL[:, s, 128 * tile:128 * tile + 128]
            pe.mm(o[:, :], a, wh[:, w], False, False, h_ok_, parts[n])
            pe.mm(o[:, :], a, wl[:, w], False, False, l_ok)
            out_ok[tile, half_] = pe.mm(o[:, :], b, wh[:, w], False, n == 127, signal=n == 127)

        for tile in range(2):
            fs = FS[:, 4 * tile:4 * tile + 4]
            (o0, _), (o1, _) = accs[2 * tile:2 * tile + 2]
            a = act.act(O[:, tile, 0:512], o0[:, :], AF.Square, out_ok[tile, 0], parts[63], accum_out=fs[:, 0:1])
            p = dve.ts(fs[:, 1:2], fs[:, 0:1], 1.0 / D, EPS_, ALU.mult, ALU.add, a)
            g = dve.tt(O[:, tile, 0:512], o0[:, :], FW[:, 0:512], ALU.mult, a, fin_ok)
            a = act.act(O[:, tile, 512:1024], o1[:, :], AF.Square, out_ok[tile, 1], accum_out=fs[:, 2:3])
            s = dve.ts(fs[:, 2:3], fs[:, 2:3], 1.0 / D, fs[:, 1:2], ALU.mult, ALU.add, a, p)
            s = pool.tt(fs[:, 3:4], fs[:, 2:3], MHALF, ALU.pow, s)
            a = [act.act(O[:, tile, 0:512], O[:, tile, 0:512], AF.Copy, s, g, scale=fs[:, 3:4]),
                 dve.stt(O[:, tile, 512:1024], o1[:, :], fs[:, 3:4], FW[:, 512:1024], ALU.mult, ALU.mult, s)]
            for half_ in range(2):
                w = slice(512 * half_, 512 * half_ + 512)
                end = sp.dma(out[0, 128 * tile:128 * tile + 128, w], O[:, tile, w], s_out, a[half_])
        sp.wait(end)
        with nc.Block() as block:
            @block.sync
            def _(e):
                sp.emit(e)

            @block.gpsimd
            def _(e):
                pool.emit(e)

            @block.tensor
            def _(e):
                pe.emit(e)

            @block.scalar
            def _(e):
                act.emit(e)

            @block.vector
            def _(e):
                dve.emit(e)


def prepare(inputs):
    import numpy as np
    f = np.float32
    x = {k: np.asarray(v) for k, v in inputs.items()}
    tiles = []

    def feature_tiles(w):
        n = w.shape[1] // 128
        tiles.append(w.reshape(8, 128, n, 128).transpose(2, 1, 0, 3).reshape(n, 128, 1024))

    def half_tiles(w):
        return w.reshape(4, 128, 4, 2, 128).transpose(2, 1, 0, 3, 4).reshape(4, 128, 1024)

    w = x["w_in"][0]
    o = np.cumsum([0, 512, 128, 128, 128, 128, 128, 128, 24, 512, 128, 128, 1024, 1024])
    part = [w[:, o[i]:o[i + 1]] for i in range(13)]
    qn, kc, vc, ks, vs, kw, vw, gn, qs, kk, vv, ga, gb = part

    def pairs(q):
        return q.reshape(1024, 2, 4, 64).transpose(0, 2, 1, 3).reshape(1024, 512)

    gates = gn.reshape(1024, 2, 4, 3).transpose(0, 3, 2, 1).reshape(1024, 24)
    feature_tiles(np.concatenate([kc, vc, ks, kw, pairs(qn)], 1))
    tm = np.concatenate([vs, vw, vv, gates, np.zeros((1024, 104), f)], 1)
    tiles.append(tm.reshape(4, 2, 128, 512).transpose(0, 2, 1, 3).reshape(4, 128, 1024))
    feature_tiles(np.concatenate([kk, pairs(qs), ga, gb], 1))
    for k in ("w_up_nsa", "w_up_swa"):
        tiles.append(half_tiles(x[k][0].reshape(2, 4, 64, 1024).transpose(1, 0, 2, 3).reshape(512, 1024)))
    feature_tiles(x["w_out"][0])
    w1, w2 = x["w_mlp_in"][0], x["w_mlp_out"][0]
    for q in range(9):
        if q < 8:
            feature_tiles(w1[:, 512 * q:512 * q + 512])
        if q > 0:
            tiles.append(half_tiles(w2[512 * q - 512:512 * q]))
    w = x["w_in_2"][0]
    xa, qkv, z, ba, ga, gb = np.split(w, [512, 3584, 4608, 4624, 5648], axis=1)
    q, k, v = np.split(qkv, 3, axis=1)
    qvz = np.stack([q, v, z], 1).reshape(1024, 3, 8, 128).transpose(0, 2, 1, 3).reshape(1024, 3072)
    feature_tiles(np.concatenate([xa, ga[:, 0:640], k, qvz, ga[:, 640:1024]], 1))
    tiles.append(half_tiles(x["w_pool_up_2"][0]))
    feature_tiles(np.concatenate([gb, x["w_dn_up_2"][0]], 1))
    feature_tiles(x["w_mix_out_2"][0])
    feature_tiles(x["peer_w_query_2"][0])
    tiles.append(x["peer_down_2"][0].reshape(128, 128, 8, 128).transpose(1, 3, 2, 0).reshape(128, 128, 1024))
    tiles.append(x["peer_up_2"][0].reshape(128, 128, 1024).transpose(1, 0, 2))
    wst = np.concatenate(tiles, 0)

    cols = [x[k].reshape(-1, 128).T for k in ("norm_mix_pre", "norm_mix_post", "norm_mlp_pre", "norm_mlp_post",
                                              "mix_norm_w_2", "ffn_norm_w_2", "pool_scale_2")]
    cols.append(x["conv_w_2"][0].reshape(4, 24, 128).transpose(2, 1, 0).reshape(128, 96))
    cols.append(x["dn_norm_w_2"].reshape(128, 1))
    cols.append(np.full((128, 1), 1e-6, f))
    cols.append(np.full((128, 1), -0.5, f))
    cols.append((np.arange(128)[:, None] // 16 == np.arange(8)).astype(f))
    cols.append(np.broadcast_to((2.0 / np.arange(1, 20, 2)).astype(f), (128, 10)))

    dist = 255 - np.arange(384)
    start = np.array([*range(17), 21, 27, 35, 46, 59, 77, 99, 128, 166, 216])
    bucket = np.searchsorted(start, dist, side="right") - 1
    oneh = np.zeros((32, 384), f)
    oneh[bucket[dist >= 0], np.arange(384)[dist >= 0]] = 8.0
    bmask = np.zeros((16, 384), f)
    bmask[:, dist < 0] = -1e30
    bmask[8:, dist >= 128] = -1e30
    relb = x["rel_bias"].reshape(32, 2, 2, 4).transpose(0, 1, 3, 2).reshape(32, 16)
    t = np.arange(256).reshape(2, 128).T
    end = np.arange(15) * 16 + 31
    ok = (end <= t[:, :, None])
    cmask = np.concatenate([np.where(ok, 0, -1e30), ok], 2).astype(f)
    sel = np.zeros((30, 128), f)
    for r in range(128):
        if r % 16 < 15:
            sel[(r // 16 % 2) * 15 + r % 16, r] = 1
    i = np.arange(128)
    tri = (i[:, None] <= i).astype(f)
    lmask = np.stack([(i[:, None] // (2 * n) == i // (2 * n)) & (i // n % 2 == 1) & (i[:, None] // n % 2 == 0)
                      for n in (16, 32, 64)], 1).astype(f)
    inv = 1.0 / np.minimum(np.arange(1, 18), np.array([[2], [4], [8], [16]]))
    keys = np.stack([x["peer_keys_1_2"][0], x["peer_keys_2_2"][0]], 1)
    d = {
        "keys": keys.transpose(3, 0, 1, 2).reshape(128, 16, 128),
        "iota16": np.broadcast_to(np.arange(16, dtype=f), (128, 16)),
        "iota": np.broadcast_to(np.arange(128, dtype=f), (128, 128)),
        "fnw": np.broadcast_to(x["final_norm_w_2"][None], (128, 1024)),
        "tri": tri, "suf": (i[:, None] > i).astype(f), "negm": np.where(i[:, None] <= i, 0, -1e30).astype(f),
        "lmask": lmask, "baw": ba.reshape(8, 128, 16).transpose(1, 0, 2).reshape(128, 128),
        "alog": np.broadcast_to(x["a_log_2"].reshape(1, 8), (128, 8)),
        "dtb": np.broadcast_to(x["dt_bias_2"].reshape(1, 8), (128, 8)),
        "poolw": x["pool_w_2"][0].transpose(1, 0, 2),
        "inv": np.broadcast_to(inv.astype(f)[None], (128, 4, 17)),
        "wst": wst,
        "xT": x["x"][0].T.reshape(8, 128, 256).transpose(1, 0, 2),
        "cols": np.concatenate(cols, 1),
        "ident": np.eye(128, dtype=f),
        "relb": relb, "oneh": oneh, "bmask": bmask,
        "pos": np.concatenate([x[k][0].reshape(16, 128).T for k in ("cmp_pos_k", "cmp_pos_v")], 1),
        "w1k": x["cmp_w1_k"][0].reshape(16, 128, 256).transpose(1, 0, 2),
        "w1v": x["cmp_w1_v"][0].reshape(16, 128, 256).transpose(1, 0, 2),
        "w2k": np.concatenate([x["cmp_w2_k"][0]] * 2, 1).reshape(2, 128, 128).transpose(1, 0, 2),
        "w2v": x["cmp_w2_v"][0].reshape(2, 128, 64).transpose(1, 0, 2),
        "sinks": np.broadcast_to(x["attn_sinks"].reshape(2, 4).T.reshape(1, 8), (128, 8)),
        "cmask": cmask, "sel": sel,
    }
    return {k: np.ascontiguousarray(v) for k, v in d.items()}


def kernel(**inputs):
    from concourse import bacc
    from concourse.bass_utils import run_bass_kernel_spmd

    arrays = prepare(inputs)
    nc = bacc.Bacc("TRN2", target_bir_lowering=False, num_devices=1)
    operands = {name: nc.dram_tensor(f"in_{name}", a.shape, mybir.dt.from_np(a.dtype), kind="ExternalInput").ap()
                for name, a in arrays.items()}
    out = nc.dram_tensor("out_0", (1, T, D), mybir.dt.float32, kind="ExternalOutput").ap()
    program(nc, operands, out)
    result = run_bass_kernel_spmd(nc, [{f"in_{name}": a for name, a in arrays.items()}], core_ids=[0])
    return result.results[0]["out_0"]
```
